# Optimizing a Trainium2 kernel written in Bass

```python
import jax
import jax.numpy as jnp
from jax import lax
import numpy as np
import math
import jax, jax.numpy as jnp

D_MODEL = 1024
BATCH = 1
SEQ = 256
DEPTH = 2

D_MIX = D_MODEL
POOL_WIDTH = D_MIX // 4
POOL_WINDOWS = (2, 4, 8, 16)
POOL_GROUP_DIM = POOL_WIDTH // len(POOL_WINDOWS)
NSA_WIDTH = D_MIX - POOL_WIDTH
N_Q_HEADS = 8
HEAD_DIM = NSA_WIDTH // N_Q_HEADS
N_KV_GROUPS = 2
HEADS_PER_GROUP = N_Q_HEADS // N_KV_GROUPS
KV_WIDTH = N_KV_GROUPS * HEAD_DIM
N_BRANCHES = 3
CMP_STRIDE = 16
CMP_BLOCK = 2 * CMP_STRIDE
SLC_BLOCK = 64
N_SELECT = 16
WINDOW = 512
Q_BLOCK = 128
D_FF = 2816
D_IN = POOL_WIDTH + NSA_WIDTH + 6 * KV_WIDTH + N_BRANCHES * N_Q_HEADS
ALPHA = (2.0 * DEPTH) ** 0.25
BETA = (8.0 * DEPTH) ** -0.25
LN_EPS = 1e-5
NEG_BIG = -1e30
SEL_BIG = 1e30


def layer_norm(x, g, b):
    xf = x.astype(jnp.float32)
    mu = jnp.mean(xf, axis=-1, keepdims=True)
    var = jnp.mean(jnp.square(xf - mu), axis=-1, keepdims=True)
    y = (xf - mu) * lax.rsqrt(var + LN_EPS) * g.astype(jnp.float32) + b.astype(jnp.float32)
    return y.astype(x.dtype)

def swiglu(x, w_gate, w_up, w_down):
    return (jax.nn.silu(x @ w_gate) * (x @ w_up)) @ w_down

def masked_softmax(s, mask):
    s = jnp.where(mask, s, NEG_BIG)
    m = jnp.max(s, axis=-1, keepdims=True)
    e = jnp.exp(s - m) * mask
    return e / jnp.maximum(jnp.sum(e, axis=-1, keepdims=True), 1e-30)

def pool_mixer(u, pool_w, pool_scale):
    B, S, _ = u.shape
    uf = u.astype(jnp.float32)
    csum = jnp.pad(jnp.cumsum(uf, axis=1), ((0, 0), (1, 0), (0, 0)))
    t = jnp.arange(S)
    groups = []
    for g, w in enumerate(POOL_WINDOWS):
        sl = slice(g * POOL_GROUP_DIM, (g + 1) * POOL_GROUP_DIM)
        cg = csum[..., sl]
        lo = jnp.maximum(t + 1 - w, 0)
        win_sum = cg[:, 1:] - cg[:, lo]
        cnt = jnp.minimum(t + 1, w).astype(jnp.float32)[None, :, None]
        groups.append(win_sum / cnt - uf[..., sl])
    pooled = jnp.stack(groups, axis=2).astype(u.dtype)
    mixed = jnp.einsum('bsgc,gcd->bsgd', pooled, pool_w)
    return mixed.reshape(B, S, POOL_WIDTH) * pool_scale

def compress(kv, pos, w1, w2):
    B, G, S, dh = kv.shape
    chunks = kv.reshape(B, G, S // CMP_STRIDE, CMP_STRIDE, dh)
    blocks = jnp.concatenate([chunks[:, :, :-1], chunks[:, :, 1:]], axis=3)
    flat = (blocks + pos).reshape(B, G, S // CMP_STRIDE - 1, CMP_BLOCK * dh)
    return jax.nn.gelu(flat @ w1) @ w2

def nsa_mixer(q, kc, vc, k_slc, v_slc, k_win, v_win, gates):
    B, S = q.shape[0], q.shape[1]
    G = N_KV_GROUPS
    NQB = S // Q_BLOCK
    NS = S // SLC_BLOCK
    NC = S // CMP_STRIDE - 1
    n_sel = min(N_SELECT, NS)
    scale = HEAD_DIM ** -0.5
    qb = (q * scale).reshape(B, NQB, Q_BLOCK, G, HEADS_PER_GROUP, HEAD_DIM).transpose(1, 0, 3, 4, 2, 5)
    gb = gates.reshape(B, NQB, Q_BLOCK, G, HEADS_PER_GROUP, N_BRANCHES).transpose(1, 0, 3, 4, 2, 5)
    ks_blocks = k_slc.reshape(B, G, NS, SLC_BLOCK, HEAD_DIM)
    vs_blocks = v_slc.reshape(B, G, NS, SLC_BLOCK, HEAD_DIM)
    kw_pad = jnp.pad(k_win, ((0, 0), (0, 0), (WINDOW, 0), (0, 0)))
    vw_pad = jnp.pad(v_win, ((0, 0), (0, 0), (WINDOW, 0), (0, 0)))
    cmp_end = jnp.arange(NC) * CMP_STRIDE + CMP_BLOCK - 1
    blk = jnp.arange(NS)
    bi = jnp.arange(B)[:, None, None, None]
    gi = jnp.arange(G)[None, :, None, None]
    slc_w = jnp.array([0.5, 1.0, 1.0, 1.0], jnp.float32)

    def one_block(args):
        c, q_c, g_c = args
        t = c * Q_BLOCK + jnp.arange(Q_BLOCK)
        s = jnp.einsum('bghtd,bgnd->bghtn', q_c, kc).astype(jnp.float32)
        p_cmp = masked_softmax(s, cmp_end[None, :] <= t[:, None])
        o_cmp = jnp.einsum('bghtn,bgnd->bghtd', p_cmp.astype(vc.dtype), vc)
        imp = jnp.pad(p_cmp.sum(axis=2), ((0, 0), (0, 0), (0, 0), (1, 1)))
        imp_slc = imp[..., :4 * NS].reshape(B, G, Q_BLOCK, NS, 4) @ slc_w + 0.5 * imp[..., 4::4]
        jt = (t // SLC_BLOCK)[:, None]
        forced = (blk == 0) | (blk == jt) | (blk == jt - 1)
        score = jnp.where(blk <= jt, jnp.where(forced, SEL_BIG, imp_slc), NEG_BIG)
        top_s, idx = lax.top_k(score, n_sel)
        sel_ok = top_s > 0.5 * NEG_BIG
        ks = ks_blocks[bi, gi, idx].reshape(B, G, Q_BLOCK, n_sel * SLC_BLOCK, HEAD_DIM)
        vs = vs_blocks[bi, gi, idx].reshape(B, G, Q_BLOCK, n_sel * SLC_BLOCK, HEAD_DIM)
        pos = (idx[..., None] * SLC_BLOCK + jnp.arange(SLC_BLOCK)).reshape(B, G, Q_BLOCK, n_sel * SLC_BLOCK)
        m_slc = (pos <= t[:, None]) & jnp.repeat(sel_ok, SLC_BLOCK, axis=-1)
        s = jnp.einsum('bghtd,bgtkd->bghtk', q_c, ks).astype(jnp.float32)
        p = masked_softmax(s, m_slc[:, :, None])
        o_slc = jnp.einsum('bghtk,bgtkd->bghtd', p.astype(vs.dtype), vs)
        start = c * Q_BLOCK
        kw = lax.dynamic_slice_in_dim(kw_pad, start, WINDOW + Q_BLOCK, axis=2)
        vw = lax.dynamic_slice_in_dim(vw_pad, start, WINDOW + Q_BLOCK, axis=2)
        s_pos = start - WINDOW + jnp.arange(WINDOW + Q_BLOCK)
        diff = t[:, None] - s_pos[None, :]
        m_win = (s_pos[None, :] >= 0) & (diff >= 0) & (diff < WINDOW)
        s = jnp.einsum('bghtd,bgkd->bghtk', q_c, kw).astype(jnp.float32)
        p = masked_softmax(s, m_win)
        o_win = jnp.einsum('bghtk,bgkd->bghtd', p.astype(vw.dtype), vw)
        o = g_c[..., 0:1] * o_cmp + g_c[..., 1:2] * o_slc + g_c[..., 2:3] * o_win
        return o.transpose(0, 3, 1, 2, 4).reshape(B, Q_BLOCK, NSA_WIDTH)

    out = lax.map(one_block, (jnp.arange(NQB), qb, gb))
    return out.transpose(1, 0, 2, 3).reshape(B, S, NSA_WIDTH)

def hybrid_mixer(x, w_in, b_gate, pool_w, pool_scale, cmp_pos_k, cmp_k_w1, cmp_k_w2,
                 cmp_pos_v, cmp_v_w1, cmp_v_w2, w_out):
    B, S, _ = x.shape
    proj = x @ w_in
    cuts = tuple(int(v) for v in np.cumsum([POOL_WIDTH, NSA_WIDTH] + [KV_WIDTH] * 6))
    u, q, kc, vc, ks, vs, kw, vw, g = jnp.split(proj, cuts, axis=-1)
    y_pool = pool_mixer(u, pool_w, pool_scale)

    def heads(a):
        return a.reshape(B, S, N_KV_GROUPS, HEAD_DIM).transpose(0, 2, 1, 3)

    k_cmp = compress(heads(kc), cmp_pos_k, cmp_k_w1, cmp_k_w2)
    v_cmp = compress(heads(vc), cmp_pos_v, cmp_v_w1, cmp_v_w2)
    gates = jax.nn.sigmoid((g + b_gate).astype(jnp.float32)).astype(x.dtype)
    gates = gates.reshape(B, S, N_Q_HEADS, N_BRANCHES)
    y_nsa = nsa_mixer(q.reshape(B, S, N_Q_HEADS, HEAD_DIM), k_cmp, v_cmp,
                      heads(ks), heads(vs), heads(kw), heads(vw), gates)
    return jnp.concatenate([y_pool, y_nsa], axis=-1) @ w_out

def first_inputs(seed: int = 0) -> dict:
    key = jax.random.key(seed)
    k = jax.random.split(key, 24)
    L = DEPTH

    def nrm(kk, shape, scale):
        return jax.random.normal(kk, shape, jnp.float32) * scale

    return {
        'x': nrm(k[0], (BATCH, SEQ, D_MODEL), 1.0),
        'ln1_g': 1.0 + nrm(k[1], (L, D_MODEL), 0.02),
        'ln1_b': nrm(k[2], (L, D_MODEL), 0.02),
        'ffn1_w_gate': nrm(k[3], (L, D_MODEL, D_FF), D_MODEL ** -0.5),
        'ffn1_w_up': nrm(k[4], (L, D_MODEL, D_FF), D_MODEL ** -0.5),
        'ffn1_w_down': nrm(k[5], (L, D_FF, D_MODEL), BETA * D_FF ** -0.5),
        'w_in': nrm(k[6], (L, D_MODEL, D_IN), D_MODEL ** -0.5),
        'b_gate': nrm(k[7], (L, N_BRANCHES * N_Q_HEADS), 0.5),
        'pool_w': nrm(k[8], (L, len(POOL_WINDOWS), POOL_GROUP_DIM, POOL_GROUP_DIM), POOL_GROUP_DIM ** -0.5),
        'pool_scale': 1.0 + nrm(k[9], (L, POOL_WIDTH), 0.02),
        'cmp_pos_k': nrm(k[10], (L, CMP_BLOCK, HEAD_DIM), 0.02),
        'cmp_k_w1': nrm(k[11], (L, CMP_BLOCK * HEAD_DIM, HEAD_DIM), (CMP_BLOCK * HEAD_DIM) ** -0.5),
        'cmp_k_w2': nrm(k[12], (L, HEAD_DIM, HEAD_DIM), HEAD_DIM ** -0.5),
        'cmp_pos_v': nrm(k[13], (L, CMP_BLOCK, HEAD_DIM), 0.02),
        'cmp_v_w1': nrm(k[14], (L, CMP_BLOCK * HEAD_DIM, HEAD_DIM), (CMP_BLOCK * HEAD_DIM) ** -0.5),
        'cmp_v_w2': nrm(k[15], (L, HEAD_DIM, HEAD_DIM), HEAD_DIM ** -0.5),
        'w_out': nrm(k[16], (L, D_MIX, D_MODEL), BETA * D_MIX ** -0.5),
        'ln2_g': 1.0 + nrm(k[17], (L, D_MODEL), 0.02),
        'ln2_b': nrm(k[18], (L, D_MODEL), 0.02),
        'ffn2_w_gate': nrm(k[19], (L, D_MODEL, D_FF), D_MODEL ** -0.5),
        'ffn2_w_up': nrm(k[20], (L, D_MODEL, D_FF), D_MODEL ** -0.5),
        'ffn2_w_down': nrm(k[21], (L, D_FF, D_MODEL), BETA * D_FF ** -0.5),
        'ln3_g': 1.0 + nrm(k[22], (L, D_MODEL), 0.02),
        'ln3_b': nrm(k[23], (L, D_MODEL), 0.02),
    }

def first_block(x, ln1_g, ln1_b, ffn1_w_gate, ffn1_w_up, ffn1_w_down, w_in, b_gate,
              pool_w, pool_scale, cmp_pos_k, cmp_k_w1, cmp_k_w2, cmp_pos_v, cmp_v_w1,
              cmp_v_w2, w_out, ln2_g, ln2_b, ffn2_w_gate, ffn2_w_up, ffn2_w_down,
              ln3_g, ln3_b):
    for l in range(DEPTH):
        x = layer_norm(ALPHA * x + 0.5 * swiglu(x, ffn1_w_gate[l], ffn1_w_up[l], ffn1_w_down[l]),
                       ln1_g[l], ln1_b[l])
        y = hybrid_mixer(x, w_in[l], b_gate[l], pool_w[l], pool_scale[l], cmp_pos_k[l],
                         cmp_k_w1[l], cmp_k_w2[l], cmp_pos_v[l], cmp_v_w1[l], cmp_v_w2[l], w_out[l])
        x = layer_norm(ALPHA * x + y, ln2_g[l], ln2_b[l])
        x = layer_norm(ALPHA * x + 0.5 * swiglu(x, ffn2_w_gate[l], ffn2_w_up[l], ffn2_w_down[l]),
                       ln3_g[l], ln3_b[l])
    return x


GRID_W = 64
CTX_LEN = 256
HEAD_DIM_2 = 64
A_Q_HEADS = 8
A_KV_HEADS = 2
B_HEADS = 4
B_KEY_DIM = 128
B_VAL_DIM = 128
HGRN_CHUNK = 32
C_HEADS = 16
NA_ROWS = 8
NA_COLS = 16
CONV_W = 3

ROPE_THETA = 10000.0
EPS = 1e-6
ATTN_SCALE = HEAD_DIM_2 ** -0.5
HGRN_SCALE = B_KEY_DIM ** -0.5

N_EVEN = (DEPTH + 1) // 2
N_ODD = DEPTH // 2
A_Q_W = A_Q_HEADS * HEAD_DIM_2
A_KV_W = A_KV_HEADS * HEAD_DIM_2
B_K_W = B_HEADS * B_KEY_DIM
B_V_W = B_HEADS * B_VAL_DIM
EVEN_IN_W = A_Q_W + 2 * A_KV_W + 3 * B_K_W + 2 * B_V_W
EVEN_SPLITS = (A_Q_W, A_Q_W + A_KV_W, A_Q_W + 2 * A_KV_W, A_Q_W + 2 * A_KV_W + B_K_W,
               A_Q_W + 2 * A_KV_W + 2 * B_K_W, A_Q_W + 2 * A_KV_W + 3 * B_K_W,
               A_Q_W + 2 * A_KV_W + 3 * B_K_W + B_V_W)
EVEN_OUT_W = A_Q_W + B_V_W
C_W = C_HEADS * HEAD_DIM_2


def rms_norm(x, w):
    xf = x.astype(jnp.float32)
    y = xf * lax.rsqrt(jnp.mean(xf * xf, axis=-1, keepdims=True) + EPS)
    return (y * w.astype(jnp.float32)).astype(x.dtype)

def axial_rope_tables(n_tokens):
    t = jnp.arange(n_tokens)
    row = (t // GRID_W).astype(jnp.float32)
    col = (t % GRID_W).astype(jnp.float32)
    n_freq = HEAD_DIM_2 // 4
    inv_freq = ROPE_THETA ** (-jnp.arange(n_freq, dtype=jnp.float32) / n_freq)
    ang = jnp.concatenate([row[:, None] * inv_freq, col[:, None] * inv_freq], axis=-1)
    return jnp.cos(ang), jnp.sin(ang)

def apply_rope(x, cos, sin):
    x1, x2 = jnp.split(x, 2, axis=-1)
    c = cos[None, :, None, :].astype(x.dtype)
    s = sin[None, :, None, :].astype(x.dtype)
    return jnp.concatenate([x1 * c - x2 * s, x1 * s + x2 * c], axis=-1)

def gqa_axial_attention(q_lat, k_lat, v_lat, q_ctx, k_ctx, v_ctx, q_norm_w, k_norm_w, with_ctx_out):
    B_, L = q_lat.shape[:2]
    n_ctx = q_ctx.shape[1]
    group = A_Q_HEADS // A_KV_HEADS
    q_lat, q_ctx = rms_norm(q_lat, q_norm_w), rms_norm(q_ctx, q_norm_w)
    k_lat, k_ctx = rms_norm(k_lat, k_norm_w), rms_norm(k_ctx, k_norm_w)
    cos, sin = axial_rope_tables(L)
    q_lat = apply_rope(q_lat, cos, sin)
    k_lat = apply_rope(k_lat, cos, sin)
    k_all = jnp.concatenate([k_ctx, k_lat], axis=1)
    v_all = jnp.concatenate([v_ctx, v_lat], axis=1)

    def attend(q, k, v):
        s = jnp.einsum("bqhgd,bkhd->bhgqk", q, k).astype(jnp.float32) * ATTN_SCALE
        p = jax.nn.softmax(s, axis=-1).astype(v.dtype)
        return jnp.einsum("bhgqk,bkhd->bqhgd", p, v)

    n_blk = L // Q_BLOCK
    q_blocks = q_lat.reshape(B_, n_blk, Q_BLOCK, A_KV_HEADS, group, HEAD_DIM_2).transpose(1, 0, 2, 3, 4, 5)
    o = lax.map(lambda qb: attend(qb, k_all, v_all), q_blocks)
    o_lat = o.transpose(1, 0, 2, 3, 4, 5).reshape(B_, L, A_Q_W)
    o_ctx = None
    if with_ctx_out:
        o_ctx = attend(q_ctx.reshape(B_, n_ctx, A_KV_HEADS, group, HEAD_DIM_2), k_ctx, v_ctx).reshape(B_, n_ctx, A_Q_W)
    return o_lat, o_ctx

def forget_gate(f_raw, lb):
    z = f_raw.astype(jnp.float32)
    log_f = jnp.logaddexp(jnp.log(lb), jnp.log1p(-lb) + jax.nn.log_sigmoid(z))
    k = (1.0 - lb) * jax.nn.sigmoid(-z)
    return k, log_f

def hgrn2_chunk_scan(q, k, log_f, v, s0):
    B_, L, H, dk = q.shape
    dv = v.shape[-1]
    n = L // HGRN_CHUNK

    def to_chunks(a):
        return a.reshape(B_, n, HGRN_CHUNK, H, a.shape[-1]).transpose(1, 0, 3, 2, 4)

    tri = jnp.tril(jnp.ones((HGRN_CHUNK, HGRN_CHUNK), dtype=bool))[None, None, :, :, None]

    def step(S, inp):
        qc, kc, gc, vc = inp
        b = jnp.cumsum(gc, axis=2)
        diff = b[:, :, :, None, :] - b[:, :, None, :, :]
        decay = jnp.exp(jnp.where(tri, diff, -jnp.inf))
        scores = jnp.einsum("bhtd,bhtsd,bhsd->bhts", qc, decay, kc)
        o = jnp.einsum("bhts,bhsv->bhtv", scores, vc) + jnp.einsum("bhtd,bhdv->bhtv", qc * jnp.exp(b), S)
        b_last = b[:, :, -1:, :]
        S_new = jnp.exp(b_last[:, :, 0, :])[..., None] * S + jnp.einsum("bhsd,bhsv->bhdv", kc * jnp.exp(b_last - b), vc)
        return S_new, o

    S, o = lax.scan(step, s0, (to_chunks(q), to_chunks(k), to_chunks(log_f), to_chunks(v)))
    o = o.transpose(1, 0, 3, 2, 4).reshape(B_, L, H, dv).astype(v.dtype)
    return o, S

def hgrn2_bidirectional(q_lat, f_lat, i_lat, q_ctx, f_ctx, i_ctx, lb):
    B_ = q_lat.shape[0]
    s0 = jnp.zeros((B_, B_HEADS, B_KEY_DIM, B_VAL_DIM), jnp.float32)
    o_lat, o_ctx = None, None
    for d in range(2):
        flip = (lambda a: a) if d == 0 else (lambda a: a[:, ::-1])
        k_l, lf_l = forget_gate(f_lat[d], lb[d])
        k_c, lf_c = forget_gate(f_ctx[d], lb[d])
        oc, s_ctx = hgrn2_chunk_scan(flip(q_ctx), flip(k_c), flip(lf_c), flip(i_ctx), s0)
        ol, _ = hgrn2_chunk_scan(flip(q_lat), flip(k_l), flip(lf_l), flip(i_lat), s_ctx)
        o_lat = flip(ol) if o_lat is None else o_lat + flip(ol)
        o_ctx = flip(oc) if o_ctx is None else o_ctx + flip(oc)
    return o_lat, o_ctx

def even_mixer(h_lat, h_ctx, w_in, w_out, q_norm_w, k_norm_w, lb, out_norm_w, with_ctx_out):
    def project(h):
        B_, n = h.shape[:2]
        aq, ak, av, bq, bff, bfb, bi, bg = jnp.split(h @ w_in, EVEN_SPLITS, axis=-1)
        bshape = (B_, n, B_HEADS, B_KEY_DIM)
        return (aq.reshape(B_, n, A_Q_HEADS, HEAD_DIM_2), ak.reshape(B_, n, A_KV_HEADS, HEAD_DIM_2),
                av.reshape(B_, n, A_KV_HEADS, HEAD_DIM_2), (jax.nn.silu(bq) * HGRN_SCALE).reshape(bshape),
                (bff.reshape(bshape), bfb.reshape(bshape)), bi.reshape(B_, n, B_HEADS, B_VAL_DIM), bg)

    aq_l, ak_l, av_l, bq_l, bf_l, bi_l, bg_l = project(h_lat)
    aq_c, ak_c, av_c, bq_c, bf_c, bi_c, bg_c = project(h_ctx)
    oa_lat, oa_ctx = gqa_axial_attention(aq_l, ak_l, av_l, aq_c, ak_c, av_c, q_norm_w, k_norm_w, with_ctx_out)
    ob_lat, ob_ctx = hgrn2_bidirectional(bq_l, bf_l, bi_l, bq_c, bf_c, bi_c, lb)

    def readout(o, g):
        B_, n = o.shape[:2]
        return (rms_norm(o, out_norm_w).reshape(B_, n, B_V_W) * jax.nn.silu(g)).astype(g.dtype)

    y_lat = jnp.concatenate([oa_lat, readout(ob_lat, bg_l)], axis=-1) @ w_out
    y_ctx = None
    if with_ctx_out:
        y_ctx = jnp.concatenate([oa_ctx, readout(ob_ctx, bg_c)], axis=-1) @ w_out
    return y_lat, y_ctx

def odd_mixer(h_lat, h_ctx, w_qkv, w_out, rpb, with_ctx_out):
    B_, L, _ = h_lat.shape
    n_ctx = h_ctx.shape[1]
    rows = L // GRID_W
    wr = min(NA_ROWS, rows)
    qkv = (h_lat @ w_qkv).reshape(B_, rows, GRID_W, 3, C_HEADS, HEAD_DIM_2)
    q, k, v = qkv[:, :, :, 0], qkv[:, :, :, 1], qkv[:, :, :, 2]
    qkv_c = (h_ctx @ w_qkv).reshape(B_, n_ctx, 3, C_HEADS, HEAD_DIM_2)
    q_c, k_c, v_c = qkv_c[:, :, 0], qkv_c[:, :, 1], qkv_c[:, :, 2]

    r_start = jnp.clip(jnp.arange(rows) - wr // 2, 0, rows - wr)
    c_start = jnp.clip(jnp.arange(GRID_W) - NA_COLS // 2, 0, GRID_W - NA_COLS)
    c_idx = c_start[:, None] + jnp.arange(NA_COLS)
    dx = c_idx - jnp.arange(GRID_W)[:, None] + (NA_COLS - 1)

    def row_block(inp):
        r, q_r = inp
        r0 = r_start[r]
        k_band = lax.dynamic_slice_in_dim(k, r0, wr, axis=1)
        v_band = lax.dynamic_slice_in_dim(v, r0, wr, axis=1)
        k_win = k_band[:, :, c_idx]
        v_win = v_band[:, :, c_idx]
        dy = r0 + jnp.arange(wr) - r + (NA_ROWS - 1)
        bias = rpb[:, dy[:, None, None], dx[None, :, :]].transpose(0, 2, 1, 3)
        s_loc = jnp.einsum("bqhd,brqjhd->bhqrj", q_r, k_win).astype(jnp.float32) * ATTN_SCALE
        s_loc = (s_loc + bias[None].astype(jnp.float32)).reshape(B_, C_HEADS, GRID_W, wr * NA_COLS)
        s_ctx = jnp.einsum("bqhd,bchd->bhqc", q_r, k_c).astype(jnp.float32) * ATTN_SCALE
        p = jax.nn.softmax(jnp.concatenate([s_loc, s_ctx], axis=-1), axis=-1).astype(v.dtype)
        p_loc = p[..., :wr * NA_COLS].reshape(B_, C_HEADS, GRID_W, wr, NA_COLS)
        p_ctx = p[..., wr * NA_COLS:]
        return jnp.einsum("bhqrj,brqjhd->bqhd", p_loc, v_win) + jnp.einsum("bhqc,bchd->bqhd", p_ctx, v_c)

    o = lax.map(row_block, (jnp.arange(rows), q.transpose(1, 0, 2, 3, 4)))
    y_lat = o.transpose(1, 0, 2, 3, 4).reshape(B_, L, C_W) @ w_out
    y_ctx = None
    if with_ctx_out:
        s = jnp.einsum("bqhd,bkhd->bhqk", q_c, k_c).astype(jnp.float32) * ATTN_SCALE
        p = jax.nn.softmax(s, axis=-1).astype(v_c.dtype)
        y_ctx = jnp.einsum("bhqk,bkhd->bqhd", p, v_c).reshape(B_, n_ctx, C_W) @ w_out
    return y_lat, y_ctx

def conv_ffn(h, w_up, conv_w, conv_b, w_down):
    u = h @ w_up
    u = lax.conv_general_dilated(u, conv_w[:, None, :], window_strides=(1,),
                                 padding=[(CONV_W // 2, CONV_W // 2)],
                                 dimension_numbers=("NWC", "WIO", "NWC"),
                                 feature_group_count=u.shape[-1]) + conv_b
    a, g = jnp.split(u, 2, axis=-1)
    return (jax.nn.silu(g) * a) @ w_down

def second_inputs(seed: int = 0) -> dict:
    key = jax.random.key(seed)
    ks = jax.random.split(key, 24)

    def nrm(k, shape, s):
        return jax.random.normal(k, shape, jnp.float32) * s

    return {
        "x": nrm(ks[0], (BATCH, SEQ, D_MODEL), 1.0),
        "c": nrm(ks[1], (BATCH, D_MODEL), 1.0),
        "ctx": nrm(ks[2], (BATCH, CTX_LEN, D_MODEL), 1.0),
        "c_ctx": nrm(ks[3], (D_MODEL,), 1.0),
        "w_mod": nrm(ks[4], (DEPTH, D_MODEL, 6 * D_MODEL), D_MODEL ** -0.5),
        "b_mod": nrm(ks[5], (DEPTH, 6 * D_MODEL), 0.02),
        "norm_pre_mix": 1.0 + nrm(ks[6], (DEPTH, D_MODEL), 0.1),
        "norm_post_mix": 1.0 + nrm(ks[7], (DEPTH, D_MODEL), 0.1),
        "norm_pre_ffn": 1.0 + nrm(ks[8], (DEPTH, D_MODEL), 0.1),
        "norm_post_ffn": 1.0 + nrm(ks[9], (DEPTH, D_MODEL), 0.1),
        "even_w_in": nrm(ks[10], (N_EVEN, D_MODEL, EVEN_IN_W), D_MODEL ** -0.5),
        "even_w_out": nrm(ks[11], (N_EVEN, EVEN_OUT_W, D_MODEL), EVEN_OUT_W ** -0.5),
        "even_q_norm": 1.0 + nrm(ks[12], (N_EVEN, HEAD_DIM_2), 0.1),
        "even_k_norm": 1.0 + nrm(ks[13], (N_EVEN, HEAD_DIM_2), 0.1),
        "hgrn_lb_logits": nrm(ks[14], (N_EVEN, 2, B_K_W), 1.0),
        "hgrn_out_norm": 1.0 + nrm(ks[15], (N_EVEN, B_VAL_DIM), 0.1),
        "odd_w_qkv": nrm(ks[16], (N_ODD, D_MODEL, 3 * C_W), D_MODEL ** -0.5),
        "odd_w_out": nrm(ks[17], (N_ODD, C_W, D_MODEL), C_W ** -0.5),
        "odd_rpb": nrm(ks[18], (N_ODD, C_HEADS, 2 * NA_ROWS - 1, 2 * NA_COLS - 1), 0.1),
        "ffn_w_up": nrm(ks[19], (DEPTH, D_MODEL, 2 * D_FF), D_MODEL ** -0.5),
        "ffn_conv_w": nrm(ks[20], (DEPTH, CONV_W, 2 * D_FF), CONV_W ** -0.5),
        "ffn_conv_b": nrm(ks[21], (DEPTH, 2 * D_FF), 0.02),
        "ffn_w_down": nrm(ks[22], (DEPTH, D_FF, D_MODEL), D_FF ** -0.5),
    }

def second_block(x, c, ctx, c_ctx, w_mod, b_mod, norm_pre_mix, norm_post_mix, norm_pre_ffn, norm_post_ffn,
              even_w_in, even_w_out, even_q_norm, even_k_norm, hgrn_lb_logits, hgrn_out_norm,
              odd_w_qkv, odd_w_out, odd_rpb, ffn_w_up, ffn_conv_w, ffn_conv_b, ffn_w_down):
    p_lb = jax.nn.softmax(hgrn_lb_logits.astype(jnp.float32), axis=0)
    lb_all = jnp.concatenate([jnp.zeros_like(p_lb[:1]), jnp.cumsum(p_lb[1:], axis=0)], axis=0)
    lb_all = lb_all.reshape(N_EVEN, 2, B_HEADS, B_KEY_DIM)

    for l in range(DEPTH):
        with_ctx_out = l < DEPTH - 1
        mod_lat = (jax.nn.silu(c) @ w_mod[l] + b_mod[l])[:, None, :]
        mod_ctx = (jax.nn.silu(c_ctx) @ w_mod[l] + b_mod[l])[None, None, :]
        sh1, sc1, g1, sh2, sc2, g2 = jnp.split(mod_lat, 6, axis=-1)
        sh1c, sc1c, g1c, sh2c, sc2c, g2c = jnp.split(mod_ctx, 6, axis=-1)

        h_lat = rms_norm(x, norm_pre_mix[l]) * (1.0 + sc1) + sh1
        h_ctx = rms_norm(ctx, norm_pre_mix[l]) * (1.0 + sc1c) + sh1c
        if l % 2 == 0:
            e = l // 2
            y_lat, y_ctx = even_mixer(h_lat, h_ctx, even_w_in[e], even_w_out[e], even_q_norm[e], even_k_norm[e],
                                      lb_all[e], hgrn_out_norm[e], with_ctx_out)
        else:
            o = l // 2
            y_lat, y_ctx = odd_mixer(h_lat, h_ctx, odd_w_qkv[o], odd_w_out[o], odd_rpb[o], with_ctx_out)
        x = x + g1 * rms_norm(y_lat, norm_post_mix[l])

        h_lat = rms_norm(x, norm_pre_ffn[l]) * (1.0 + sc2) + sh2
        x = x + g2 * rms_norm(conv_ffn(h_lat, ffn_w_up[l], ffn_conv_w[l], ffn_conv_b[l], ffn_w_down[l]), norm_post_ffn[l])
        if with_ctx_out:
            ctx = ctx + g1c * rms_norm(y_ctx, norm_post_mix[l])
            h_ctx = rms_norm(ctx, norm_pre_ffn[l]) * (1.0 + sc2c) + sh2c
            ctx = ctx + g2c * rms_norm(conv_ffn(h_ctx, ffn_w_up[l], ffn_conv_w[l], ffn_conv_b[l], ffn_w_down[l]), norm_post_ffn[l])
    return x


def setup_inputs(seed=0):
    out = dict(first_inputs(seed))
    for name, value in second_inputs(seed + 1).items():
        if name != "x":
            out[name + "_2"] = value
    return out


def reference(
    x, ln1_g, ln1_b, ffn1_w_gate, ffn1_w_up, ffn1_w_down, w_in, b_gate, pool_w, pool_scale,
    cmp_pos_k, cmp_k_w1, cmp_k_w2, cmp_pos_v, cmp_v_w1, cmp_v_w2, w_out, ln2_g, ln2_b,
    ffn2_w_gate, ffn2_w_up, ffn2_w_down, ln3_g, ln3_b, c_2, ctx_2, c_ctx_2, w_mod_2, b_mod_2,
    norm_pre_mix_2, norm_post_mix_2, norm_pre_ffn_2, norm_post_ffn_2, even_w_in_2, even_w_out_2,
    even_q_norm_2, even_k_norm_2, hgrn_lb_logits_2, hgrn_out_norm_2, odd_w_qkv_2, odd_w_out_2,
    odd_rpb_2, ffn_w_up_2, ffn_conv_w_2, ffn_conv_b_2, ffn_w_down_2,
):
    x = first_block(
        x, ln1_g, ln1_b, ffn1_w_gate, ffn1_w_up, ffn1_w_down, w_in, b_gate, pool_w, pool_scale,
        cmp_pos_k, cmp_k_w1, cmp_k_w2, cmp_pos_v, cmp_v_w1, cmp_v_w2, w_out, ln2_g, ln2_b,
        ffn2_w_gate, ffn2_w_up, ffn2_w_down, ln3_g, ln3_b,
    )
    return second_block(
        x, c_2, ctx_2, c_ctx_2, w_mod_2, b_mod_2, norm_pre_mix_2, norm_post_mix_2,
        norm_pre_ffn_2, norm_post_ffn_2, even_w_in_2, even_w_out_2, even_q_norm_2,
        even_k_norm_2, hgrn_lb_logits_2, hgrn_out_norm_2, odd_w_qkv_2, odd_w_out_2, odd_rpb_2,
        ffn_w_up_2, ffn_conv_w_2, ffn_conv_b_2, ffn_w_down_2,
    )


_drawn_inputs = setup_inputs


def setup_inputs(seed=0):
    import zlib

    import numpy as np

    out = dict(_drawn_inputs(seed))
    spreads = {}
    factors = {'pool_scale': 8.0,
     'cmp_pos_k': 57.01,
     'cmp_pos_v': 8.0,
     'even_q_norm_2': 6.966,
     'even_k_norm_2': 8.0,
     'odd_rpb_2': 8.0,
     'ffn_conv_b_2': 4.206}
    for name, (base, spread) in spreads.items():
        noise = np.random.default_rng([zlib.crc32(name.encode()), seed]).standard_normal(out[name].shape)
        drawn = base * np.exp(spread * noise) if base else spread * noise
        out[name] = jnp.asarray(drawn.astype(out[name].dtype))
    for name, factor in factors.items():
        out[name] = (out[name] * factor).astype(out[name].dtype)
    return out
```

```python
from contextlib import ExitStack, contextmanager

import numpy as np

import concourse.bass as bass
from concourse import mybir

class Buffers:
    pass


class Unit:

    def __init__(self, q, key, n, bias, v, out):
        self.q, self.key, self.n, self.bias, self.v, self.out = q, key, n, bias, v, out


class Conv:

    def __init__(self, tap, bias):
        self.tap, self.bias = tap, bias


F32 = mybir.dt.float32
ALU = mybir.AluOpType
ACT = mybir.ActivationFunctionType
AX = mybir.AxisListType
ds = bass.ds

P = 128
D = 1024
FT = D // P
S = 256
CTX = 256
TT = S // P
DEPTH = 2
D_FF = 2816
NF = D_FF // P
BANK = 512

ALPHA = (2.0 * DEPTH) ** 0.25
LN_EPS = 1e-5
RMS_EPS = 1e-6
NEG = -1e30

POOL_WINDOWS = (2, 4, 8, 16)
POOL_C = 64
HD = 96
NH = 8
NG = 2
HPG = NH // NG
KVW = NG * HD
STRIDE = 16
CBLK = 32
NC = S // STRIDE - 1
U0, Q0 = 0, 256
KC0, VC0, KS0, VS0, KW0, VW0, G0 = (1024 + i * KVW for i in range(7))
D_IN = G0 + 3 * NH

HD2 = 64
GQ, GKV = 8, 2
BH = 4
HGRN_SCALE = 128 ** -0.5
BQ0 = GQ * HD2 + 2 * GKV * HD2
LEVELS = (1, 2, 4, 8, 16, 32, 64)
NLV = len(LEVELS)
CUM = (NLV + 2) * P
NSC = (NLV + 1) * P
GW = 64
NROW = S // GW
CH = 16
NAC = 16
DY = 15
DX = 31
CONV = 3
CT = 2 * NF

PAR = dict(ln1_g=0, ln1_b=16, ln2_g=32, ln2_b=48, ln3_g=64, ln3_b=80, pre_mix=96, post_mix=112,
           pre_ffn=128, post_ffn=144, b_mod=160, conv_w=256, conv_b=640, pool_scale=768, c=772, c_ctx=780)
PAR_TILES = 7


def conv_col(l, j):
    row = (l * CONV + j) * CT
    return PAR["conv_w"] + row // 88 * P + row % 88


def shape_constants():
    c = {}
    eye = np.eye(P, dtype=np.float32)
    c["c_ident"] = eye
    c["c_alpha"] = (np.float32(ALPHA) * eye).astype(np.float32)
    c["c_mean"] = np.full((P, P), 1.0 / D, np.float32)
    i = np.arange(P)
    c["c_causal"] = np.where(i[None, :] <= i[:, None], 0.0, NEG).astype(np.float32)
    t = np.arange(S)
    ends = np.arange(NC) * STRIDE + CBLK - 1
    cm = np.where(ends[None, :] <= t[:, None], 0.0, NEG).astype(np.float32)
    c["c_cmp"] = cm.reshape(TT, P, NC).transpose(1, 0, 2).copy()
    c["c_any"] = (t >= ends[0]).astype(np.float32).reshape(TT, P).T.copy()
    band = np.zeros((S, len(POOL_WINDOWS), S), np.float32)
    for g, w in enumerate(POOL_WINDOWS):
        for tt in range(S):
            band[max(tt + 1 - w, 0):tt + 1, g, tt] = 1.0 / min(tt + 1, w)
        band[t, g, t] -= 1.0
    c["c_band"] = band.reshape(TT, P, len(POOL_WINDOWS), S).transpose(1, 0, 2, 3).copy()
    nf = HD2 // 4
    inv = 10000.0 ** (-np.arange(nf, dtype=np.float32) / np.float32(nf))
    ang = np.concatenate([(t // GW)[:, None] * inv, (t % GW)[:, None] * inv], axis=1).astype(np.float32)
    for name, f in (("c_cos", np.cos), ("c_sin", np.sin)):
        c[name] = f(ang).astype(np.float32).reshape(TT, P, 2 * nf).transpose(1, 0, 2).copy()
    u, tc = i[:, None], i[None, :]
    cum = np.zeros((2, P, NLV + 2, P), np.float32)
    msk = np.zeros((2, P, NLV + 1, P), np.float32)
    for n, h in enumerate(LEVELS):
        mid = tc // (2 * h) * 2 * h + h
        late = tc % (2 * h) >= h
        cum[0, :, n + 1] = np.where(late, (u >= mid) & (u <= tc), (u > tc) & (u < mid))
        cum[1, :, n + 1] = np.where(late, (u >= mid) & (u < tc), (u >= tc) & (u < mid))
        same = u // (2 * h) == tc // (2 * h)
        msk[0, :, n] = same & (u % (2 * h) < h) & late
        msk[1, :, n] = same & (u % (2 * h) >= h) & ~late
    cum[0, :, 0], cum[0, :, NLV + 1] = u > tc, u <= tc
    cum[1, :, 0], cum[1, :, NLV + 1] = u < tc, u >= tc
    msk[:, :, NLV] = eye
    c["c_cum"] = cum.transpose(1, 0, 2, 3).reshape(P, 2, CUM).copy()
    c["c_lvl"] = msk.transpose(1, 0, 2, 3).reshape(P, 2, NSC).copy()
    start = np.clip(np.arange(GW) - NAC // 2, 0, GW - NAC)
    pick = np.zeros((2, 32, GW, 2, GW), np.float32)
    for q in range(GW):
        for k in range(GW):
            x = k - q + NAC - 1 if start[q] <= k < start[q] + NAC else DX
            for r in range(2):
                pick[r, x, k, r, q] = 1.0
    c["c_pick"] = pick.reshape(2 * 32, GW, P).copy()
    return c


@contextmanager
def phase(nc, names):
    with ExitStack() as ctx:
        handles = [ctx.enter_context(nc.semaphore(f"{n}_{nc.next_id()}")) for n in names]
        s = dict(zip(names, handles))
        with nc.Block() as block:
            yield block, s
        for h in handles:
            nc.gpsimd.sem_clear(h)
        nc.all_engine_barrier()


class Chain:

    def __init__(self, eng, sem, base=0):
        self.eng, self.sem, self.base, self.n = eng, sem, base, 0

    def link(self, ins):
        self.n += 1
        ins.then_inc(self.sem, 1)
        self.eng.wait_ge(self.sem, self.base + self.n)


def params_phase(nc, k, w):
    names = ["zeroed", "rows_in", "consts_in", "turned", "x_in", "x_turned", "x_used"]
    with ExitStack() as ctx:
        rows = ctx.enter_context(nc.sbuf_tensor("par_rows", [P, PAR_TILES, P], F32))
        x_rows = ctx.enter_context(nc.sbuf_tensor("x_rows", [P, 4, D], F32))
        vectors = [("ln1_g", 0, 0), ("ln1_b", 0, 16), ("ln2_g", 0, 32), ("ln2_b", 0, 48), ("ln3_g", 0, 64),
                   ("ln3_b", 0, 80), ("norm_pre_mix_2", 0, 96), ("norm_post_mix_2", 0, 112),
                   ("norm_pre_ffn_2", 1, 0), ("norm_post_ffn_2", 1, 16), ("b_mod_2", 1, 32),
                   ("ffn_conv_b_2", 5, 0), ("pool_scale", 6, 0), ("c_2", 6, 4), ("c_ctx_2", 6, 12)]
        consts = [(k.ident[:, :], w["c_ident"]), (k.alpha[:, :], w["c_alpha"]), (k.mean[:, :], w["c_mean"]), (k.causal[:, :], w["c_causal"]),
                  (k.cmp_mask[:, :, :], w["c_cmp"]), (k.any_cmp[:, :], w["c_any"])]
        n_rows = len(vectors) + CONV
        with phase(nc, names) as (block, s):

            @block.sync
            def _(sp):
                for dst, src in consts:
                    sp.dma_start(dst, src).then_inc(s["consts_in"], 16)
                for tt in range(TT):
                    sp.dma_start(x_rows[:, tt, :], w["x"][0, tt * P:(tt + 1) * P, :]).then_inc(s["x_in"], 16)
                    sp.dma_start(x_rows[:, TT + tt, :], w["ctx_2"][0, tt * P:(tt + 1) * P, :]).then_inc(s["x_in"], 16)
                sp.wait_ge(s["zeroed"], 1)
                for name, tile, r in vectors:
                    a = w[name]
                    src = a.rearrange("(r p) -> r p", p=P) if len(a.shape) == 1 else a.rearrange("l (r p) -> (l r) p", p=P)
                    sp.dma_start(rows[r:r + src.shape[0], tile, :], src).then_inc(s["rows_in"], 16)
                taps = w["ffn_conv_w_2"].rearrange("l j (r p) -> (l j r) p", p=P)
                for n in range(CONV):
                    sp.dma_start(rows[0:88, 2 + n, :], taps[88 * n:88 * n + 88, :]).then_inc(s["rows_in"], 16)

            @block.gpsimd
            def _(pool):
                pool.memset(rows[:, :, :], 0.0).then_inc(s["zeroed"], 1)
                pool.memset(k.eps[:, 0:1], LN_EPS)
                pool.memset(k.eps[:, 1:2], RMS_EPS)
                pool.memset(k.eps[:, 2:3], 1.0)
                pool.memset(k.zero[:, :], 0.0)
                pool.memset(k.one_row[:, :], 1.0)

            @block.tensor
            def _(pe):
                pe.wait_ge(s["consts_in"], 16 * len(consts))
                pe.wait_ge(s["x_in"], 16 * 2 * TT)
                for f in range(FT):
                    if f >= 4:
                        pe.wait_ge(s["x_used"], f - 3)
                    for tt in range(2 * TT):
                        last = pe.transpose(k.ps[:, f % 4, tt * P:(tt + 1) * P], x_rows[:, tt, f * P:(f + 1) * P],
                                            k.ident[:, :])
                    last.then_inc(s["x_turned"], 1)
                pe.wait_ge(s["rows_in"], 16 * n_rows)
                for n in range(PAR_TILES):
                    last = pe.transpose(k.ps[:, 4 + n // 4, n % 4 * P:(n % 4 + 1) * P], rows[:, n, :], k.ident[:, :])
                last.then_inc(s["turned"], 1)

            @block.vector
            def _(dve):
                for f in range(FT):
                    dve.wait_ge(s["x_turned"], f + 1)
                    dve.tensor_copy(k.x_T[:, f, :], k.ps[:, f % 4, :]).then_inc(s["x_used"], 1)
                dve.wait_ge(s["turned"], 1)
                dve.tensor_copy(k.par[:, 0:512], k.ps[:, 4, :])
                dve.tensor_copy(k.par[:, 512:PAR_TILES * P], k.ps[:, 5, 0:(PAR_TILES - 4) * P])


LN_SEMS = ["ln_stats", "ln_mv", "ln_std", "ln_rstd", "ln_z", "ln_turned"]


def ln_vector(dve, k, s, t, par_g, par_b):
    for tt in range(TT):
        for n in range(2):
            dve.bn_stats(t.stats[:, tt, n, :], k.ps[:, 2 * tt + n, :]).then_inc(s["ln_stats"], 1)
        dve.wait_ge(s["ln_stats"], 2 * tt + 2)
        dve.bn_aggr(t.mv[:, tt, :], t.stats[:, tt, :, :]).then_inc(s["ln_mv"], 1)
    for tt in range(TT):
        dve.wait_ge(s["ln_std"], tt + 1)
        dve.reciprocal(t.rstd[:, tt:tt + 1], t.std[:, tt:tt + 1]).then_inc(s["ln_rstd"], 1)
        dve.wait_ge(s["ln_rstd"], tt + 1)
        dve.tensor_scalar(t.z[:, tt, :], k.ps[:, 2 * tt:2 * tt + 2, :].rearrange("p b n -> p (b n)"),
                          t.mv[:, tt, 0:1], t.rstd[:, tt:tt + 1], ALU.subtract, ALU.mult).then_inc(s["ln_z"], 1)
    for f in (2, 3, 6, 7):
        dve.wait_ge(s["ln_turned"], f // 2 + 1)
        dve.tensor_scalar(k.x_T[:, f, 0:S], turned(k, f), par_g(f), par_b(f), ALU.mult, ALU.add)


def ln_scalar(act, k, s, t, par_g, par_b):
    for tt in range(TT):
        act.wait_ge(s["ln_mv"], tt + 1)
        act.activation(t.std[:, tt:tt + 1], t.mv[:, tt, 1:2], ACT.Sqrt, bias=k.eps[:, 0:1]).then_inc(s["ln_std"], 1)
    for f in (0, 1, 4, 5):
        act.wait_ge(s["ln_turned"], f // 2 + 1)
        act.activation(k.x_T[:, f, 0:S], turned(k, f), ACT.Identity, bias=par_b(f), scale=par_g(f))


def turned(k, f):
    return k.ps[:, 4 + f // 2, f % 2 * S:(f % 2 + 1) * S]


def turn_tensor(pe, k, z, z_ready, sem):
    pe.wait_ge(z_ready, TT)
    for f in range(FT):
        for tt in range(TT):
            last = pe.transpose(turned(k, f)[:, tt * P:(tt + 1) * P], z[:, tt, f * P:(f + 1) * P], k.ident[:, :])
        if f % 2:
            last.then_inc(sem, 1)


def ln_buffers(nc, ctx):
    def sb(name, shape):
        return ctx.enter_context(nc.sbuf_tensor(f"{name}_{nc.next_id()}", shape, F32))
    got = Buffers()
    got.stats = sb("ln_stats_b", [P, TT, 2, 6])
    got.mv = sb("ln_mv_b", [P, TT, 2])
    got.std = sb("ln_std_b", [P, TT])
    got.rstd = sb("ln_rstd_b", [P, TT])
    got.z = sb("ln_z_b", [P, TT, D])
    return got


POST_SEMS = ["po_sq", "po_ss", "po_std", "po_r", "po_z", "po_turned"]


def post_scalar(act, k, s, t):
    for tt in range(TT):
        act.activation(t.z[:, tt, :], k.ps[:, 2 * tt:2 * tt + 2, :].rearrange("p b n -> p (b n)"), ACT.Square,
                       accum_out=t.mv[:, tt, 0:1]).then_inc(s["po_sq"], 1)
    for tt in range(TT):
        act.wait_ge(s["po_sq"], tt + 1)
        act.activation(t.std[:, tt:tt + 1], t.mv[:, tt, 0:1], ACT.Sqrt, bias=k.eps[:, 1:2], scale=1.0 / D).then_inc(s["po_std"], 1)


def post_vector(dve, k, s, t, gain, cols):
    for tt in range(TT):
        dve.wait_ge(s["po_std"], tt + 1)
        dve.reciprocal(t.rstd[:, tt:tt + 1], t.std[:, tt:tt + 1]).then_inc(s["po_r"], 1)
        dve.wait_ge(s["po_r"], tt + 1)
        dve.tensor_scalar(t.z[:, tt, :], k.ps[:, 2 * tt:2 * tt + 2, :].rearrange("p b n -> p (b n)"),
                          t.rstd[:, tt:tt + 1], None, ALU.mult).then_inc(s["po_z"], 1)
    for f in range(FT):
        dve.wait_ge(s["po_turned"], f // 2 + 1)
        dve.scalar_tensor_tensor(k.x_T[:, f, cols:cols + S], turned(k, f), gain(f), k.x_T[:, f, cols:cols + S],
                                 ALU.mult, ALU.add)


def ffn_phase(nc, k, w_gate, w_up, w_down, src, ln=None, conv=None, post=None):
    names = ["gu0_in", "gu1_in", "dn0_in", "dn1_in", "gu_done", "act_done", "mid_done", "h_ready", "down_done"]
    names += LN_SEMS if ln else POST_SEMS
    with ExitStack() as ctx:
        def sb(name, shape):
            return ctx.enter_context(nc.sbuf_tensor(f"{name}_{nc.next_id()}", shape, F32))
        wgu = [sb(f"w_gu{n}", [P, 2, FT, P]) for n in range(2)]
        wdn = [sb(f"w_dn{n}", [P, D]) for n in range(2)]
        sil = [sb(f"silu{n}", [P, S]) for n in range(2)]
        hid = [sb(f"hid{n}", [P, S]) for n in range(2)]
        cv = [sb(f"conv{n}", [P, 2, S]) for n in range(2)] if conv else None
        t = ln_buffers(nc, ctx)
        with phase(nc, names) as (block, s):
            gu_in, dn_in = [s["gu0_in"], s["gu1_in"]], [s["dn0_in"], s["dn1_in"]]

            def gu(n):
                return k.ps[:, 4 + n, :].rearrange("p (a t) -> p a t", a=2)

            @block.sync
            def _(sp):
                def load_gu(i, n):
                    sp.dma_start(wgu[n][:, 0, :, :], w_gate[i]).then_inc(gu_in[n], 16)
                    sp.dma_start(wgu[n][:, 1, :, :], w_up[i]).then_inc(gu_in[n], 16)

                def load_dn(i, n):
                    sp.dma_start(wdn[n][:, :], w_down[i]).then_inc(dn_in[n], 16)

                for n in range(2):
                    load_gu(n, n)
                    load_dn(n, n)
                with sp.Fori(0, NF // 2 - 1) as j:
                    for n in range(2):
                        sp.wait_ge(s["gu_done"], j * 2 + n + 1)
                        load_gu(j * 2 + (n + 2), n)
                        sp.wait_ge(s["down_done"], j * 2 + n + 1)
                        load_dn(j * 2 + (n + 2), n)

            @block.tensor
            def _(pe):
                def gate_up(n, arrived):
                    pe.wait_ge(gu_in[n], arrived)
                    for a in range(2):
                        for f in range(FT):
                            last = pe.matmul(gu(n)[:, a, :], wgu[n][:, a, f, :], src(f), start=(f == 0), stop=(f == FT - 1))
                    last.then_inc(s["gu_done"], 1)

                def down(n, arrived, tile, first=False, end=False):
                    pe.wait_ge(dn_in[n], arrived)
                    pe.wait_ge(s["h_ready"], tile + 1)
                    for tt in range(TT):
                        for c in range(2):
                            last = pe.matmul(k.ps[:, 2 * tt + c, :], hid[n][:, tt * P:(tt + 1) * P],
                                             wdn[n][:, c * BANK:(c + 1) * BANK], start=first, stop=end,
                                             skip_group_check=True)
                    last.then_inc(s["down_done"], 1)

                if ln:
                    for tt in range(TT):
                        for f in range(FT):
                            pe.matmul(k.ps[:, 2 * tt + f // 4, f % 4 * P:(f % 4 + 1) * P], k.x_T[:, f, tt * P:(tt + 1) * P],
                                      k.alpha[:, :], start=(f % 4 == 0), stop=False, skip_group_check=True)
                gate_up(0, 32)
                gate_up(1, 32)
                down(0, 16, 0, first=not ln)
                with pe.Fori(0, NF // 2 - 1) as j:
                    pe.wait_ge(s["h_ready"], j * 2 + 1)
                    gate_up(0, j * 32 + 64)
                    down(1, j * 16 + 16, j * 2 + 1)
                    pe.wait_ge(s["h_ready"], j * 2 + 2)
                    gate_up(1, j * 32 + 64)
                    down(0, j * 16 + 32, j * 2 + 2)
                down(1, 16 * (NF // 2), NF - 1, end=True)
                turn_tensor(pe, k, t.z, s["ln_z"] if ln else s["po_z"], s["ln_turned"] if ln else s["po_turned"])

            @block.scalar
            def _(act):
                with act.Fori(0, NF // 2) as j:
                    for n in range(2):
                        act.wait_ge(s["gu_done"], j * 2 + n + 1)
                        if conv is None:
                            act.activation(sil[n][:, :], gu(n)[:, 0, :], ACT.Silu).then_inc(s["act_done"], 1)
                        else:
                            for a in range(2):
                                act.activation(cv[n][:, a, :], gu(n)[:, a, :], ACT.Identity,
                                               bias=conv.bias(j * 2 + n, a), scale=conv.tap(1, j * 2 + n, a)).then_inc(s["act_done"], 1)
                            act.wait_ge(s["mid_done"], j * 8 + 4 * n + 4)
                            act.activation(sil[n][:, :], cv[n][:, 1, :], ACT.Silu).then_inc(s["act_done"], 1)
                act.wait_ge(s["down_done"], NF)
                if ln:
                    ln_scalar(act, k, s, t, *ln)
                else:
                    post_scalar(act, k, s, t)

            @block.vector
            def _(dve):
                with dve.Fori(0, NF // 2) as j:
                    for n in range(2):
                        if conv is None:
                            dve.wait_ge(s["act_done"], j * 2 + n + 1)
                            dve.scalar_tensor_tensor(hid[n][:, :], sil[n][:, :], 0.5, gu(n)[:, 1, :], ALU.mult,
                                                     ALU.mult).then_inc(s["h_ready"], 1)
                        else:
                            for a in range(2):
                                dve.wait_ge(s["act_done"], j * 6 + 3 * n + 2)
                                dve.scalar_tensor_tensor(cv[n][:, a, 1:S], gu(n)[:, a, 0:S - 1], conv.tap(0, j * 2 + n, a),
                                                         cv[n][:, a, 1:S], ALU.mult, ALU.add).then_inc(s["mid_done"], 1)
                            for a in range(2):
                                dve.wait_ge(s["mid_done"], j * 8 + 4 * n + a + 1)
                                dve.scalar_tensor_tensor(cv[n][:, a, 0:S - 1], gu(n)[:, a, 1:S], conv.tap(2, j * 2 + n, a),
                                                         cv[n][:, a, 0:S - 1], ALU.mult, ALU.add).then_inc(s["mid_done"], 1)
                            dve.wait_ge(s["act_done"], j * 6 + 3 * n + 3)
                            dve.tensor_tensor(hid[n][:, :], sil[n][:, :], cv[n][:, 0, :], ALU.mult).then_inc(s["h_ready"], 1)
                dve.wait_ge(s["down_done"], NF)
                if ln:
                    ln_vector(dve, k, s, t, *ln)
                else:
                    post_vector(dve, k, s, t, *post)


def out_phase(nc, k, chunks, ln=None, post=None):
    names = ["sum_done"] + (LN_SEMS if ln else POST_SEMS)
    with ExitStack() as ctx:
        t = ln_buffers(nc, ctx)
        with phase(nc, names) as (block, s):

            @block.tensor
            def _(pe):
                if ln:
                    for tt in range(TT):
                        for f in range(FT):
                            pe.matmul(k.ps[:, 2 * tt + f // 4, f % 4 * P:(f % 4 + 1) * P], k.x_T[:, f, tt * P:(tt + 1) * P],
                                      k.alpha[:, :], start=(f % 4 == 0), stop=False, skip_group_check=True)
                for tt in range(TT):
                    for n, (stationary, moving) in enumerate(chunks):
                        for c in range(2):
                            last = pe.matmul(k.ps[:, 2 * tt + c, :], stationary(tt), moving[:, c * BANK:(c + 1) * BANK],
                                             start=(n == 0 and not ln), stop=(n == len(chunks) - 1), skip_group_check=True)
                last.then_inc(s["sum_done"], 1)
                turn_tensor(pe, k, t.z, s["ln_z"] if ln else s["po_z"], s["ln_turned"] if ln else s["po_turned"])

            @block.scalar
            def _(act):
                act.wait_ge(s["sum_done"], 1)
                if ln:
                    ln_scalar(act, k, s, t, *ln)
                else:
                    post_scalar(act, k, s, t)

            @block.vector
            def _(dve):
                dve.wait_ge(s["sum_done"], 1)
                if ln:
                    ln_vector(dve, k, s, t, *ln)
                else:
                    post_vector(dve, k, s, t, *post)


def mixer1_project(nc, k, m, w, l):
    names = ["w_in", "pool_in", "cmp_in", "pos_in", "tok_done", "tok_used", "feat_done", "feat_used", "q_done", "q_used",
             "pos_turned", "pos_ready", "blocks_ready", "hid_done", "hid_ready", "cmp_done", "band_done", "band_used",
             "mix_done", "gate_ready"]
    FEAT = (KC0, VC0, KS0, KW0)
    with ExitStack() as ctx:
        def sb(name, shape):
            return ctx.enter_context(nc.sbuf_tensor(f"{name}_{nc.next_id()}", shape, F32))
        win = sb("w_in_b", [P, FT, D_IN])
        w1 = sb("cmp_w1_b", [HD, 2, CBLK, HD])
        w2 = sb("cmp_w2_b", [HD, 2, HD])
        pos_rows = sb("pos_rows", [CBLK, 2, HD])
        pos = sb("pos_T", [HD, 2, CBLK])
        blocks = sb("cmp_blocks", [HD, 2, CBLK, NG, NC])
        hidden = sb("cmp_hidden", [HD, 2, NG, NC])
        pool_w = sb("pool_w_b", [P, 2, POOL_C])
        band = sb("band_b", [P, TT, len(POOL_WINDOWS), S])
        u_tok = sb("u_tok", [P, TT, 256])
        pooled = sb("pooled", [P, 2, S])
        with phase(nc, names) as (block, s):

            @block.sync
            def _(sp):
                w_in = w["w_in"].rearrange("l (f p) n -> l p f n", p=P)
                for f in range(FT):
                    sp.dma_start(win[:, f, :], w_in[l, :, f, :]).then_inc(s["w_in"], 16)
                sp.dma_start(k.b_gate[0:1, :], w["b_gate"].unsqueeze(1)[l]).then_inc(s["w_in"], 16)
                for n, kv in enumerate("kv"):
                    sp.dma_start(pos_rows[:, n, :], w[f"cmp_pos_{kv}"][l]).then_inc(s["pos_in"], 16)
                for n, kv in enumerate("kv"):
                    sp.dma_start(w1[:, n, :, :], w[f"cmp_{kv}_w1"].rearrange("l (c d) j -> l d c j", d=HD)[l]).then_inc(s["cmp_in"], 16)
                    sp.dma_start(w2[:, n, :], w[f"cmp_{kv}_w2"][l]).then_inc(s["cmp_in"], 16)
                sp.dma_start(band[:, :, :, :], w["c_band"]).then_inc(s["pool_in"], 16)
                pw = w["pool_w"].rearrange("l (a b) c d -> l b c a d", b=2)
                for b in range(2):
                    sp.dma_start(pool_w[64 * b:64 * b + 64, :, :], pw[l, b]).then_inc(s["pool_in"], 16)

            @block.tensor
            def _(pe):
                pe.wait_ge(s["pos_in"], 32)
                for n in range(2):
                    last = pe.transpose(k.ps[0:HD, 7, n * CBLK:(n + 1) * CBLK], pos_rows[:, n, :], k.ident[0:CBLK, 0:CBLK])
                last.then_inc(s["pos_turned"], 1)
                pe.wait_ge(s["w_in"], 16 * (FT + 1))
                for tt in range(TT):
                    for bank, at, col, n in ((tt, 0, U0, 256), (tt, 256, VS0, KVW), (2 + tt, 0, VW0, KVW + 3 * NH)):
                        for f in range(FT):
                            last = pe.matmul(k.ps[:, bank, at:at + n], k.x_T[:, f, tt * P:(tt + 1) * P], win[:, f, col:col + n],
                                             start=(f == 0), stop=(f == FT - 1), skip_group_check=True)
                    last = pe.matmul(k.ps[:, 2 + tt, KVW:KVW + 3 * NH], k.one_row[0:1, :], k.b_gate[0:1, :], start=False,
                                     stop=True, skip_group_check=True)
                    last.then_inc(s["tok_done"], 1)
                for n, col in enumerate(FEAT):
                    if n == 3:
                        pe.wait_ge(s["pos_ready"], 1)
                    for g in range(NG):
                        for f in range(FT):
                            last = pe.matmul(k.ps[0:HD, 4 + n, g * S:(g + 1) * S], win[:, f, col + g * HD:col + (g + 1) * HD],
                                             k.x_T[:, f, 0:S], start=(f == 0), stop=(f == FT - 1), skip_group_check=True)
                    last.then_inc(s["feat_done"], 1)
                for n in range(NH // 2):
                    if n < 2:
                        pe.wait_ge(s["tok_used"], 4 * TT)
                    else:
                        pe.wait_ge(s["q_used"], n - 1)
                    for a in range(2):
                        for f in range(FT):
                            h = 2 * n + a
                            last = pe.matmul(k.ps[0:HD, n % 2, a * S:(a + 1) * S], win[:, f, Q0 + h * HD:Q0 + (h + 1) * HD],
                                             k.x_T[:, f, 0:S], start=(f == 0), stop=(f == FT - 1), skip_group_check=True)
                    last.then_inc(s["q_done"], 1)
                pe.wait_ge(s["pool_in"], 48)
                for g in range(4):
                    for tt in range(TT):
                        last = pe.matmul(k.ps[64 * (g % 2):64 * (g % 2) + 64, 2 + g // 2, 0:S], u_tok[:, tt, g * POOL_C:(g + 1) * POOL_C],
                                         band[:, tt, g, :], start=(tt == 0), stop=(tt == TT - 1), skip_group_check=True)
                last.then_inc(s["band_done"], 1)
                pe.wait_ge(s["cmp_in"], 64)
                for n in range(2):
                    pe.wait_ge(s["blocks_ready"], 4 * n + 4)
                    for c in range(CBLK):
                        last = pe.matmul(k.ps[0:HD, 4 + n, 0:NG * NC], w1[:, n, c, :], blocks[:, n, c, :, :].rearrange("d g b -> d (g b)"),
                                         start=(c == 0), stop=(c == CBLK - 1))
                    last.then_inc(s["hid_done"], 1)
                pe.wait_ge(s["band_used"], 2)
                for g in range(4):
                    r = 64 * (g % 2)
                    last = pe.matmul(k.ps[r:r + 64, 2 + g // 2, S:2 * S], pool_w[r:r + 64, g // 2, :], pooled[r:r + 64, g // 2, :],
                                     start=True, stop=True, skip_group_check=True)
                last.then_inc(s["mix_done"], 1)
                pe.wait_ge(s["feat_used"], 2)
                pe.wait_ge(s["hid_ready"], 2)
                pe.matmul(k.ps[0:HD, 6, 0:NG * NC], w2[:, 0, :], hidden[:, 0, :, :].rearrange("d g b -> d (g b)"), start=True, stop=True)
                for g in range(NG):
                    last = pe.matmul(k.ps[0:NC, 7, g * HD:(g + 1) * HD], hidden[:, 1, g, :], w2[:, 1, :], start=True, stop=True,
                                     skip_group_check=True)
                last.then_inc(s["cmp_done"], 1)

            @block.scalar
            def _(act):
                for tt in range(TT):
                    act.wait_ge(s["tok_done"], tt + 1)
                    act.activation(m.gates[:, tt, :], k.ps[:, 2 + tt, KVW:KVW + 3 * NH], ACT.Sigmoid).then_inc(s["gate_ready"], 1)
                    act.activation(m.v_win[:, tt, :], k.ps[:, 2 + tt, 0:KVW], ACT.Copy).then_inc(s["tok_used"], 2)
                for n in range(2):
                    act.wait_ge(s["feat_done"], 3 + n)
                    act.activation((m.ks_T, m.kw_T)[n][:, :, :].rearrange("d g t -> d (g t)"), k.ps[0:HD, 6 + n, :], ACT.Copy).then_inc(s["feat_used"], 1)
                for n in range(NH // 2):
                    act.wait_ge(s["q_done"], n + 1)
                    act.activation(m.q_T[:, 2 * n:2 * n + 2, :].rearrange("d h t -> d (h t)"), k.ps[0:HD, n % 2, :], ACT.Copy,
                                   scale=HD ** -0.5).then_inc(s["q_used"], 1)
                act.wait_ge(s["band_done"], 1)
                for a in range(2):
                    act.activation(pooled[:, a, :], k.ps[:, 2 + a, 0:S], ACT.Copy).then_inc(s["band_used"], 1)
                for n in range(2):
                    act.wait_ge(s["hid_done"], n + 1)
                    act.activation(hidden[:, n, :, :].rearrange("d g b -> d (g b)"), k.ps[0:HD, 4 + n, 0:NG * NC], ACT.Gelu_apprx_tanh).then_inc(s["hid_ready"], 1)
                act.wait_ge(s["cmp_done"], 1)
                act.activation(m.kc_T[:, :, :].rearrange("d g b -> d (g b)"), k.ps[0:HD, 6, 0:NG * NC], ACT.Copy)
                act.activation(m.v_cmp[:, :, :].rearrange("b g d -> b (g d)"), k.ps[0:NC, 7, 0:KVW], ACT.Copy)

            @block.vector
            def _(dve):
                dve.wait_ge(s["pos_turned"], 1)
                dve.tensor_copy(pos[:, :, :].rearrange("d n c -> d (n c)"), k.ps[0:HD, 7, 0:2 * CBLK]).then_inc(s["pos_ready"], 1)
                for tt in range(TT):
                    dve.wait_ge(s["tok_done"], tt + 1)
                    dve.tensor_copy(u_tok[:, tt, :], k.ps[:, tt, 0:256])
                    dve.tensor_copy(m.v_slc[:, tt, :], k.ps[:, tt, 256:256 + KVW]).then_inc(s["tok_used"], 2)
                    dve.wait_ge(s["gate_ready"], tt + 1)
                    g_cmp = m.gates[:, tt, :].rearrange("p (h b) -> p h b", b=3)[:, :, 0]
                    dve.tensor_scalar(g_cmp, g_cmp, k.any_cmp[:, tt:tt + 1], None, ALU.mult)
                dve.wait_ge(s["pos_ready"], 1)
                for n in range(2):
                    dve.wait_ge(s["feat_done"], n + 1)
                    for g in range(NG):
                        toks = k.ps[0:HD, 4 + n, g * S:(g + 1) * S].rearrange("d (b c) -> d c b", c=STRIDE)
                        for half in range(2):
                            c0 = half * STRIDE
                            dve.tensor_tensor(blocks[:, n, c0:c0 + STRIDE, g, :], toks[:, :, half:half + NC],
                                              pos[:, n, c0:c0 + STRIDE].unsqueeze(2).broadcast_to([HD, STRIDE, NC]),
                                              ALU.add).then_inc(s["blocks_ready"], 1)
                dve.wait_ge(s["mix_done"], 1)
                for a in range(2):
                    dve.tensor_scalar(m.y_pool[:, a, :], k.ps[:, 2 + a, S:2 * S], k.col("pool_scale", l * 2 + a), None, ALU.mult)


def mixer1_attend(nc, k, m, w, l):
    names = ["q_staged", "s_done", "max_ready", "e_ready", "rs_step", "p_ready", "t_done", "t_ready", "pv_done", "o_used",
             "out_w"]
    UNITS = [(g, tt) for g in range(NG) for tt in range(TT)]
    NU = len(UNITS)
    with ExitStack() as ctx:
        def sb(name, shape):
            return ctx.enter_context(nc.sbuf_tensor(f"{name}_{nc.next_id()}", shape, F32))
        q_st = sb("q_staged_b", [HD, NG, S])
        nmax = sb("nmax", [P, 2, 3])
        sums = sb("sums", [P, 2, 3])
        rs = sb("rs", [P, 2, 3])
        e = sb("e_b", [P, 2, 2, S])
        ec = sb("ec_b", [P, 2, NC])
        pt = sb("pt_b", [P, 2, 2, TT, P])
        ptc = sb("ptc_b", [NC, 2, P])
        with phase(nc, names) as (block, s):

            @block.sync
            def _(sp):
                sp.dma_start(m.wo_pool[:, :, :], w["w_out"].rearrange("l (a p) n -> l p a n", p=P)[l, :, 0:2, :]).then_inc(s["out_w"], 16)
                sp.dma_start(m.wo_att[:, :, :], w["w_out"][l, 256:D, :].rearrange("(h d) n -> d h n", d=HD)).then_inc(s["out_w"], 16)
                sp.wait_ge(s["out_w"], 32)

            @block.gpsimd
            def _(pool):
                with pool.Fori(0, HPG) as j:
                    for g in range(NG):
                        pool.tensor_copy(q_st[:, g, :], m.q_T[:, ds(j + g * HPG, 1), :].rearrange("d a t -> d (a t)")).then_inc(s["q_staged"], 1)
                    pool.wait_ge(s["o_used"], j * 2 + 2)

            def s_bank(u):
                return k.ps[:, u % 2, :].rearrange("p (b t) -> p b t", b=2)

            def c_bank(u):
                return k.ps[:, 2 + u % 2, 0:NC]

            def ct_bank(u):
                return k.ps[0:NC, 7, 0:P]

            def t_bank(u):
                return k.ps[:, 4 + u % 2, :].rearrange("p (b c t) -> p b c t", b=2, c=TT)

            def o_bank(g):
                return k.ps[0:HD, 6, g * S:(g + 1) * S]

            @block.tensor
            def _(pe):
                with pe.Fori(0, HPG) as j:
                    def scores(u):
                        g, tt = UNITS[u]
                        n = (tt + 1) * P
                        if tt == 0:
                            pe.wait_ge(s["q_staged"], j * 2 + g + 1)
                        if u >= 2:
                            pe.wait_ge(s["e_ready"], j * NU + (u - 1))
                        q = q_st[:, g, tt * P:(tt + 1) * P]
                        for b, key in enumerate((m.ks_T, m.kw_T)):
                            pe.matmul(s_bank(u)[:, b, 0:n], q, key[:, g, 0:n], start=True, stop=False, skip_group_check=True)
                            pe.matmul(s_bank(u)[:, b, n - P:n], k.ident[:, :], k.causal[:, :], start=False, stop=True,
                                      skip_group_check=True)
                        pe.matmul(c_bank(u), q, m.kc_T[:, g, :], start=True, stop=False, skip_group_check=True)
                        pe.matmul(c_bank(u), k.ident[:, :], k.cmp_mask[:, tt, :], start=False, stop=True,
                                  skip_group_check=True).then_inc(s["s_done"], 1)

                    def turn(u):
                        g, tt = UNITS[u]
                        pe.wait_ge(s["p_ready"], j * NU + (u + 1))
                        if u >= 1:
                            pe.wait_ge(s["t_ready"], j * NU + u)
                        for b in range(2):
                            for c in range(tt + 1):
                                pe.transpose(t_bank(u)[:, b, c, :], e[:, u % 2, b, c * P:(c + 1) * P], k.ident[:, :])
                        pe.transpose(ct_bank(u), ec[:, u % 2, :], k.ident[:, :]).then_inc(s["t_done"], 1)

                    def values(u):
                        g, tt = UNITS[u]
                        pe.wait_ge(s["t_ready"], j * NU + (u + 1))
                        o = o_bank(g)[:, tt * P:(tt + 1) * P]
                        pe.matmul(o, m.v_cmp[:, g, :], ptc[:, u % 2, :], start=True, stop=False, skip_group_check=True)
                        for b, v in enumerate((m.v_slc, m.v_win)):
                            for c in range(tt + 1):
                                last = pe.matmul(o, v[:, c, g * HD:(g + 1) * HD], pt[:, u % 2, b, c, :], start=False,
                                                 stop=(b == 1 and c == tt), skip_group_check=True)
                        last.then_inc(s["pv_done"], 1)

                    for u in range(NU + 2):
                        if u < NU:
                            scores(u)
                        if 1 <= u <= NU:
                            turn(u - 1)
                        if u >= 2:
                            values(u - 2)
                    pe.wait_ge(s["o_used"], j * 2 + 2)

            @block.vector
            def _(dve):
                with dve.Fori(0, HPG) as j:
                    for u in range(NU + 1):
                        if u < NU:
                            n = (UNITS[u][1] + 1) * P
                            dve.wait_ge(s["s_done"], j * NU + (u + 1))
                            dve.tensor_reduce(nmax[:, u % 2, 0:1], c_bank(u), AX.X, ALU.max, negate=True)
                            dve.tensor_reduce(nmax[:, u % 2, 1:3], s_bank(u)[:, :, 0:n], AX.X, ALU.max, negate=True).then_inc(s["max_ready"], 1)
                        if u >= 1:
                            v = u - 1
                            g, tt = UNITS[v]
                            n = (tt + 1) * P
                            c = Chain(dve, s["rs_step"], j * (3 * NU) + 3 * v)
                            dve.wait_ge(s["e_ready"], j * NU + (v + 1))
                            c.link(dve.tensor_scalar(rs[:, v % 2, :], sums[:, v % 2, :], 1e-30, None, ALU.max))
                            c.link(dve.reciprocal(rs[:, v % 2, :], rs[:, v % 2, :]))
                            c.link(dve.tensor_tensor(rs[:, v % 2, :], rs[:, v % 2, :], m.gates[:, tt, ds((j + g * HPG) * 3, 3)], ALU.mult))
                            dve.tensor_scalar(ec[:, v % 2, :], ec[:, v % 2, :], rs[:, v % 2, 0:1], None, ALU.mult)
                            for b in range(2):
                                last = dve.tensor_scalar(e[:, v % 2, b, 0:n], e[:, v % 2, b, 0:n], rs[:, v % 2, b + 1:b + 2], None, ALU.mult)
                            last.then_inc(s["p_ready"], 1)

            @block.scalar
            def _(act):
                with act.Fori(0, HPG) as j:
                    for u in range(NU + 1):
                        if u < NU:
                            n = (UNITS[u][1] + 1) * P
                            act.wait_ge(s["max_ready"], j * NU + (u + 1))
                            if u >= 2:
                                act.wait_ge(s["t_done"], j * NU + (u - 1))
                            act.activation(ec[:, u % 2, :], c_bank(u), ACT.Exp, bias=nmax[:, u % 2, 0:1], accum_out=sums[:, u % 2, 0:1])
                            for b in range(2):
                                last = act.activation(e[:, u % 2, b, 0:n], s_bank(u)[:, b, 0:n], ACT.Exp, bias=nmax[:, u % 2, b + 1:b + 2],
                                                      accum_out=sums[:, u % 2, b + 1:b + 2])
                            last.then_inc(s["e_ready"], 1)
                        if u >= 1:
                            v = u - 1
                            g, tt = UNITS[v]
                            act.wait_ge(s["t_done"], j * NU + (v + 1))
                            if v >= 2:
                                act.wait_ge(s["pv_done"], j * NU + (v - 1))
                            act.activation(ptc[:, v % 2, :], ct_bank(v), ACT.Copy)
                            act.activation(pt[:, v % 2, :, 0:tt + 1, :], t_bank(v)[:, :, 0:tt + 1, :], ACT.Copy).then_inc(s["t_ready"], 1)
                    for g in range(NG):
                        act.wait_ge(s["pv_done"], j * NU + NU)
                        act.activation(m.o_T[:, ds(j + g * HPG, 1), :].rearrange("d a t -> d (a t)"), o_bank(g), ACT.Copy).then_inc(s["o_used"], 1)


def mixer1(nc, k, w, l):
    with ExitStack() as ctx:
        def sb(name, shape):
            return ctx.enter_context(nc.sbuf_tensor(f"{name}_{nc.next_id()}", shape, F32))
        m = Buffers()
        m.q_T = sb("q_T", [HD, NH, S])
        m.ks_T = sb("ks_T", [HD, NG, S])
        m.kw_T = sb("kw_T", [HD, NG, S])
        m.kc_T = sb("kc_T", [HD, NG, NC])
        m.v_slc = sb("v_slc", [P, TT, KVW])
        m.v_win = sb("v_win", [P, TT, KVW])
        m.v_cmp = sb("v_cmp", [NC, NG, HD])
        m.gates = sb("gates", [P, TT, 3 * NH])
        m.y_pool = sb("y_pool", [P, 2, S])
        m.o_T = sb("o_T", [HD, NH, S])
        m.wo_pool = sb("wo_pool", [P, 2, D])
        m.wo_att = sb("wo_att", [HD, NH, D])
        mixer1_project(nc, k, m, w, l)
        mixer1_attend(nc, k, m, w, l)
        chunks = [(lambda tt, a=a: m.y_pool[:, a, tt * P:(tt + 1) * P], m.wo_pool[:, a, :]) for a in range(2)]
        chunks += [(lambda tt, h=h: m.o_T[:, h, tt * P:(tt + 1) * P], m.wo_att[:, h, :]) for h in range(NH)]
        out_phase(nc, k, chunks, ln=(lambda f: k.col("ln2_g", l * FT + f), lambda f: k.col("ln2_b", l * FT + f)))


def modulation_phase(nc, k, b, w):
    names = ["w0_in", "w1_in", "c_ready", "mod_done", "mod_used", "gain_step", "rpb_in", "pick_in", "masked", "rpb_turned",
             "rpb_ready", "bias_done", "bias_used"]
    NCH = 6 * D // BANK
    PER = 5
    NJ = 6
    with ExitStack() as ctx:
        def sb(name, shape):
            return ctx.enter_context(nc.sbuf_tensor(f"{name}_{nc.next_id()}", shape, F32))
        wm = [sb(f"w_mod{n}", [P, FT, BANK]) for n in range(2)]
        cs = sb("c_silu", [P, FT, 2])
        pick = sb("pick", [2 * 32, GW, P])
        rpb = sb("rpb_rows", [NJ * CH, 2, 32])
        rpb_T = sb("rpb_T", [2 * 32, NJ * CH])
        with phase(nc, names) as (block, s):
            w_in = [s["w0_in"], s["w1_in"]]
            chunks = w["w_mod_2"].rearrange("l (f p) (c n) -> l c p f n", p=P, n=BANK)

            @block.sync
            def _(sp):
                for n in range(2):
                    sp.dma_start(wm[n][:, :, :], chunks[0, n]).then_inc(w_in[n], 16)
                sp.dma_start(pick[:, :, :], w["c_pick"]).then_inc(s["pick_in"], 16)
                sp.wait_ge(s["masked"], 1)
                for r in range(2):
                    for j in range(NJ):
                        sp.dma_start(rpb[j * CH:(j + 1) * CH, r, 0:DX], w["odd_rpb_2"][0, :, j + 5 - r, :]).then_inc(s["rpb_in"], 16)
                for l in range(DEPTH):
                    with sp.Fori(1 - l, NCH // 2) as j:
                        for n in range(2):
                            sp.wait_ge(s["mod_done"], j * 2 + (l * NCH + n - 1))
                            sp.dma_start(wm[n][:, :, :], chunks[l, j * 2 + n]).then_inc(w_in[n], 16)

            @block.gpsimd
            def _(pool):
                pool.memset(rpb[:, :, :], NEG).then_inc(s["masked"], 1)

            @block.scalar
            def _(act):
                for n, name in enumerate(("c", "c_ctx")):
                    act.activation(cs[:, :, n], k.par[:, PAR[name]:PAR[name] + FT], ACT.Silu).then_inc(s["c_ready"], 1)

            @block.tensor
            def _(pe):
                pe.wait_ge(s["rpb_in"], 16 * 2 * NJ)
                pe.transpose(k.ps[0:64, 6, 0:NJ * CH], rpb[:, :, :].rearrange("a r x -> a (r x)"),
                             k.ident[0:NJ * CH, 0:NJ * CH]).then_inc(s["rpb_turned"], 1)
                pe.wait_ge(s["pick_in"], 16)
                pe.wait_ge(s["rpb_ready"], 1)
                for c in range(GW):
                    n = c // PER
                    if c % PER == 0 and n >= 4:
                        pe.wait_ge(s["bias_used"], n - 3)
                    last = pe.matmul(k.ps[:, 2 + n % 4, c % PER * NJ * CH:(c % PER + 1) * NJ * CH], pick[:, c, :], rpb_T[:, :],
                                     start=True, stop=True, skip_group_check=True)
                    if c % PER == PER - 1 or c == GW - 1:
                        last.then_inc(s["bias_done"], 1)
                pe.wait_ge(s["c_ready"], 2)
                for l in range(DEPTH):
                    with pe.Fori(0, NCH // 2) as j:
                        for n in range(2):
                            pe.wait_ge(w_in[n], j * 16 + (l * NCH // 2 + 1) * 16)
                            for m in range(4):
                                for f in range(FT):
                                    last = pe.matmul(k.ps[:, n, 2 * m:2 * m + 2], wm[n][:, f, m * P:(m + 1) * P], cs[:, f, :],
                                                     start=(f == 0), stop=(f == FT - 1), skip_group_check=True)
                            last.then_inc(s["mod_done"], 1)
                        pe.wait_ge(s["mod_used"], j * 2 + (l * NCH + 2))

            @block.vector
            def _(dve):
                dve.wait_ge(s["rpb_turned"], 1)
                dve.tensor_copy(rpb_T[:, :], k.ps[0:64, 6, 0:NJ * CH]).then_inc(s["rpb_ready"], 1)
                for n in range((GW + PER - 1) // PER):
                    m = min(PER, GW - n * PER)
                    dve.wait_ge(s["bias_done"], n + 1)
                    for j in range(NJ):
                        last = dve.tensor_copy(b.bias[:, :, j, n * PER:n * PER + m].rearrange("p h c -> p c h"),
                                               k.ps[:, 2 + n % 4, 0:m * NJ * CH].rearrange("p (c j h) -> p c j h", j=NJ, h=CH)[:, :, j, :])
                    last.then_inc(s["bias_used"], 1)
                for l in range(DEPTH):
                    with dve.Fori(0, NCH // 2) as j:
                        for n in range(2):
                            dve.wait_ge(s["mod_done"], j * 2 + (l * NCH + n + 1))
                            bias = k.par[:, ds(j * 8 + (PAR["b_mod"] + l * 48 + 4 * n), 4)].unsqueeze(2).broadcast_to([P, 4, 2])
                            dve.tensor_tensor(b.mod[:, l, ds(j * 8 + 4 * n, 4), :], k.ps[:, n, 0:8].rearrange("p (m s) -> p m s", s=2),
                                              bias, ALU.add).then_inc(s["mod_used"], 1)
                dve.wait_ge(s["mod_used"], DEPTH * NCH)
                for l in range(DEPTH):
                    for at, name, plus in ((1, "pre_mix", 1.0), (2, "post_mix", 0.0), (4, "pre_ffn", 1.0), (5, "post_ffn", 0.0)):
                        part = b.mod[:, l, at * FT:(at + 1) * FT, :]
                        weight = k.par[:, PAR[name] + l * FT:PAR[name] + (l + 1) * FT].unsqueeze(2).broadcast_to([P, FT, 2])
                        dve.scalar_tensor_tensor(part, part, plus, weight, ALU.add, ALU.mult)


def prenorm_phase(nc, k, b, l, ffn, streams):
    names = ["sq_done", "sum_done", "std_done", "r_done", "n_done"]
    c0, n = streams[0] * S, len(streams) * S
    with ExitStack() as ctx:
        def sb(name, shape):
            return ctx.enter_context(nc.sbuf_tensor(f"{name}_{nc.next_id()}", shape, F32))
        sq = sb("squares", [P, FT, n])
        std = sb("pre_std", [P, n])
        r = sb("pre_r", [P, n])
        with phase(nc, names) as (block, s):
            def scale(f, st):
                return b.mod[:, l, (4 if ffn else 1) * FT + f, st:st + 1]

            def shift(f, st):
                return b.mod[:, l, (3 if ffn else 0) * FT + f, st:st + 1]

            @block.scalar
            def _(act):
                for f in range(FT):
                    act.activation(sq[:, f, :], k.x_T[:, f, c0:c0 + n], ACT.Square).then_inc(s["sq_done"], 1)
                act.wait_ge(s["sum_done"], 1)
                act.activation(std[:, :], k.ps[:, 0, 0:n], ACT.Sqrt, bias=k.eps[:, 1:2]).then_inc(s["std_done"], 1)
                for f in range(FT):
                    act.wait_ge(s["n_done"], f + 1)
                    for st in streams:
                        cols = slice(st * S, (st + 1) * S)
                        act.activation(b.h_T[:, f, cols], b.h_T[:, f, cols], ACT.Identity, bias=shift(f, st), scale=scale(f, st))

            @block.tensor
            def _(pe):
                for f in range(FT):
                    pe.wait_ge(s["sq_done"], f + 1)
                    last = pe.matmul(k.ps[:, 0, 0:n], k.mean[:, :], sq[:, f, :], start=(f == 0), stop=(f == FT - 1))
                last.then_inc(s["sum_done"], 1)

            @block.vector
            def _(dve):
                dve.wait_ge(s["std_done"], 1)
                dve.reciprocal(r[:, :], std[:, :]).then_inc(s["r_done"], 1)
                dve.wait_ge(s["r_done"], 1)
                for f in range(FT):
                    dve.tensor_tensor(b.h_T[:, f, c0:c0 + n], k.x_T[:, f, c0:c0 + n], r[:, :], ALU.mult).then_inc(s["n_done"], 1)


def gqa_project(nc, k, b, m, w):
    names = ["w_in", "tab_in", "p_done", "p_used", "copied", "sq_done", "ss_done", "std_done", "step", "rot_done", "turned"]
    NQK = GQ + GKV
    with ExitStack() as ctx:
        def sb(name, shape):
            return ctx.enter_context(nc.sbuf_tensor(f"{name}_{nc.next_id()}", shape, F32))
        wq = sb("gqa_w", [P, FT, BQ0])
        gain = sb("qk_gain", [P, NQK, HD2])
        cos, sin = sb("cos", [P, TT, HD2 // 2]), sb("sin", [P, TT, HD2 // 2])
        sq = sb("qk_sq", [P, NQK * HD2])
        ss, std, r = sb("qk_ss", [P, NQK]), sb("qk_std", [P, NQK]), sb("qk_r", [P, NQK])
        part = [sb(f"rot{n}", [P, NQK, HD2 // 2]) for n in range(4)]
        kd = sb("k_twice", [P, 2 * TT, GKV, 2, HD2])
        with phase(nc, names) as (block, s):

            @block.sync
            def _(sp):
                w_in = w["even_w_in_2"][0].rearrange("(f p) n -> p f n", p=P)
                for f in range(FT):
                    sp.dma_start(wq[:, f, :], w_in[:, f, 0:BQ0]).then_inc(s["w_in"], 16)
                for h in range(NQK):
                    g = w["even_q_norm_2"] if h < GQ else w["even_k_norm_2"]
                    sp.dma_start(gain[:, h, :], g.broadcast_to([P, HD2])).then_inc(s["tab_in"], 16)
                sp.dma_start(cos[:, :, :], w["c_cos"]).then_inc(s["tab_in"], 16)
                sp.dma_start(sin[:, :, :], w["c_sin"]).then_inc(s["tab_in"], 16)

            @block.tensor
            def _(pe):
                pe.wait_ge(s["w_in"], 16 * FT)
                for tt in range(2 * TT):
                    if tt >= 2:
                        pe.wait_ge(s["p_used"], tt - 1)
                    for bank, c0, c1 in ((0, 0, BANK), (1, BANK, BQ0)):
                        for f in range(FT):
                            last = pe.matmul(k.ps[:, 2 * (tt % 2) + bank, 0:c1 - c0], b.h_T[:, f, tt * P:(tt + 1) * P], wq[:, f, c0:c1],
                                             start=(f == 0), stop=(f == FT - 1))
                    last.then_inc(s["p_done"], 1)
                pe.wait_ge(s["rot_done"], 2 * TT)
                for g in range(GKV):
                    for tt in range(2 * TT):
                        last = pe.transpose(k.ps[:, 4 + g, tt * P:(tt + 1) * P], kd[:, tt, g, :, :].rearrange("p a d -> p (a d)"), k.ident[:, :])
                    last.then_inc(s["turned"], 1)

            @block.scalar
            def _(act):
                for tt in range(2 * TT):
                    act.wait_ge(s["p_done"], tt + 1)
                    both = k.ps[:, 2 * (tt % 2):2 * (tt % 2) + 2, :].rearrange("p b n -> p (b n)")
                    act.activation(m.qk[:, tt, :], both[:, 0:NQK * HD2], ACT.Copy).then_inc(s["copied"], 1)
                    act.activation(m.v[:, tt, :], both[:, NQK * HD2:BQ0], ACT.Copy).then_inc(s["p_used"], 1)
                    act.wait_ge(s["copied"], tt + 1)
                    if tt >= 1:
                        act.wait_ge(s["std_done"], tt)
                    act.activation(sq[:, :], m.qk[:, tt, :], ACT.Square).then_inc(s["sq_done"], 1)
                    act.wait_ge(s["ss_done"], tt + 1)
                    act.activation(std[:, :], ss[:, :], ACT.Sqrt, bias=k.eps[:, 1:2], scale=1.0 / HD2).then_inc(s["std_done"], 1)
                for g in range(GKV):
                    act.wait_ge(s["turned"], g + 1)
                    act.activation(m.k_T[:, g, :], k.ps[:, 4 + g, :], ACT.Copy)

            @block.vector
            def _(dve):
                c = Chain(dve, s["step"])
                dve.wait_ge(s["tab_in"], 16 * (NQK + 2))
                half = HD2 // 2
                for tt in range(2 * TT):
                    qk = m.qk[:, tt, :].rearrange("p (h d) -> p h d", d=HD2)
                    dve.wait_ge(s["sq_done"], tt + 1)
                    dve.reduce_sum(ss[:, :], sq[:, :].rearrange("p (h d) -> p h d", d=HD2), AX.X).then_inc(s["ss_done"], 1)
                    dve.wait_ge(s["std_done"], tt + 1)
                    c.link(dve.reciprocal(r[:, :], std[:, :]))
                    c.link(dve.tensor_tensor(qk, qk, r[:, :].unsqueeze(2).broadcast_to([P, NQK, HD2]), ALU.mult))
                    c.link(dve.tensor_tensor(qk, qk, gain[:, :, :], ALU.mult))
                    if tt < TT:
                        x1, x2 = qk[:, :, 0:half], qk[:, :, half:HD2]
                        ct, st = (a[:, tt, :].unsqueeze(1).broadcast_to([P, NQK, half]) for a in (cos, sin))
                        dve.tensor_tensor(part[0][:, :, :], x1, ct, ALU.mult)
                        dve.tensor_tensor(part[1][:, :, :], x2, st, ALU.mult)
                        dve.tensor_tensor(part[2][:, :, :], x1, st, ALU.mult)
                        c.link(dve.tensor_tensor(part[3][:, :, :], x2, ct, ALU.mult))
                        dve.tensor_tensor(x1, part[0][:, :, :], part[1][:, :, :], ALU.subtract)
                        c.link(dve.tensor_tensor(x2, part[2][:, :, :], part[3][:, :, :], ALU.add))
                    keys = m.qk[:, tt, GQ * HD2:NQK * HD2].rearrange("p (g d) -> p g d", d=HD2)
                    for a in range(2):
                        last = dve.tensor_copy(kd[:, tt, :, a, :], keys)
                    last.then_inc(s["rot_done"], 1)


def soft_tensor(pe, k, s, a, units, base, extra):
    def scores(u):
        if u >= 2:
            pe.wait_ge(s["e_ready"], base + (u - 1))
        pe.matmul(k.ps[:, u % 2, 0:units[u].n], units[u].q, units[u].key, start=True, stop=True).then_inc(s["s_done"], 1)

    def turn(u):
        pe.wait_ge(s["p_ready"], base + (u + 1))
        if u >= 2:
            pe.wait_ge(s["t_ready"], base + (u - 1))
        for c in range(units[u].n // P):
            last = pe.transpose(k.ps[:, 2 + u % 2, c * P:(c + 1) * P], a.e[:, u % 2, c * P:(c + 1) * P], k.ident[:, :])
        last.then_inc(s["t_done"], 1)

    def values(u):
        pe.wait_ge(s["t_ready"], base + (u + 1))
        for c, v in enumerate(units[u].v):
            last = pe.matmul(units[u].out, v, a.pt[:, u % 2, c, :], start=(c == 0), stop=(c == len(units[u].v) - 1),
                             skip_group_check=True)
        last.then_inc(s["pv_done"], 1)

    nu = len(units)
    for u in range(nu + 2):
        if u < nu:
            extra(u)
            scores(u)
        if 1 <= u <= nu:
            turn(u - 1)
        if u >= 2:
            values(u - 2)


def soft_vector(dve, k, s, a, units, base):
    nu = len(units)
    for u in range(nu + 1):
        if u < nu:
            n, bias = units[u].n, units[u].bias
            dve.wait_ge(s["s_done"], base + (u + 1))
            if bias is not None:
                part = k.ps[:, u % 2, 0:S].rearrange("p (r c) -> p r c", c=GW)
                dve.tensor_tensor(part, part, bias, ALU.add).then_inc(s["bias_step"], 1)
                dve.wait_ge(s["bias_step"], base + (u + 1))
            dve.reduce_max(a.nmax[:, u % 2:u % 2 + 1], k.ps[:, u % 2, 0:n], AX.X, negate=True).then_inc(s["max_ready"], 1)
        if u >= 1:
            v = u - 1
            dve.wait_ge(s["e_ready"], base + (v + 1))
            dve.reciprocal(a.rs[:, v % 2:v % 2 + 1], a.sums[:, v % 2:v % 2 + 1]).then_inc(s["rs_step"], 1)
            dve.wait_ge(s["rs_step"], base + (v + 1))
            e = a.e[:, v % 2, 0:units[v].n]
            dve.tensor_scalar(e, e, a.rs[:, v % 2:v % 2 + 1], None, ALU.mult).then_inc(s["p_ready"], 1)


def soft_scalar(act, k, s, a, units, base):
    nu = len(units)
    for u in range(nu + 1):
        if u < nu:
            n = units[u].n
            act.wait_ge(s["max_ready"], base + (u + 1))
            if u >= 2:
                act.wait_ge(s["t_done"], base + (u - 1))
            act.activation(a.e[:, u % 2, 0:n], k.ps[:, u % 2, 0:n], ACT.Exp, bias=a.nmax[:, u % 2:u % 2 + 1],
                           accum_out=a.sums[:, u % 2:u % 2 + 1]).then_inc(s["e_ready"], 1)
        if u >= 1:
            v = u - 1
            n = units[v].n
            act.wait_ge(s["t_done"], base + (v + 1))
            if v >= 2:
                act.wait_ge(s["pv_done"], base + (v - 1))
            act.activation(a.pt[:, v % 2, 0:n // P, :].rearrange("p c t -> p (c t)"), k.ps[:, 2 + v % 2, 0:n], ACT.Copy).then_inc(s["t_ready"], 1)


SOFT_SEMS = ["s_done", "bias_step", "max_ready", "e_ready", "rs_step", "p_ready", "t_done", "t_ready", "pv_done"]


def soft_buffers(nc, ctx):
    def sb(name, shape):
        return ctx.enter_context(nc.sbuf_tensor(f"{name}_{nc.next_id()}", shape, F32))
    got = Buffers()
    got.e = sb("soft_e", [P, 2, 2 * S])
    got.pt = sb("soft_pt", [P, 2, 4, P])
    got.nmax = sb("soft_max", [P, 2])
    got.sums = sb("soft_sums", [P, 2])
    got.rs = sb("soft_rs", [P, 2])
    return got


def gqa_attend(nc, k, b, m, w):
    names = ["q_staged", "q_turned", "q_ready", "o_used"] + SOFT_SEMS
    NP = GQ // GKV // 2
    with ExitStack() as ctx:
        def sb(name, shape):
            return ctx.enter_context(nc.sbuf_tensor(f"{name}_{nc.next_id()}", shape, F32))
        q_st = sb("gqa_q_st", [P, GKV, 2 * TT, P])
        q_T = sb("gqa_q_T", [P, GKV, S + CTX])
        a = soft_buffers(nc, ctx)
        with phase(nc, names) as (block, s):
            units = []
            for g in range(GKV):
                for hh in range(2):
                    rows = slice(HD2 * hh, HD2 * hh + HD2)
                    for tt in range(2 * TT):
                        first = 0 if tt < TT else TT
                        units.append(Unit(
                            q=q_T[rows, g, tt * P:(tt + 1) * P], key=m.k_T[rows, g, first * P:S + CTX], n=(2 * TT - first) * P, bias=None,
                            v=[m.v[:, c, g * HD2:(g + 1) * HD2] for c in range(first, 2 * TT)],
                            out=k.ps[rows, 4 + g, tt * P:(tt + 1) * P]))
            nu = len(units)

            @block.gpsimd
            def _(pool):
                with pool.Fori(0, NP) as j:
                    for g in range(GKV):
                        pool.tensor_copy(q_st[:, g, :, :], m.qk[:, :, ds((j + g * NP) * P, P)]).then_inc(s["q_staged"], 1)
                    pool.wait_ge(s["o_used"], j * 2 + 2)

            @block.tensor
            def _(pe):
                with pe.Fori(0, NP) as j:
                    for g in range(GKV):
                        pe.wait_ge(s["q_staged"], j * 2 + (g + 1))
                        for tt in range(2 * TT):
                            last = pe.transpose(k.ps[:, 6 + g, tt * P:(tt + 1) * P], q_st[:, g, tt, :], k.ident[:, :])
                        last.then_inc(s["q_turned"], 1)

                    def queries(u):
                        if u % (nu // GKV) == 0:
                            pe.wait_ge(s["q_ready"], j * 2 + (u // (nu // GKV) + 1))
                    soft_tensor(pe, k, s, a, units, j * nu, queries)
                    pe.wait_ge(s["o_used"], j * 2 + 2)

            @block.vector
            def _(dve):
                with dve.Fori(0, NP) as j:
                    soft_vector(dve, k, s, a, units, j * nu)

            @block.scalar
            def _(act):
                with act.Fori(0, NP) as j:
                    for g in range(GKV):
                        act.wait_ge(s["q_turned"], j * 2 + (g + 1))
                        act.activation(q_T[:, g, :], k.ps[:, 6 + g, :], ACT.Copy, scale=HD2 ** -0.5).then_inc(s["q_ready"], 1)
                    soft_scalar(act, k, s, a, units, j * nu)
                    for g in range(GKV):
                        act.wait_ge(s["pv_done"], j * nu + (g + 1) * (nu // GKV))
                        act.activation(b.y_T[:, ds(j + g * NP, 1), :].rearrange("p a t -> p (a t)"), k.ps[:, 4 + g, :], ACT.Copy).then_inc(s["o_used"], 1)


def odd_attend(nc, k, b, w):
    names = ["w0_in", "w1_in", "proj_done", "proj_used", "o_used"] + SOFT_SEMS
    NPAIR = CH // 2
    with ExitStack() as ctx:
        def sb(name, shape):
            return ctx.enter_context(nc.sbuf_tensor(f"{name}_{nc.next_id()}", shape, F32))
        wq = [sb(f"odd_w{n}", [P, 3, FT, P]) for n in range(2)]
        q_T = sb("odd_q_T", [P, 2, S])
        k_T = sb("odd_k_T", [P, 2, S + CTX])
        v = sb("odd_v", [P, 2, 2 * TT, P])
        a = soft_buffers(nc, ctx)
        with phase(nc, names) as (block, s):
            w_in = [s["w0_in"], s["w1_in"]]
            cols = w["odd_w_qkv_2"][0].rearrange("(f p) (a i n) -> i a p f n", p=P, a=3, n=P)

            def make_units(j):
                units = []
                for pp in range(2):
                    for hh in range(2):
                        rows = slice(HD2 * hh, HD2 * hh + HD2)
                        for tt in range(TT):
                            bias = None if j is None else b.bias[:, ds(j * 4 + (2 * pp + hh), 1), 2 - 2 * tt:2 - 2 * tt + NROW, :].rearrange(
                                "p a r c -> p (a r) c")
                            units.append(Unit(
                                q=q_T[rows, pp, tt * P:(tt + 1) * P], key=k_T[rows, pp, :], n=S + CTX, bias=bias,
                                v=[v[:, pp, c, rows] for c in range(2 * TT)],
                                out=k.ps[rows, 4, pp * S + tt * P:pp * S + (tt + 1) * P]))
                return units
            nu = len(make_units(None))

            @block.sync
            def _(sp):
                def load(i, n):
                    for part in range(3):
                        sp.dma_start(wq[n][:, part, :, :], cols[i, part]).then_inc(w_in[n], 16)
                for n in range(2):
                    load(n, n)
                with sp.Fori(0, NPAIR // 2 - 1) as j:
                    for n in range(2):
                        sp.wait_ge(s["proj_done"], j * 6 + (3 * n + 3))
                        load(j * 2 + (n + 2), n)

            @block.tensor
            def _(pe):
                with pe.Fori(0, NPAIR // 2) as j:
                    for n in range(2):
                        pe.wait_ge(w_in[n], j * 48 + 48)
                        if n == 1:
                            pe.wait_ge(s["proj_used"], j * 6 + 1)
                        for f in range(FT):
                            last = pe.matmul(k.ps[:, 6, 0:S], wq[n][:, 0, f, :], b.h_T[:, f, 0:S], start=(f == 0), stop=(f == FT - 1))
                        last.then_inc(s["proj_done"], 1)
                        if n == 1:
                            pe.wait_ge(s["proj_used"], j * 6 + 2)
                        for f in range(FT):
                            last = pe.matmul(k.ps[:, 7, :], wq[n][:, 1, f, :], b.h_T[:, f, :], start=(f == 0), stop=(f == FT - 1))
                        last.then_inc(s["proj_done"], 1)
                        if n == 1:
                            pe.wait_ge(s["proj_used"], j * 6 + 3)
                        for tt in range(2 * TT):
                            for f in range(FT):
                                last = pe.matmul(k.ps[:, 5, tt * P:(tt + 1) * P], b.h_T[:, f, tt * P:(tt + 1) * P], wq[n][:, 2, f, :],
                                                 start=(f == 0), stop=(f == FT - 1), skip_group_check=True)
                        last.then_inc(s["proj_done"], 1)

                    def pair(u):
                        if u % (nu // 2) == 0:
                            pe.wait_ge(s["proj_used"], j * 6 + (3 * (u // (nu // 2)) + 3))
                    soft_tensor(pe, k, s, a, make_units(None), j * nu, pair)
                    pe.wait_ge(s["o_used"], j + 1)

            @block.vector
            def _(dve):
                with dve.Fori(0, NPAIR // 2) as j:
                    soft_vector(dve, k, s, a, make_units(j), j * nu)

            @block.scalar
            def _(act):
                with act.Fori(0, NPAIR // 2) as j:
                    for n in range(2):
                        act.wait_ge(s["proj_done"], j * 6 + (3 * n + 1))
                        act.activation(q_T[:, n, :], k.ps[:, 6, 0:S], ACT.Copy, scale=HD2 ** -0.5).then_inc(s["proj_used"], 1)
                        act.wait_ge(s["proj_done"], j * 6 + (3 * n + 2))
                        act.activation(k_T[:, n, :], k.ps[:, 7, :], ACT.Copy).then_inc(s["proj_used"], 1)
                        act.wait_ge(s["proj_done"], j * 6 + (3 * n + 3))
                        act.activation(v[:, n, :, :].rearrange("p t d -> p (t d)"), k.ps[:, 5, :], ACT.Copy).then_inc(s["proj_used"], 1)
                    soft_scalar(act, k, s, a, make_units(None), j * nu)
                    act.wait_ge(s["pv_done"], j * nu + nu)
                    act.activation(b.y_T[:, ds(j * 2, 2), 0:S], k.ps[:, 4, :].rearrange("p (a t) -> p a t", a=2), ACT.Copy).then_inc(s["o_used"], 1)


def hgrn_phase(nc, k, b, w):
    names = ["w_in", "tab_in", "proj_done", "q_ready", "q_scaled", "k_ready", "abs_ready", "soft_step", "g_ready", "v_ready", "g_turned",
             "g_tok", "cum_done", "e_ready", "qk_q", "qk_k", "sc_done", "masked", "p_ready", "pv_done", "x_ready", "x_done", "x_used",
             "o_done", "sq_done", "std_done", "r_step", "y_ready", "y_turned", "y_used"]
    TILES = 2 * TT
    NU = 2 * TILES
    UNITS = [(d, tt) for d in range(2) for tt in range(TILES)]
    N9 = NLV + 2
    N8 = NLV + 1
    with ExitStack() as ctx:
        def sb(name, shape):
            return ctx.enter_context(nc.sbuf_tensor(f"{name}_{nc.next_id()}", shape, F32))
        wh = sb("hgrn_w", [P, FT, 5, P])
        cum = sb("hgrn_cum", [P, 2, N9 * P])
        lvl = sb("hgrn_lvl", [P, 2, N8 * P])
        gain = sb("hgrn_gain", [P, P])
        q = sb("hgrn_q", [P, TILES, P])
        kk = sb("hgrn_k", [P, 2, TILES, P])
        ab = sb("hgrn_abs", [P, 2, TILES * P])
        g = sb("hgrn_g", [P, 2, TILES, P])
        g_tok = sb("hgrn_g_tok", [P, 2, TILES, P])
        v = sb("hgrn_v", [P, TILES, P])
        sg = sb("hgrn_gate", [P, TILES, P])
        e = sb("hgrn_e", [P, 2, N9, P])
        kd = sb("hgrn_kd", [P, 2, NLV, P])
        qd = sb("hgrn_qd", [P, 2, NLV, P])
        ke = sb("hgrn_ke", [P, NU, P])
        qs = sb("hgrn_qs", [P, NU, P])
        pm = sb("hgrn_pm", [P, 2, N8, P])
        pr = sb("hgrn_p", [P, 2, P])
        tot = sb("hgrn_tot", [P, NU])
        kx = sb("hgrn_kx", [P, 2, P])
        qx = sb("hgrn_qx", [P, 2, P])
        px = sb("hgrn_px", [P, 2, 6, P])
        sq = sb("hgrn_sq", [P, TILES, P])
        ss, std, r = sb("hgrn_ss", [P, TILES]), sb("hgrn_std", [P, TILES]), sb("hgrn_r", [P, TILES])
        y = sb("hgrn_y", [P, TILES, P])
        with phase(nc, names) as (block, s):
            cols = w["even_w_in_2"][0][:, BQ0:BQ0 + 5 * BH * P].rearrange("(f p) (a i n) -> i a p f n", p=P, a=5, n=P)
            flat = k.ps[:, :, :].rearrange("p b n -> p (b n)")
            CUM_PS = flat[:, 0:N9 * P]
            SC_PS = flat[:, 3 * BANK:3 * BANK + N8 * P]
            X_PS = flat[:, 5 * BANK:5 * BANK + 6 * P]
            O = 7

            def order(d, stream):
                tiles = (0, 1) if stream == 0 else (2, 3)
                return tiles if d == 0 else tiles[::-1]

            def cross(d):
                l0, l1 = order(d, 0)
                c0, c1 = order(d, 1)
                key = lambda tt: ke[:, d * TILES + tt, :]
                qry = lambda tt: qs[:, d * TILES + tt, :]
                return [(c0, c1, key(c0), qry(c1)), (l0, l1, key(l0), qry(l1)),
                        (c0, l0, kx[:, d, :], qry(l0)), (c0, l1, kx[:, d, :], qx[:, d, :]),
                        (c1, l0, key(c1), qry(l0)), (c1, l1, key(c1), qx[:, d, :])]

            @block.sync
            def _(sp):
                sp.dma_start(cum[:, :, :], w["c_cum"]).then_inc(s["tab_in"], 16)
                sp.dma_start(lvl[:, :, :], w["c_lvl"]).then_inc(s["tab_in"], 16)
                sp.dma_start(gain[:, :], w["hgrn_out_norm_2"].broadcast_to([P, P])).then_inc(s["tab_in"], 16)

                def load(i):
                    for part in range(5):
                        sp.dma_start(wh[:, :, part, :], cols[i, part]).then_inc(s["w_in"], 16)
                load(0)
                with sp.Fori(0, BH - 1) as i:
                    sp.wait_ge(s["proj_done"], i * 5 + 5)
                    load(i + 1)

            @block.tensor
            def _(pe):
                pe.wait_ge(s["tab_in"], 48)
                with pe.Fori(0, BH) as i:
                    pe.wait_ge(s["w_in"], i * 80 + 80)
                    for part in range(3):
                        for f in range(FT):
                            last = pe.matmul(k.ps[:, part, :], wh[:, f, part, :], b.h_T[:, f, :], start=(f == 0), stop=(f == FT - 1))
                        last.then_inc(s["proj_done"], 1)
                    for tt in range(TILES):
                        for f in range(FT):
                            last = pe.matmul(k.ps[:, 3 + tt // 2, tt % 2 * 2 * P:(tt % 2 + 1) * 2 * P], b.h_T[:, f, tt * P:(tt + 1) * P],
                                             wh[:, f, 3:5, :].rearrange("p a n -> p (a n)"), start=(f == 0), stop=(f == FT - 1),
                                             skip_group_check=True)
                        if tt % 2:
                            last.then_inc(s["proj_done"], 1)
                    for d in range(2):
                        pe.wait_ge(s["g_ready"], i * 2 + (d + 1))
                        for tt in range(TILES):
                            last = pe.transpose(k.ps[:, 5 + d, tt * P:(tt + 1) * P], g[:, d, tt, :], k.ident[:, :])
                        last.then_inc(s["g_turned"], 1)
                    pe.matmul(k.ps[:, O, :], k.zero[:, :], b.h_T[:, 0, :], start=True, stop=False, skip_group_check=True)
                    pe.wait_ge(s["g_tok"], i * 2 + 2)
                    pe.wait_ge(s["q_ready"], i + 1)
                    pe.wait_ge(s["k_ready"], i * 2 + 2)

                    def sums(u):
                        d, tt = UNITS[u]
                        if u >= 1:
                            pe.wait_ge(s["e_ready"], i * NU + u)
                        for c in range(0, N9 * P, BANK):
                            n = min(BANK, N9 * P - c)
                            last = pe.matmul(CUM_PS[:, c:c + n], g_tok[:, d, tt, :], cum[:, d, c:c + n], start=True, stop=True)
                        last.then_inc(s["cum_done"], 1)

                    def scores(u):
                        d, tt = UNITS[u]
                        pe.wait_ge(s["qk_q"], i * NU + (u + 1))
                        pe.wait_ge(s["qk_k"], i * NU + (u + 1))
                        if u >= 1:
                            pe.wait_ge(s["masked"], i * NU + u)
                        else:
                            pe.wait_ge(s["v_ready"], i * 2 + 2)
                        for n in range(NLV):
                            pe.matmul(SC_PS[:, n * P:(n + 1) * P], kd[:, u % 2, n, :], qd[:, u % 2, n, :], start=True, stop=True,
                                      skip_group_check=True)
                        pe.matmul(SC_PS[:, NLV * P:N8 * P], kk[:, d, tt, :], q[:, tt, :], start=True, stop=True,
                                  skip_group_check=True).then_inc(s["sc_done"], 1)

                    def values(u):
                        d, tt = UNITS[u]
                        pe.wait_ge(s["p_ready"], i * NU + (u + 1))
                        pe.matmul(k.ps[:, O, tt * P:(tt + 1) * P], pr[:, u % 2, :], v[:, tt, :], start=False, stop=False,
                                  skip_group_check=True).then_inc(s["pv_done"], 1)

                    for u in range(NU + 2):
                        if u < NU:
                            sums(u)
                        if 1 <= u <= NU:
                            scores(u - 1)
                        if u >= 2:
                            values(u - 2)
                    for d in range(2):
                        pe.wait_ge(s["x_ready"], i * 2 + (d + 1))
                        if d == 1:
                            pe.wait_ge(s["x_used"], i * 2 + 1)
                        for n, (_, _, key, qry) in enumerate(cross(d)):
                            last = pe.matmul(X_PS[:, n * P:(n + 1) * P], key, qry, start=True, stop=True, skip_group_check=True)
                        last.then_inc(s["x_done"], 1)
                    for d in range(2):
                        pe.wait_ge(s["x_used"], i * 2 + (d + 1))
                        for n, (src, dst, _, _) in enumerate(cross(d)):
                            last = pe.matmul(k.ps[:, O, dst * P:(dst + 1) * P], px[:, d, n, :], v[:, src, :], start=False,
                                             stop=(d == 1), skip_group_check=True)
                    last.then_inc(s["o_done"], 1)
                    pe.wait_ge(s["y_ready"], i + 1)
                    for tt in range(TILES):
                        last = pe.transpose(k.ps[:, 5, tt * P:(tt + 1) * P], y[:, tt, :], k.ident[:, :])
                    last.then_inc(s["y_turned"], 1)
                    pe.wait_ge(s["y_used"], i + 1)

            @block.scalar
            def _(act):
                with act.Fori(0, BH) as i:
                    act.wait_ge(s["proj_done"], i * 5 + 1)
                    act.activation(q[:, :, :].rearrange("p t d -> p (t d)"), k.ps[:, 0, :], ACT.Silu).then_inc(s["q_ready"], 1)
                    for n in range(2):
                        act.wait_ge(s["proj_done"], i * 5 + (4 + n))
                        both = k.ps[:, 3 + n, :].rearrange("p (t a d) -> p t a d", t=2, a=2)
                        act.activation(sg[:, 2 * n:2 * n + 2, :], both[:, :, 1, :], ACT.Silu)
                        act.activation(v[:, 2 * n:2 * n + 2, :], both[:, :, 0, :], ACT.Copy).then_inc(s["v_ready"], 1)
                    for d in range(2):
                        act.activation(kk[:, d, :, :].rearrange("p t d -> p (t d)"), k.ps[:, 1 + d, :], ACT.Sigmoid, scale=-1.0)
                        act.activation(ab[:, d, :], k.ps[:, 1 + d, :], ACT.Abs).then_inc(s["abs_ready"], 1)
                    act.wait_ge(s["abs_ready"], i * 2 + 2)
                    for d in range(2):
                        act.activation(ab[:, d, :], ab[:, d, :], ACT.Exp, scale=-1.0).then_inc(s["soft_step"], 1)
                    act.wait_ge(s["soft_step"], i * 4 + 2)
                    for d in range(2):
                        act.activation(ab[:, d, :], ab[:, d, :], ACT.Ln, bias=k.eps[:, 2:3]).then_inc(s["soft_step"], 1)
                    for d in range(2):
                        act.wait_ge(s["g_turned"], i * 2 + (d + 1))
                        act.activation(g_tok[:, d, :, :].rearrange("p t d -> p (t d)"), k.ps[:, 5 + d, :], ACT.Copy).then_inc(s["g_tok"], 1)
                    for u in range(NU):
                        act.wait_ge(s["cum_done"], i * NU + (u + 1))
                        if u >= 2:
                            act.wait_ge(s["qk_q"], i * NU + (u - 1))
                            act.wait_ge(s["qk_k"], i * NU + (u - 1))
                        act.activation(e[:, u % 2, :, :].rearrange("p n t -> p (n t)"), CUM_PS, ACT.Exp).then_inc(s["e_ready"], 1)
                    for d in range(2):
                        act.wait_ge(s["x_done"], i * 2 + (d + 1))
                        act.activation(px[:, d, :, :].rearrange("p n t -> p (n t)"), X_PS, ACT.Copy).then_inc(s["x_used"], 1)
                    act.wait_ge(s["o_done"], i + 1)
                    for tt in range(TILES):
                        last = act.activation(sq[:, tt, :], k.ps[:, O, tt * P:(tt + 1) * P], ACT.Square, accum_out=ss[:, tt:tt + 1])
                    last.then_inc(s["sq_done"], 1)
                    act.wait_ge(s["sq_done"], i + 1)
                    act.activation(std[:, :], ss[:, :], ACT.Sqrt, bias=k.eps[:, 1:2], scale=1.0 / P).then_inc(s["std_done"], 1)
                    act.wait_ge(s["y_turned"], i + 1)
                    act.activation(b.y_T[:, ds(i + BH, 1), :].rearrange("p a t -> p (a t)"), k.ps[:, 5, :], ACT.Copy).then_inc(s["y_used"], 1)

            @block.gpsimd
            def _(pool):
                with pool.Fori(0, BH) as i:
                    pool.wait_ge(s["abs_ready"], i * 2 + 2)
                    for u in range(NU):
                        d, tt = UNITS[u]
                        pool.wait_ge(s["e_ready"], i * NU + (u + 1))
                        if u >= 2:
                            pool.wait_ge(s["sc_done"], i * NU + (u - 1))
                        pool.tensor_tensor(ke[:, u, :], e[:, u % 2, 0, :], kk[:, d, tt, :], ALU.mult)
                        pool.tensor_tensor(kd[:, u % 2, :, :], e[:, u % 2, 1:N8, :], kk[:, d, tt, :].unsqueeze(1).broadcast_to([P, NLV, P]),
                                           ALU.mult).then_inc(s["qk_k"], 1)

            @block.vector
            def _(dve):
                with dve.Fori(0, BH) as i:
                    dve.wait_ge(s["q_ready"], i + 1)
                    q_all = q[:, :, :].rearrange("p t d -> p (t d)")
                    dve.tensor_scalar(q_all, q_all, HGRN_SCALE, None, ALU.mult).then_inc(s["q_scaled"], 1)
                    for d in range(2):
                        dve.wait_ge(s["soft_step"], i * 4 + (3 + d))
                        dve.scalar_tensor_tensor(g[:, d, :, :].rearrange("p t d -> p (t d)"), k.ps[:, 1 + d, :], 0.0, ab[:, d, :], ALU.min,
                                                 ALU.subtract).then_inc(s["g_ready"], 1)
                    dve.wait_ge(s["g_ready"], i * 2 + 2)
                    dve.wait_ge(s["v_ready"], i * 2 + 2)
                    dve.tensor_tensor(sg[:, :, :], sg[:, :, :], gain[:, :].unsqueeze(1).broadcast_to([P, TILES, P]), ALU.mult).then_inc(s["k_ready"], 2)
                    dve.wait_ge(s["q_scaled"], i + 1)

                    def probs(u):
                        dve.wait_ge(s["sc_done"], i * NU + (u + 1))
                        if u >= 2:
                            dve.wait_ge(s["p_ready"], i * NU + (u - 1))
                        dve.tensor_tensor(pm[:, u % 2, :, :].rearrange("p n t -> p (n t)"), SC_PS, lvl[:, UNITS[u][0], :], ALU.mult).then_inc(s["masked"], 1)
                        dve.wait_ge(s["masked"], i * NU + (u + 1))
                        if u >= 2:
                            dve.wait_ge(s["pv_done"], i * NU + (u - 1))
                        dve.reduce_sum(pr[:, u % 2, :], pm[:, u % 2, :, :].rearrange("p n t -> p t n"), AX.X).then_inc(s["p_ready"], 1)

                    for u in range(NU + 1):
                        if u < NU:
                            d, tt = UNITS[u]
                            dve.wait_ge(s["e_ready"], i * NU + (u + 1))
                            end = P - 1 if d == 0 else 0
                            dve.tensor_copy(tot[:, u:u + 1], e[:, u % 2, N9 - 1, end:end + 1])
                            dve.tensor_tensor(qs[:, u, :], e[:, u % 2, N8, :], q[:, tt, :], ALU.mult)
                            dve.tensor_tensor(qd[:, u % 2, :, :], e[:, u % 2, 1:N8, :], q[:, tt, :].unsqueeze(1).broadcast_to([P, NLV, P]),
                                              ALU.mult).then_inc(s["qk_q"], 1)
                        if u >= 1:
                            probs(u - 1)
                    dve.wait_ge(s["qk_q"], i * NU + NU)
                    dve.wait_ge(s["qk_k"], i * NU + NU)
                    for d in range(2):
                        l0, l1 = order(d, 0)
                        c0, c1 = order(d, 1)
                        dve.tensor_scalar(kx[:, d, :], ke[:, d * TILES + c0, :], tot[:, d * TILES + c1:d * TILES + c1 + 1], None, ALU.mult)
                        dve.tensor_scalar(qx[:, d, :], qs[:, d * TILES + l1, :], tot[:, d * TILES + l0:d * TILES + l0 + 1], None,
                                          ALU.mult).then_inc(s["x_ready"], 1)
                    dve.wait_ge(s["std_done"], i + 1)
                    dve.reciprocal(r[:, :], std[:, :]).then_inc(s["r_step"], 1)
                    dve.wait_ge(s["r_step"], i + 1)
                    for tt in range(TILES):
                        last = dve.scalar_tensor_tensor(y[:, tt, :], k.ps[:, O, tt * P:(tt + 1) * P], r[:, tt:tt + 1], sg[:, tt, :],
                                                        ALU.mult, ALU.mult)
                    last.then_inc(s["y_ready"], 1)


def load_out(nc, k, dst, src):
    with phase(nc, ["out_w"]) as (block, s):
        @block.sync
        def _(sp):
            sp.dma_start(dst[:, :, :], src.rearrange("(f p) n -> p f n", p=P)).then_inc(s["out_w"], 16)
            sp.wait_ge(s["out_w"], 16)


def second_block(nc, k, w):
    with ExitStack() as ctx:
        def sb(stack, name, shape):
            return stack.enter_context(nc.sbuf_tensor(f"{name}_{nc.next_id()}", shape, F32))
        b = Buffers()
        b.h_T = sb(ctx, "h_T", [P, FT, S + CTX])
        b.y_T = sb(ctx, "y_T", [P, FT, S + CTX])
        b.mod = sb(ctx, "mod", [P, DEPTH, 6 * FT, 2])
        b.bias = sb(ctx, "na_bias", [P, CH, 6, GW])
        modulation_phase(nc, k, b, w)

        def ffn(l, st):
            prenorm_phase(nc, k, b, l, True, [st])
            up = w["ffn_w_up_2"][l].rearrange("(f p) (a i n) -> a i p f n", p=P, a=2, n=P)
            conv = Conv(
                tap=lambda n, i, a: k.par[:, ds(i + (conv_col(l, n) + a * NF), 1)],
                bias=lambda i, a: k.par[:, ds(i + (PAR["conv_b"] + l * CT + a * NF), 1)])
            ffn_phase(nc, k, up[0], up[1], w["ffn_w_down_2"][l].rearrange("(i p) n -> i p n", p=P),
                      lambda f: b.h_T[:, f, st * S:(st + 1) * S], conv=conv,
                      post=(lambda f: b.mod[:, l, 5 * FT + f, st:st + 1], st * S))

        def project_out(l, src, streams):
            with ExitStack() as inner:
                wo = sb(inner, "w_out2", [P, FT, D])
                load_out(nc, k, wo, src)
                for st in streams:
                    chunks = [(lambda tt, f=f: b.y_T[:, f, st * S + tt * P:st * S + (tt + 1) * P], wo[:, f, :]) for f in range(FT)]
                    out_phase(nc, k, chunks, post=(lambda f: b.mod[:, l, 2 * FT + f, st:st + 1], st * S))

        prenorm_phase(nc, k, b, 0, False, [0, 1])
        with ExitStack() as inner:
            m = Buffers()
            m.qk = sb(inner, "gqa_qk", [P, 2 * TT, (GQ + GKV) * HD2])
            m.v = sb(inner, "gqa_v", [P, 2 * TT, GKV * HD2])
            m.k_T = sb(inner, "gqa_k_T", [P, GKV, S + CTX])
            gqa_project(nc, k, b, m, w)
            gqa_attend(nc, k, b, m, w)
        hgrn_phase(nc, k, b, w)
        project_out(0, w["even_w_out_2"][0], [0, 1])
        ffn(0, 0)
        ffn(0, 1)
        prenorm_phase(nc, k, b, 1, False, [0, 1])
        odd_attend(nc, k, b, w)
        project_out(1, w["odd_w_out_2"][0], [0])
        ffn(1, 0)


def build(nc, w, out):
    with ExitStack() as ctx:
        def sb(name, shape):
            return ctx.enter_context(nc.sbuf_tensor(f"{name}_{nc.next_id()}", shape, F32))
        k = Buffers()
        k.ps = ctx.enter_context(nc.psum_tensor("ps", [P, 8, BANK], F32))
        k.x_T = sb("x_T", [P, FT, S + CTX])
        k.ident = sb("ident", [P, P])
        k.alpha = sb("alpha", [P, P])
        k.mean = sb("mean", [P, P])
        k.par = sb("par", [P, PAR_TILES * P])
        k.eps = sb("eps", [P, 3])
        k.zero = sb("zero", [P, P])
        k.one_row = sb("one_row", [1, P])
        k.b_gate = sb("b_gate_b", [1, 3 * NH])
        k.causal = sb("causal", [P, P])
        k.cmp_mask = sb("cmp_mask", [P, TT, NC])
        k.any_cmp = sb("any_cmp", [P, TT])
        k.col = lambda name, i: k.par[:, ds(i + PAR[name], 1)]
        params_phase(nc, k, w)

        def hidden_tiles(name):
            return w[name].rearrange("l (f p) (i n) -> l i p f n", p=P, n=P)

        def down_tiles(name):
            return w[name].rearrange("l (i p) n -> l i p n", p=P)

        with nc.Fori(0, DEPTH) as l:
            for n in (1, 2):
                ffn_phase(nc, k, hidden_tiles(f"ffn{n}_w_gate")[l], hidden_tiles(f"ffn{n}_w_up")[l], down_tiles(f"ffn{n}_w_down")[l],
                          lambda f: k.x_T[:, f, 0:S], ln=(lambda f, v=2 * n - 1: k.col(f"ln{v}_g", l * FT + f),
                                                          lambda f, v=2 * n - 1: k.col(f"ln{v}_b", l * FT + f)))
                if n == 1:
                    mixer1(nc, k, w, l)
        second_block(nc, k, w)
        store_phase(nc, k, out)


def store_phase(nc, k, out):
    with ExitStack() as ctx:
        rows = ctx.enter_context(nc.sbuf_tensor("out_rows", [P, TT, D], F32))
        with phase(nc, ["turned", "ready", "stored"]) as (block, s):

            @block.tensor
            def _(pe):
                for tt in range(TT):
                    for f in range(FT):
                        last = pe.transpose(k.ps[:, 2 * tt + f // 4, f % 4 * P:(f % 4 + 1) * P], k.x_T[:, f, tt * P:(tt + 1) * P],
                                            k.ident[:, :])
                    last.then_inc(s["turned"], 1)

            @block.vector
            def _(dve):
                for tt in range(TT):
                    dve.wait_ge(s["turned"], tt + 1)
                    dve.tensor_copy(rows[:, tt, :], k.ps[:, 2 * tt:2 * tt + 2, :].rearrange("p b n -> p (b n)")).then_inc(s["ready"], 1)

            @block.sync
            def _(sp):
                for tt in range(TT):
                    sp.wait_ge(s["ready"], tt + 1)
                    sp.dma_start(out[0, tt * P:(tt + 1) * P, :], rows[:, tt, :]).then_inc(s["stored"], 16)
                sp.wait_ge(s["stored"], 16 * TT)


_INS = ['x', 'ln1_g', 'ln1_b', 'ffn1_w_gate', 'ffn1_w_up', 'ffn1_w_down', 'w_in', 'b_gate', 'pool_w', 'pool_scale',
        'cmp_pos_k', 'cmp_k_w1', 'cmp_k_w2', 'cmp_pos_v', 'cmp_v_w1', 'cmp_v_w2', 'w_out', 'ln2_g', 'ln2_b',
        'ffn2_w_gate', 'ffn2_w_up', 'ffn2_w_down', 'ln3_g', 'ln3_b', 'c_2', 'ctx_2', 'c_ctx_2', 'w_mod_2', 'b_mod_2',
        'norm_pre_mix_2', 'norm_post_mix_2', 'norm_pre_ffn_2', 'norm_post_ffn_2', 'even_w_in_2', 'even_w_out_2',
        'even_q_norm_2', 'even_k_norm_2', 'hgrn_out_norm_2', 'odd_w_qkv_2', 'odd_w_out_2', 'odd_rpb_2', 'ffn_w_up_2',
        'ffn_conv_w_2', 'ffn_conv_b_2', 'ffn_w_down_2']


def kernel(**inputs):
    import concourse.bacc as _bacc
    from concourse.bass_utils import run_bass_kernel_spmd as _run

    nc = _bacc.Bacc("TRN2", target_bir_lowering=False, num_devices=1)
    arrays, w = {}, {}
    host = {name: np.ascontiguousarray(inputs[name]) for name in _INS}
    host.update(shape_constants())
    for name, a in host.items():
        arrays[f"in_{name}"] = a
        w[name] = nc.dram_tensor(f"in_{name}", a.shape, mybir.dt.from_np(a.dtype), kind="ExternalInput").ap()
    out = nc.dram_tensor("out", (1, S, D), F32, kind="ExternalOutput").ap()
    build(nc, w, out)
    r = _run(nc, [arrays], core_ids=[0])
    return r.results[0]["out"]
```

```python
from contextlib import ExitStack, contextmanager

import numpy as np

import concourse.bass as bass
from concourse import mybir

class Buffers:
    pass


class Unit:

    def __init__(self, q, key, n, bias, v, out):
        self.q, self.key, self.n, self.bias, self.v, self.out = q, key, n, bias, v, out


class Conv:

    def __init__(self, tap, bias):
        self.tap, self.bias = tap, bias


F32 = mybir.dt.float32
F32R = mybir.dt.float32r
ALU = mybir.AluOpType
ACT = mybir.ActivationFunctionType
AX = mybir.AxisListType
ds = bass.ds

P = 128
D = 1024
FT = D // P
S = 256
CTX = 256
TT = S // P
DEPTH = 2
D_FF = 2816
NF = D_FF // P
BANK = 512

ALPHA = (2.0 * DEPTH) ** 0.25
LN_EPS = 1e-5
RMS_EPS = 1e-6
NEG = -1e30

POOL_WINDOWS = (2, 4, 8, 16)
POOL_C = 64
HD = 96
NH = 8
NG = 2
HPG = NH // NG
KVW = NG * HD
STRIDE = 16
CBLK = 32
NC = S // STRIDE - 1
U0, Q0 = 0, 256
KC0, VC0, KS0, VS0, KW0, VW0, G0 = (1024 + i * KVW for i in range(7))
D_IN = G0 + 3 * NH

HD2 = 64
GQ, GKV = 8, 2
BH = 4
HGRN_SCALE = 128 ** -0.5
BQ0 = GQ * HD2 + 2 * GKV * HD2
LEVELS = (1, 2, 4, 8, 16, 32, 64)
NLV = len(LEVELS)
CUM = (NLV + 2) * P
NSC = (NLV + 1) * P
GW = 64
NROW = S // GW
CH = 16
NAC = 16
DY = 15
DX = 31
CONV = 3
CT = 2 * NF

PAR = dict(ln1_g=0, ln1_b=16, ln2_g=32, ln2_b=48, ln3_g=64, ln3_b=80, pre_mix=96, post_mix=112,
           pre_ffn=128, post_ffn=144, b_mod=160, conv_w=256, conv_b=640, pool_scale=768, c=772, c_ctx=780)
PAR_TILES = 7


def conv_col(l, j):
    row = (l * CONV + j) * CT
    return PAR["conv_w"] + row // 88 * P + row % 88


def shape_constants():
    c = {}
    eye = np.eye(P, dtype=np.float32)
    c["c_ident"] = eye
    c["c_alpha"] = (np.float32(ALPHA) * eye).astype(np.float32)
    c["c_mean"] = np.full((P, P), 1.0 / D, np.float32)
    i = np.arange(P)
    c["c_causal"] = np.where(i[None, :] <= i[:, None], 0.0, NEG).astype(np.float32)
    t = np.arange(S)
    ends = np.arange(NC) * STRIDE + CBLK - 1
    cm = np.where(ends[None, :] <= t[:, None], 0.0, NEG).astype(np.float32)
    c["c_cmp"] = cm.reshape(TT, P, NC).transpose(1, 0, 2).copy()
    c["c_any"] = (t >= ends[0]).astype(np.float32).reshape(TT, P).T.copy()
    band = np.zeros((S, len(POOL_WINDOWS), S), np.float32)
    for g, w in enumerate(POOL_WINDOWS):
        for tt in range(S):
            band[max(tt + 1 - w, 0):tt + 1, g, tt] = 1.0 / min(tt + 1, w)
        band[t, g, t] -= 1.0
    c["c_band"] = band.reshape(TT, P, len(POOL_WINDOWS), S).transpose(1, 0, 2, 3).copy()
    nf = HD2 // 4
    inv = 10000.0 ** (-np.arange(nf, dtype=np.float32) / np.float32(nf))
    ang = np.concatenate([(t // GW)[:, None] * inv, (t % GW)[:, None] * inv], axis=1).astype(np.float32)
    for name, f in (("c_cos", np.cos), ("c_sin", np.sin)):
        c[name] = f(ang).astype(np.float32).reshape(TT, P, 2 * nf).transpose(1, 0, 2).copy()
    u, tc = i[:, None], i[None, :]
    cum = np.zeros((2, P, NLV + 2, P), np.float32)
    msk = np.zeros((2, P, NLV + 1, P), np.float32)
    for n, h in enumerate(LEVELS):
        mid = tc // (2 * h) * 2 * h + h
        late = tc % (2 * h) >= h
        cum[0, :, n + 1] = np.where(late, (u >= mid) & (u <= tc), (u > tc) & (u < mid))
        cum[1, :, n + 1] = np.where(late, (u >= mid) & (u < tc), (u >= tc) & (u < mid))
        same = u // (2 * h) == tc // (2 * h)
        msk[0, :, n] = same & (u % (2 * h) < h) & late
        msk[1, :, n] = same & (u % (2 * h) >= h) & ~late
    cum[0, :, 0], cum[0, :, NLV + 1] = u > tc, u <= tc
    cum[1, :, 0], cum[1, :, NLV + 1] = u < tc, u >= tc
    msk[:, :, NLV] = eye
    c["c_cum"] = cum.transpose(1, 0, 2, 3).reshape(P, 2, CUM).copy()
    c["c_lvl"] = msk.transpose(1, 0, 2, 3).reshape(P, 2, NSC).copy()
    start = np.clip(np.arange(GW) - NAC // 2, 0, GW - NAC)
    pick = np.zeros((2, 32, GW, 2, GW), np.float32)
    for q in range(GW):
        for k in range(GW):
            x = k - q + NAC - 1 if start[q] <= k < start[q] + NAC else DX
            for r in range(2):
                pick[r, x, k, r, q] = 1.0
    c["c_pick"] = pick.reshape(2 * 32, GW, P).copy()
    return c


@contextmanager
def phase(nc, names):
    with ExitStack() as ctx:
        handles = [ctx.enter_context(nc.semaphore(f"{n}_{nc.next_id()}")) for n in names]
        s = dict(zip(names, handles))
        with nc.Block() as block:
            yield block, s
        for h in handles:
            nc.gpsimd.sem_clear(h)
        nc.all_engine_barrier()


class Chain:

    def __init__(self, eng, sem, base=0):
        self.eng, self.sem, self.base, self.n = eng, sem, base, 0

    def link(self, ins):
        self.n += 1
        ins.then_inc(self.sem, 1)
        self.eng.wait_ge(self.sem, self.base + self.n)


def params_phase(nc, k, w):
    names = ["zeroed", "rows_in", "consts_in", "turned", "x_in", "x_turned", "x_used", "par_ready"]
    with ExitStack() as ctx:
        rows = ctx.enter_context(nc.sbuf_tensor("par_rows", [P, PAR_TILES, P], F32))
        x_rows = ctx.enter_context(nc.sbuf_tensor("x_rows", [P, 4, D], F32))
        vectors = [("ln1_g", 0, 0), ("ln1_b", 0, 16), ("ln2_g", 0, 32), ("ln2_b", 0, 48), ("ln3_g", 0, 64),
                   ("ln3_b", 0, 80), ("norm_pre_mix_2", 0, 96), ("norm_post_mix_2", 0, 112),
                   ("norm_pre_ffn_2", 1, 0), ("norm_post_ffn_2", 1, 16), ("b_mod_2", 1, 32),
                   ("ffn_conv_b_2", 5, 0), ("pool_scale", 6, 0), ("c_2", 6, 4), ("c_ctx_2", 6, 12)]
        consts = [(k.ident[:, :], w["c_ident"]), (k.alpha[:, :], w["c_alpha"]), (k.mean[:, :], w["c_mean"]), (k.causal[:, :], w["c_causal"]),
                  (k.cmp_mask[:, :, :], w["c_cmp"]), (k.any_cmp[:, :], w["c_any"])]
        n_rows = len(vectors) + CONV
        with phase(nc, names) as (block, s):

            @block.sync
            def _(sp):
                for dst, src in consts:
                    sp.dma_start(dst, src).then_inc(s["consts_in"], 16)
                for tt in range(TT):
                    sp.dma_start(x_rows[:, tt, :], w["x"][0, tt * P:(tt + 1) * P, :]).then_inc(s["x_in"], 16)
                    sp.dma_start(x_rows[:, TT + tt, :], w["ctx_2"][0, tt * P:(tt + 1) * P, :]).then_inc(s["x_in"], 16)
                sp.wait_ge(s["zeroed"], 1)
                for name, tile, r in vectors:
                    a = w[name]
                    src = a.rearrange("(r p) -> r p", p=P) if len(a.shape) == 1 else a.rearrange("l (r p) -> (l r) p", p=P)
                    sp.dma_start(rows[r:r + src.shape[0], tile, :], src).then_inc(s["rows_in"], 16)
                taps = w["ffn_conv_w_2"].rearrange("l j (r p) -> (l j r) p", p=P)
                for n in range(CONV):
                    sp.dma_start(rows[0:88, 2 + n, :], taps[88 * n:88 * n + 88, :]).then_inc(s["rows_in"], 16)

            @block.gpsimd
            def _(pool):
                pool.memset(rows[:, :, :], 0.0).then_inc(s["zeroed"], 1)
                pool.memset(k.eps[:, 0:1], LN_EPS)
                pool.memset(k.eps[:, 1:2], RMS_EPS)
                pool.memset(k.eps[:, 2:3], 1.0)
                pool.memset(k.zero[:, :], 0.0)
                pool.memset(k.one_row[:, :], 1.0)

            @block.tensor
            def _(pe):
                pe.wait_ge(s["consts_in"], 16 * len(consts))
                pe.wait_ge(s["x_in"], 16 * 2 * TT)
                for f in range(FT):
                    if f >= 4:
                        pe.wait_ge(s["x_used"], f - 3)
                    for tt in range(2 * TT):
                        last = pe.transpose(k.ps[:, f % 4, tt * P:(tt + 1) * P], x_rows[:, tt, f * P:(f + 1) * P],
                                            k.ident[:, :])
                    last.then_inc(s["x_turned"], 1)
                pe.wait_ge(s["rows_in"], 16 * n_rows)
                for n in range(PAR_TILES):
                    last = pe.transpose(k.ps[:, 4 + n // 4, n % 4 * P:(n % 4 + 1) * P], rows[:, n, :], k.ident[:, :])
                last.then_inc(s["turned"], 1)

            @block.scalar
            def _(act):
                act.wait_ge(s["par_ready"], 1)
                for n, name in enumerate(("c", "c_ctx")):
                    act.activation(k.c_silu[:, :, n], k.par[:, PAR[name]:PAR[name] + FT], ACT.Silu)

            @block.vector
            def _(dve):
                for f in range(FT):
                    dve.wait_ge(s["x_turned"], f + 1)
                    dve.tensor_copy(k.x_T[:, f, :], k.ps[:, f % 4, :]).then_inc(s["x_used"], 1)
                dve.wait_ge(s["turned"], 1)
                dve.tensor_copy(k.par[:, 0:512], k.ps[:, 4, :])
                dve.tensor_copy(k.par[:, 512:PAR_TILES * P], k.ps[:, 5, 0:(PAR_TILES - 4) * P]).then_inc(s["par_ready"], 1)


LN_SEMS = ["ln_stats", "ln_mv", "ln_std", "ln_rstd", "ln_z", "ln_turned"]


def ln_vector(dve, k, s, t, par_g, par_b):
    for tt in range(TT):
        for n in range(2):
            dve.bn_stats(t.stats[:, tt, n, :], k.ps[:, 2 * tt + n, :]).then_inc(s["ln_stats"], 1)
        dve.wait_ge(s["ln_stats"], 2 * tt + 2)
        dve.bn_aggr(t.mv[:, tt, :], t.stats[:, tt, :, :]).then_inc(s["ln_mv"], 1)
    for tt in range(TT):
        dve.wait_ge(s["ln_std"], tt + 1)
        dve.reciprocal(t.rstd[:, tt:tt + 1], t.std[:, tt:tt + 1]).then_inc(s["ln_rstd"], 1)
        dve.wait_ge(s["ln_rstd"], tt + 1)
        dve.tensor_scalar(t.z[:, tt, :], k.ps[:, 2 * tt:2 * tt + 2, :].rearrange("p b n -> p (b n)"),
                          t.mv[:, tt, 0:1], t.rstd[:, tt:tt + 1], ALU.subtract, ALU.mult).then_inc(s["ln_z"], 1)
    for f in (2, 3, 6, 7):
        dve.wait_ge(s["ln_turned"], f // 2 + 1)
        dve.tensor_scalar(k.x_T[:, f, 0:S], turned(k, f), par_g(f), par_b(f), ALU.mult, ALU.add)


def ln_scalar(act, k, s, t, par_g, par_b):
    for tt in range(TT):
        act.wait_ge(s["ln_mv"], tt + 1)
        act.activation(t.std[:, tt:tt + 1], t.mv[:, tt, 1:2], ACT.Sqrt, bias=k.eps[:, 0:1]).then_inc(s["ln_std"], 1)
    for f in (0, 1, 4, 5):
        act.wait_ge(s["ln_turned"], f // 2 + 1)
        act.activation(k.x_T[:, f, 0:S], turned(k, f), ACT.Identity, bias=par_b(f), scale=par_g(f))


def turned(k, f):
    return k.ps[:, 4 + f // 2, f % 2 * S:(f % 2 + 1) * S]


def turn_tensor(pe, k, z, z_ready, sem):
    pe.wait_ge(z_ready, TT)
    for f in range(FT):
        for tt in range(TT):
            last = pe.transpose(turned(k, f)[:, tt * P:(tt + 1) * P], z[:, tt, f * P:(f + 1) * P], k.ident[:, :])
        if f % 2:
            last.then_inc(sem, 1)


def ln_buffers(nc, ctx):
    def sb(name, shape):
        return ctx.enter_context(nc.sbuf_tensor(f"{name}_{nc.next_id()}", shape, F32))
    got = Buffers()
    got.stats = sb("ln_stats_b", [P, TT, 2, 6])
    got.mv = sb("ln_mv_b", [P, TT, 2])
    got.std = sb("ln_std_b", [P, TT])
    got.rstd = sb("ln_rstd_b", [P, TT])
    got.z = sb("ln_z_b", [P, TT, D])
    return got


POST_SEMS = ["po_sq", "po_ss", "po_std", "po_r", "po_z", "po_turned"]


def post_scalar(act, k, s, t):
    for tt in range(TT):
        act.activation(t.z[:, tt, :], k.ps[:, 2 * tt:2 * tt + 2, :].rearrange("p b n -> p (b n)"), ACT.Square,
                       accum_out=t.mv[:, tt, 0:1]).then_inc(s["po_sq"], 1)
    for tt in range(TT):
        act.wait_ge(s["po_sq"], tt + 1)
        act.activation(t.std[:, tt:tt + 1], t.mv[:, tt, 0:1], ACT.Sqrt, bias=k.eps[:, 1:2], scale=1.0 / D).then_inc(s["po_std"], 1)


def post_vector(dve, k, s, t, gain, cols):
    for tt in range(TT):
        dve.wait_ge(s["po_std"], tt + 1)
        dve.reciprocal(t.rstd[:, tt:tt + 1], t.std[:, tt:tt + 1]).then_inc(s["po_r"], 1)
        dve.wait_ge(s["po_r"], tt + 1)
        dve.tensor_scalar(t.z[:, tt, :], k.ps[:, 2 * tt:2 * tt + 2, :].rearrange("p b n -> p (b n)"),
                          t.rstd[:, tt:tt + 1], None, ALU.mult).then_inc(s["po_z"], 1)
    for f in range(FT):
        dve.wait_ge(s["po_turned"], f // 2 + 1)
        dve.scalar_tensor_tensor(k.x_T[:, f, cols:cols + S], turned(k, f), gain(f), k.x_T[:, f, cols:cols + S],
                                 ALU.mult, ALU.add)


def ffn_phase(nc, k, w_gate, w_up, w_down, src, ln=None, conv=None, post=None, mod=None):
    names = ["gu0_in", "gu1_in", "dn0_in", "dn1_in", "x_hi", "x_lo", "w_hi", "gu_split", "dn_split", "gu_done", "mid_ready",
             "mid_step", "act_done", "h_full", "h_hi", "h_ready", "down_done", "wm0_in", "wm1_in", "acc_step", "prod_step", "mod_done", "mod_used"]
    names += LN_SEMS if ln else POST_SEMS
    LAST = NF - 1
    TURNS = (NF - 6) // 2
    MT = 3
    with ExitStack() as ctx:
        def sb(name, shape, dt=F32):
            return ctx.enter_context(nc.sbuf_tensor(f"{name}_{nc.next_id()}", shape, dt))
        x_hi, x_lo = sb("x_hi", [P, FT, S], F32R), sb("x_lo", [P, FT, S], F32R)
        wgu = [sb(f"w_gu{n}", [P, 2, FT, P]) for n in range(2)]
        wdn = [sb(f"w_dn{n}", [P, D]) for n in range(2)]
        gu_hi = [sb(f"gu_hi{n}", [P, 2, FT, P], F32R) for n in range(2)]
        gu_lo = [sb(f"gu_lo{n}", [P, 2, FT, P], F32R) for n in range(2)]
        dn_hi = [sb(f"dn_hi{n}", [P, D], F32R) for n in range(2)]
        dn_lo = [sb(f"dn_lo{n}", [P, D], F32R) for n in range(2)]
        sil = [sb(f"silu{n}", [P, S]) for n in range(2)]
        hid = [sb(f"hid{n}", [P, S]) for n in range(2)]
        h_hi = [sb(f"h_hi{n}", [P, S], F32R) for n in range(2)]
        h_lo = [sb(f"h_lo{n}", [P, S], F32R) for n in range(2)]
        cv = [sb(f"conv{n}", [P, 2, S]) for n in range(2)] if conv else None
        wm = sb("w_mod", [P, FT, MT * P]) if mod else None
        acc = sb("mod_acc", [P, MT * P]) if mod else None
        prod = sb("mod_prod", [P, FT, MT * P]) if mod else None
        t_ln = ln_buffers(nc, ctx)
        with phase(nc, names) as (block, s):
            gu_in, dn_in = [s["gu0_in"], s["gu1_in"]], [s["dn0_in"], s["dn1_in"]]

            def gu(n):
                return k.ps[:, 4 + n, :].rearrange("p (a t) -> p a t", a=2)

            def tiles(eng, step):
                for t in range(4):
                    step(t, t % 2, t)
                with eng.Fori(0, TURNS - 1) as j:
                    for n in range(2):
                        step(j * 2 + (4 + n), n, None)
                    step(j, None, "turn")
                for t in range(NF - 4, NF):
                    step(t, t % 2, t)
                    if t == NF - 3:
                        step(TURNS - 1, None, "turn")

            @block.sync
            def _(sp):
                def load_gu(i, n):
                    sp.dma_start(wgu[n][:, 0, :, :], w_gate[i]).then_inc(gu_in[n], 16)
                    sp.dma_start(wgu[n][:, 1, :, :], w_up[i]).then_inc(gu_in[n], 16)

                def load_dn(i, n):
                    sp.dma_start(wdn[n][:, :], w_down[i]).then_inc(dn_in[n], 16)

                for n in range(2):
                    load_gu(n, n)
                    load_dn(n, n)
                with sp.Fori(0, NF // 2 - 1) as j:
                    for n in range(2):
                        sp.wait_ge(s["gu_split"], j * 2 + n + 1)
                        load_gu(j * 2 + (n + 2), n)
                        sp.wait_ge(s["dn_split"], j * 2 + n + 1)
                        load_dn(j * 2 + (n + 2), n)

            @block.tensor
            def _(pe):
                def gate_up(t, n):
                    pe.wait_ge(s["gu_split"], t + 1)
                    for a in range(2):
                        for f in range(FT):
                            for p, (wt, x) in enumerate(((gu_hi, x_hi), (gu_hi, x_lo), (gu_lo, x_hi))):
                                last = pe.matmul(gu(n)[:, a, :], wt[n][:, a, f, :], x[:, f, :], start=(f == 0 and p == 0),
                                                 stop=(f == FT - 1 and p == 2), skip_group_check=True)
                    last.then_inc(s["gu_done"], 1)

                def down(t, n, first=False, end=False):
                    pe.wait_ge(s["dn_split"], t + 1)
                    pe.wait_ge(s["h_ready"], t + 1)
                    for tt in range(TT):
                        for c in range(2):
                            for p, (h, wt) in enumerate(((h_hi, dn_hi), (h_hi, dn_lo), (h_lo, dn_hi))):
                                last = pe.matmul(k.ps[:, 2 * tt + c, :], h[n][:, tt * P:(tt + 1) * P], wt[n][:, c * BANK:(c + 1) * BANK],
                                                 start=(first and p == 0), stop=(end and p == 2), skip_group_check=True)
                    last.then_inc(s["down_done"], 1)

                def step(t, n, fixed):
                    if fixed == "turn":
                        if mod:
                            pe.wait_ge(s["acc_step"], t * FT + FT)
                            pe.wait_ge(s["prod_step"], t * 5 + 5)
                            pe.wait_ge(s["mod_used"], t + 1)
                            for m in range(MT):
                                for st in range(2):
                                    last = pe.matmul(k.ps[:, 6, 2 * m + st:2 * m + st + 1], (acc[:, m * P:(m + 1) * P], prod[:, 0, m * P:(m + 1) * P])[st], k.eps[:, 2:3],
                                                     start=True, stop=True, skip_group_check=True)
                            last.then_inc(s["mod_done"], 1)
                        return
                    if fixed is None or fixed >= 2:
                        pe.wait_ge(s["h_full"], t - 1)
                    gate_up(t, n)
                    if fixed is None or fixed >= 1:
                        down(t - 1, 1 - n, first=(fixed == 1 and not ln))

                if ln:
                    for tt in range(TT):
                        for f in range(FT):
                            pe.matmul(k.ps[:, 2 * tt + f // 4, f % 4 * P:(f % 4 + 1) * P], k.x_T[:, f, tt * P:(tt + 1) * P],
                                      k.alpha[:, :], start=(f % 4 == 0), stop=False, skip_group_check=True)
                pe.wait_ge(s["x_lo"], FT)
                tiles(pe, step)
                down(LAST, LAST % 2, end=True)
                turn_tensor(pe, k, t_ln.z, s["ln_z"] if ln else s["po_z"], s["ln_turned"] if ln else s["po_turned"])

            @block.scalar
            def _(act):
                def hi_gu(t, n, a, fixed):
                    if a == 0:
                        act.wait_ge(gu_in[n], 16 * (fixed - n) + 32 if fixed is not None else (t - n) * 16 + 32)
                    act.activation(gu_hi[n][:, a, :, :], wgu[n][:, a, :, :], ACT.Copy).then_inc(s["w_hi"], 1)

                def hi_dn(t, n, fixed):
                    act.wait_ge(dn_in[n], 8 * (fixed - n) + 16 if fixed is not None else (t - n) * 8 + 16)
                    act.activation(dn_hi[n][:, :], wdn[n][:, :], ACT.Copy).then_inc(s["w_hi"], 1)

                def step(t, n, fixed):
                    if fixed == "turn":
                        return
                    more_gu = fixed is None or fixed + 2 <= LAST
                    more_dn = fixed is None or 1 <= fixed < LAST
                    act.wait_ge(s["gu_done"], t + 1)
                    if conv is None:
                        act.activation(sil[n][:, :], gu(n)[:, 0, :], ACT.Silu).then_inc(s["act_done"], 1)
                    else:
                        for a in range(2):
                            act.activation(cv[n][:, a, :], gu(n)[:, a, :], ACT.Identity, bias=conv.bias(t, a),
                                           scale=conv.tap(1, t, a)).then_inc(s["mid_ready"], 1)
                    if more_gu:
                        hi_gu(t + 2, n, 0, None if fixed is None else fixed + 2)
                    if conv is not None:
                        act.wait_ge(s["mid_step"], t * 4 + 4)
                        act.activation(sil[n][:, :], cv[n][:, 1, :], ACT.Silu).then_inc(s["act_done"], 1)
                    if more_gu:
                        hi_gu(t + 2, n, 1, None if fixed is None else fixed + 2)
                    act.wait_ge(s["h_full"], t + 1)
                    act.activation(h_hi[n][:, :], hid[n][:, :], ACT.Copy).then_inc(s["h_hi"], 1)
                    if more_dn:
                        act.wait_ge(s["down_done"], t)
                        hi_dn(t + 1, 1 - n, None if fixed is None else fixed + 1)
                    if mod and ((fixed is None and n == 1) or fixed == 3):
                        act.wait_ge(s["mod_used"], (t - 3) // 2 + 1)
                        load_mod(1, (t - 3) // 2)
                    if mod and fixed is None and n == 0:
                        act.wait_ge(s["acc_step"], (t - 3) * (FT // 2))
                        act.wait_ge(s["prod_step"], (t - 4) // 2 * 5 + 1)
                        load_mod(0, (t - 4) // 2 + 1)

                def load_mod(half, j):
                    f0 = half * (FT // 2)
                    act.dma_start(wm[:, f0:f0 + FT // 2, :], mod[0](j)[:, f0:f0 + FT // 2, :]).then_inc(s[f"wm{half}_in"], 16)

                if mod:
                    load_mod(0, 0)
                for f in range(FT):
                    act.activation(x_hi[:, f, :], src(f), ACT.Copy).then_inc(s["x_hi"], 1)
                for n in range(2):
                    hi_gu(n, n, 0, n)
                    hi_gu(n, n, 1, n)
                    hi_dn(n, n, n)
                tiles(act, step)
                act.wait_ge(s["down_done"], NF)
                if ln:
                    ln_scalar(act, k, s, t_ln, *ln)
                else:
                    post_scalar(act, k, s, t_ln)

            @block.gpsimd
            def _(pool):
                H = FT // 2

                def turn(j):
                    pool.wait_ge(s["mod_used"], j + 1)
                    for n in range(2):
                        pool.wait_ge(s[f"wm{n}_in"], j * 16 + 16)
                        half = slice(n * H, (n + 1) * H)
                        pool.tensor_tensor(prod[:, half, :], wm[:, half, :], k.c_silu[:, half, 1:2].broadcast_to([P, H, MT * P]),
                                           ALU.mult).then_inc(s["prod_step"], 1)
                    for n, half in enumerate((4, 2, 1)):
                        pool.wait_ge(s["prod_step"], j * 5 + (2 + n))
                        pool.tensor_tensor(prod[:, 0:half, :], prod[:, 0:half, :], prod[:, half:2 * half, :], ALU.add).then_inc(s["prod_step"], 1)

                if mod:
                    with pool.Fori(0, TURNS - 1) as j:
                        turn(j)
                    turn(TURNS - 1)

            @block.vector
            def _(dve):
                def lo_gu(n, a, made):
                    dve.wait_ge(s["w_hi"], made)
                    last = dve.tensor_tensor(gu_lo[n][:, a, :, :], wgu[n][:, a, :, :], gu_hi[n][:, a, :, :].bitcast(F32), ALU.subtract)
                    if a == 1:
                        last.then_inc(s["gu_split"], 1)

                def lo_dn(n, made):
                    dve.wait_ge(s["w_hi"], made)
                    dve.tensor_tensor(dn_lo[n][:, :], wdn[n][:, :], dn_hi[n][:, :].bitcast(F32), ALU.subtract).then_inc(s["dn_split"], 1)

                def step(t, n, fixed):
                    if fixed == "turn":
                        if mod:
                            dve.wait_ge(s["mod_done"], t + 1)
                            dve.tensor_tensor(mod[1](t), k.ps[:, 6, 0:2 * MT].rearrange("p (m s) -> p m s", s=2), mod[2](t),
                                              ALU.add).then_inc(s["mod_used"], 1)
                            if not (isinstance(t, int) and t == TURNS - 1):
                                latent_mod(t * 2 + 5, 0)
                        return
                    more_gu = fixed is None or fixed + 2 <= LAST
                    more_dn = fixed is None or 1 <= fixed < LAST
                    made = 6 if fixed == 0 else t * 3 + 5
                    if conv is not None:
                        dve.wait_ge(s["mid_ready"], t * 2 + 2)
                        for a in range(2):
                            dve.scalar_tensor_tensor(cv[n][:, a, 1:S], gu(n)[:, a, 0:S - 1], conv.tap(0, t, a),
                                                     cv[n][:, a, 1:S], ALU.mult, ALU.add).then_inc(s["mid_step"], 1)
                        for a in range(2):
                            dve.wait_ge(s["mid_step"], t * 4 + (a + 1))
                            dve.scalar_tensor_tensor(cv[n][:, a, 0:S - 1], gu(n)[:, a, 1:S], conv.tap(2, t, a),
                                                     cv[n][:, a, 0:S - 1], ALU.mult, ALU.add).then_inc(s["mid_step"], 1)
                    else:
                        dve.wait_ge(s["act_done"], t + 1)
                        dve.scalar_tensor_tensor(hid[n][:, :], sil[n][:, :], 0.5, gu(n)[:, 1, :], ALU.mult, ALU.mult).then_inc(s["h_full"], 1)
                    if more_gu:
                        lo_gu(n, 0, made + 1)
                    if conv is not None:
                        dve.wait_ge(s["act_done"], t + 1)
                        dve.tensor_tensor(hid[n][:, :], sil[n][:, :], cv[n][:, 0, :], ALU.mult).then_inc(s["h_full"], 1)
                    if more_gu:
                        lo_gu(n, 1, made + 2)
                    dve.wait_ge(s["h_hi"], t + 1)
                    dve.tensor_tensor(h_lo[n][:, :], hid[n][:, :], h_hi[n][:, :].bitcast(F32), ALU.subtract).then_inc(s["h_ready"], 1)
                    if more_dn:
                        lo_dn(1 - n, made + (3 if more_gu else 1))
                    if mod and (fixed == 3 or (n == 0 and (fixed is None or fixed == NF - 4))):
                        latent_mod(t, 1 - n)

                def latent_mod(t, half):
                    dve.wait_ge(s[f"wm{half}_in"], (t - 3 - half) * 8 + 16)
                    if half == 0:
                        dve.wait_ge(s["mod_used"], (t - 3) // 2 + 1)
                    for i in range(FT // 2):
                        f = half * (FT // 2) + i
                        if f == 0:
                            part = dve.tensor_scalar(acc[:, :], wm[:, f, :], k.c_silu[:, f, 0:1], None, ALU.mult)
                        else:
                            dve.wait_ge(s["acc_step"], (t - 3) * (FT // 2) + i)
                            part = dve.scalar_tensor_tensor(acc[:, :], wm[:, f, :], k.c_silu[:, f, 0:1], acc[:, :], ALU.mult, ALU.add)
                        part.then_inc(s["acc_step"], 1)

                if mod:
                    dve.sem_inc(s["mod_used"], 1)
                for f in range(FT):
                    dve.wait_ge(s["x_hi"], f + 1)
                    dve.tensor_tensor(x_lo[:, f, :], src(f), x_hi[:, f, :].bitcast(F32), ALU.subtract).then_inc(s["x_lo"], 1)
                for n in range(2):
                    lo_gu(n, 0, 3 * n + 1)
                    lo_gu(n, 1, 3 * n + 2)
                    lo_dn(n, 3 * n + 3)
                tiles(dve, step)
                dve.wait_ge(s["down_done"], NF)
                if ln:
                    ln_vector(dve, k, s, t_ln, *ln)
                else:
                    post_vector(dve, k, s, t_ln, *post)


def out_phase(nc, k, chunks, ln=None, post=None):
    names = ["sum_done"] + (LN_SEMS if ln else POST_SEMS)
    with ExitStack() as ctx:
        t = ln_buffers(nc, ctx)
        with phase(nc, names) as (block, s):

            @block.tensor
            def _(pe):
                if ln:
                    for tt in range(TT):
                        for f in range(FT):
                            pe.matmul(k.ps[:, 2 * tt + f // 4, f % 4 * P:(f % 4 + 1) * P], k.x_T[:, f, tt * P:(tt + 1) * P],
                                      k.alpha[:, :], start=(f % 4 == 0), stop=False, skip_group_check=True)
                for tt in range(TT):
                    for n, (stationary, moving) in enumerate(chunks):
                        for c in range(2):
                            last = pe.matmul(k.ps[:, 2 * tt + c, :], stationary(tt), moving[:, c * BANK:(c + 1) * BANK],
                                             start=(n == 0 and not ln), stop=(n == len(chunks) - 1), skip_group_check=True)
                last.then_inc(s["sum_done"], 1)
                turn_tensor(pe, k, t.z, s["ln_z"] if ln else s["po_z"], s["ln_turned"] if ln else s["po_turned"])

            @block.scalar
            def _(act):
                act.wait_ge(s["sum_done"], 1)
                if ln:
                    ln_scalar(act, k, s, t, *ln)
                else:
                    post_scalar(act, k, s, t)

            @block.vector
            def _(dve):
                dve.wait_ge(s["sum_done"], 1)
                if ln:
                    ln_vector(dve, k, s, t, *ln)
                else:
                    post_vector(dve, k, s, t, *post)


def mixer1_project(nc, k, m, w, l):
    names = ["w_in", "pool_in", "cmp_in", "pos_in", "tok_done", "tok_used", "feat_done", "feat_used", "q_done", "q_used",
             "pos_turned", "pos_ready", "blocks_ready", "hid_done", "hid_ready", "cmp_done", "band_done", "band_used",
             "mix_done", "gate_ready"]
    FEAT = (KC0, VC0, KS0, KW0)
    with ExitStack() as ctx:
        def sb(name, shape):
            return ctx.enter_context(nc.sbuf_tensor(f"{name}_{nc.next_id()}", shape, F32))
        win = sb("w_in_b", [P, FT, D_IN])
        w1 = sb("cmp_w1_b", [HD, 2, CBLK, HD])
        w2 = sb("cmp_w2_b", [HD, 2, HD])
        pos_rows = sb("pos_rows", [CBLK, 2, HD])
        pos = sb("pos_T", [HD, 2, CBLK])
        blocks = sb("cmp_blocks", [HD, 2, CBLK, NG, NC])
        hidden = sb("cmp_hidden", [HD, 2, NG, NC])
        pool_w = sb("pool_w_b", [P, 2, POOL_C])
        band = sb("band_b", [P, TT, len(POOL_WINDOWS), S])
        u_tok = sb("u_tok", [P, TT, 256])
        pooled = sb("pooled", [P, 2, S])
        with phase(nc, names) as (block, s):

            @block.sync
            def _(sp):
                w_in = w["w_in"].rearrange("l (f p) n -> l p f n", p=P)
                for f in range(FT):
                    sp.dma_start(win[:, f, :], w_in[l, :, f, :]).then_inc(s["w_in"], 16)
                sp.dma_start(k.b_gate[0:1, :], w["b_gate"].unsqueeze(1)[l]).then_inc(s["w_in"], 16)
                for n, kv in enumerate("kv"):
                    sp.dma_start(pos_rows[:, n, :], w[f"cmp_pos_{kv}"][l]).then_inc(s["pos_in"], 16)
                for n, kv in enumerate("kv"):
                    sp.dma_start(w1[:, n, :, :], w[f"cmp_{kv}_w1"].rearrange("l (c d) j -> l d c j", d=HD)[l]).then_inc(s["cmp_in"], 16)
                    sp.dma_start(w2[:, n, :], w[f"cmp_{kv}_w2"][l]).then_inc(s["cmp_in"], 16)
                sp.dma_start(band[:, :, :, :], w["c_band"]).then_inc(s["pool_in"], 16)
                pw = w["pool_w"].rearrange("l (a b) c d -> l b c a d", b=2)
                for b in range(2):
                    sp.dma_start(pool_w[64 * b:64 * b + 64, :, :], pw[l, b]).then_inc(s["pool_in"], 16)

            @block.tensor
            def _(pe):
                pe.wait_ge(s["pos_in"], 32)
                for n in range(2):
                    last = pe.transpose(k.ps[0:HD, 7, n * CBLK:(n + 1) * CBLK], pos_rows[:, n, :], k.ident[0:CBLK, 0:CBLK])
                last.then_inc(s["pos_turned"], 1)
                pe.wait_ge(s["w_in"], 16 * (FT + 1))
                for tt in range(TT):
                    for bank, at, col, n in ((tt, 0, U0, 256), (tt, 256, VS0, KVW), (2 + tt, 0, VW0, KVW + 3 * NH)):
                        for f in range(FT):
                            last = pe.matmul(k.ps[:, bank, at:at + n], k.x_T[:, f, tt * P:(tt + 1) * P], win[:, f, col:col + n],
                                             start=(f == 0), stop=(f == FT - 1), skip_group_check=True)
                    last = pe.matmul(k.ps[:, 2 + tt, KVW:KVW + 3 * NH], k.one_row[0:1, :], k.b_gate[0:1, :], start=False,
                                     stop=True, skip_group_check=True)
                    last.then_inc(s["tok_done"], 1)
                for n, col in enumerate(FEAT):
                    if n == 3:
                        pe.wait_ge(s["pos_ready"], 1)
                    for g in range(NG):
                        for f in range(FT):
                            last = pe.matmul(k.ps[0:HD, 4 + n, g * S:(g + 1) * S], win[:, f, col + g * HD:col + (g + 1) * HD],
                                             k.x_T[:, f, 0:S], start=(f == 0), stop=(f == FT - 1), skip_group_check=True)
                    last.then_inc(s["feat_done"], 1)
                for n in range(NH // 2):
                    if n < 2:
                        pe.wait_ge(s["tok_used"], 4 * TT)
                    else:
                        pe.wait_ge(s["q_used"], n - 1)
                    for a in range(2):
                        for f in range(FT):
                            h = 2 * n + a
                            last = pe.matmul(k.ps[0:HD, n % 2, a * S:(a + 1) * S], win[:, f, Q0 + h * HD:Q0 + (h + 1) * HD],
                                             k.x_T[:, f, 0:S], start=(f == 0), stop=(f == FT - 1), skip_group_check=True)
                    last.then_inc(s["q_done"], 1)
                pe.wait_ge(s["pool_in"], 48)
                for g in range(4):
                    for tt in range(TT):
                        last = pe.matmul(k.ps[64 * (g % 2):64 * (g % 2) + 64, 2 + g // 2, 0:S], u_tok[:, tt, g * POOL_C:(g + 1) * POOL_C],
                                         band[:, tt, g, :], start=(tt == 0), stop=(tt == TT - 1), skip_group_check=True)
                last.then_inc(s["band_done"], 1)
                pe.wait_ge(s["cmp_in"], 64)
                for n in range(2):
                    pe.wait_ge(s["blocks_ready"], 4 * n + 4)
                    for c in range(CBLK):
                        last = pe.matmul(k.ps[0:HD, 4 + n, 0:NG * NC], w1[:, n, c, :], blocks[:, n, c, :, :].rearrange("d g b -> d (g b)"),
                                         start=(c == 0), stop=(c == CBLK - 1))
                    last.then_inc(s["hid_done"], 1)
                pe.wait_ge(s["band_used"], 2)
                for g in range(4):
                    r = 64 * (g % 2)
                    last = pe.matmul(k.ps[r:r + 64, 2 + g // 2, S:2 * S], pool_w[r:r + 64, g // 2, :], pooled[r:r + 64, g // 2, :],
                                     start=True, stop=True, skip_group_check=True)
                last.then_inc(s["mix_done"], 1)
                pe.wait_ge(s["feat_used"], 2)
                pe.wait_ge(s["hid_ready"], 2)
                pe.matmul(k.ps[0:HD, 6, 0:NG * NC], w2[:, 0, :], hidden[:, 0, :, :].rearrange("d g b -> d (g b)"), start=True, stop=True)
                for g in range(NG):
                    last = pe.matmul(k.ps[0:NC, 7, g * HD:(g + 1) * HD], hidden[:, 1, g, :], w2[:, 1, :], start=True, stop=True,
                                     skip_group_check=True)
                last.then_inc(s["cmp_done"], 1)

            @block.scalar
            def _(act):
                for tt in range(TT):
                    act.wait_ge(s["tok_done"], tt + 1)
                    act.activation(m.gates[:, tt, :], k.ps[:, 2 + tt, KVW:KVW + 3 * NH], ACT.Sigmoid).then_inc(s["gate_ready"], 1)
                    act.activation(m.v_win[:, tt, :], k.ps[:, 2 + tt, 0:KVW], ACT.Copy).then_inc(s["tok_used"], 2)
                for n in range(2):
                    act.wait_ge(s["feat_done"], 3 + n)
                    act.activation((m.ks_T, m.kw_T)[n][:, :, :].rearrange("d g t -> d (g t)"), k.ps[0:HD, 6 + n, :], ACT.Copy).then_inc(s["feat_used"], 1)
                for n in range(NH // 2):
                    act.wait_ge(s["q_done"], n + 1)
                    act.activation(m.q_T[:, 2 * n:2 * n + 2, :].rearrange("d h t -> d (h t)"), k.ps[0:HD, n % 2, :], ACT.Copy,
                                   scale=HD ** -0.5).then_inc(s["q_used"], 1)
                act.wait_ge(s["band_done"], 1)
                for a in range(2):
                    act.activation(pooled[:, a, :], k.ps[:, 2 + a, 0:S], ACT.Copy).then_inc(s["band_used"], 1)
                for n in range(2):
                    act.wait_ge(s["hid_done"], n + 1)
                    act.activation(hidden[:, n, :, :].rearrange("d g b -> d (g b)"), k.ps[0:HD, 4 + n, 0:NG * NC], ACT.Gelu_apprx_tanh).then_inc(s["hid_ready"], 1)
                act.wait_ge(s["cmp_done"], 1)
                act.activation(m.kc_T[:, :, :].rearrange("d g b -> d (g b)"), k.ps[0:HD, 6, 0:NG * NC], ACT.Copy)
                act.activation(m.v_cmp[:, :, :].rearrange("b g d -> b (g d)"), k.ps[0:NC, 7, 0:KVW], ACT.Copy)

            @block.vector
            def _(dve):
                dve.wait_ge(s["pos_turned"], 1)
                dve.tensor_copy(pos[:, :, :].rearrange("d n c -> d (n c)"), k.ps[0:HD, 7, 0:2 * CBLK]).then_inc(s["pos_ready"], 1)
                for tt in range(TT):
                    dve.wait_ge(s["tok_done"], tt + 1)
                    dve.tensor_copy(u_tok[:, tt, :], k.ps[:, tt, 0:256])
                    dve.tensor_copy(m.v_slc[:, tt, :], k.ps[:, tt, 256:256 + KVW]).then_inc(s["tok_used"], 2)
                    dve.wait_ge(s["gate_ready"], tt + 1)
                    g_cmp = m.gates[:, tt, :].rearrange("p (h b) -> p h b", b=3)[:, :, 0]
                    dve.tensor_scalar(g_cmp, g_cmp, k.any_cmp[:, tt:tt + 1], None, ALU.mult)
                dve.wait_ge(s["pos_ready"], 1)
                for n in range(2):
                    dve.wait_ge(s["feat_done"], n + 1)
                    for g in range(NG):
                        toks = k.ps[0:HD, 4 + n, g * S:(g + 1) * S].rearrange("d (b c) -> d c b", c=STRIDE)
                        for half in range(2):
                            c0 = half * STRIDE
                            dve.tensor_tensor(blocks[:, n, c0:c0 + STRIDE, g, :], toks[:, :, half:half + NC],
                                              pos[:, n, c0:c0 + STRIDE].unsqueeze(2).broadcast_to([HD, STRIDE, NC]),
                                              ALU.add).then_inc(s["blocks_ready"], 1)
                dve.wait_ge(s["mix_done"], 1)
                for a in range(2):
                    dve.tensor_scalar(m.y_pool[:, a, :], k.ps[:, 2 + a, S:2 * S], k.col("pool_scale", l * 2 + a), None, ALU.mult)


def mixer1_attend(nc, k, m, w, l):
    names = ["q_staged", "c_done", "c_max", "c_exp", "c_step", "c_ready", "ct_done", "ct_ready",
             "s_done", "max_ready", "e_ready", "rs_step", "p_ready", "t_done", "t_ready", "pv_done", "o_used", "out_w"]
    UNITS = [(g, tt) for g in range(NG) for tt in range(TT)]
    NU = len(UNITS)
    with ExitStack() as ctx:
        def sb(name, shape):
            return ctx.enter_context(nc.sbuf_tensor(f"{name}_{nc.next_id()}", shape, F32))
        q_st = sb("q_staged_b", [HD, NG, S])
        nmax = sb("nmax", [P, 3, 2])
        sums = sb("sums", [P, 3, 2])
        rs = sb("rs", [P, 3, 2])
        e = sb("e_b", [P, 3, 2, S])
        pt = sb("pt_b", [P, 2, 2, TT, P])
        nmax_c, sums_c, rs_c = sb("nmax_c", [P, NU]), sb("sums_c", [P, NU]), sb("rs_c", [P, NU])
        ec = sb("ec_b", [P, NU, NC])
        ptc = sb("ptc_b", [NC, NU, P])
        with phase(nc, names) as (block, s):

            @block.sync
            def _(sp):
                sp.dma_start(m.wo_pool[:, :, :], w["w_out"].rearrange("l (a p) n -> l p a n", p=P)[l, :, 0:2, :]).then_inc(s["out_w"], 16)
                sp.dma_start(m.wo_att[:, :, :], w["w_out"][l, 256:D, :].rearrange("(h d) n -> d h n", d=HD)).then_inc(s["out_w"], 16)
                sp.wait_ge(s["out_w"], 32)

            @block.gpsimd
            def _(pool):
                with pool.Fori(0, HPG) as j:
                    for g in range(NG):
                        pool.tensor_copy(q_st[:, g, :], m.q_T[:, ds(j + g * HPG, 1), :].rearrange("d a t -> d (a t)")).then_inc(s["q_staged"], 1)
                    pool.wait_ge(s["s_done"], j * NU + NU)

            def s_bank(u):
                return k.ps[:, (0, 1, 3)[u % 3], :].rearrange("p (b t) -> p b t", b=2)

            c_bank = k.ps[:, 2, 0:NU * NC].rearrange("p (u n) -> p u n", u=NU)
            ct_bank = k.ps[0:NC, 7, :].rearrange("n (u t) -> n u t", u=NU)

            def t_bank(u):
                return k.ps[:, 4 + u % 2, :].rearrange("p (b c t) -> p b c t", b=2, c=TT)

            def o_bank(g):
                return k.ps[0:HD, 6, g * S:(g + 1) * S]

            @block.tensor
            def _(pe):
                with pe.Fori(0, HPG) as j:
                    def compressed():
                        pe.wait_ge(s["q_staged"], j * 2 + 2)
                        for u, (g, tt) in enumerate(UNITS):
                            pe.matmul(c_bank[:, u, :], q_st[:, g, tt * P:(tt + 1) * P], m.kc_T[:, g, :], start=True, stop=False,
                                      skip_group_check=True)
                            last = pe.matmul(c_bank[:, u, :], k.ident[:, :], k.cmp_mask[:, tt, :], start=False, stop=True, skip_group_check=True)
                        last.then_inc(s["c_done"], 1)

                    def compressed_turn():
                        pe.wait_ge(s["c_ready"], j + 1)
                        for u in range(NU):
                            last = pe.transpose(ct_bank[:, u, :], ec[:, u, :], k.ident[:, :])
                        last.then_inc(s["ct_done"], 1)

                    def scores(u):
                        g, tt = UNITS[u]
                        n = (tt + 1) * P
                        if u >= 3:
                            pe.wait_ge(s["e_ready"], j * NU + (u - 2))
                        for b, key in enumerate((m.ks_T, m.kw_T)):
                            pe.matmul(s_bank(u)[:, b, 0:n], q_st[:, g, tt * P:(tt + 1) * P], key[:, g, 0:n], start=True, stop=False,
                                      skip_group_check=True)
                            last = pe.matmul(s_bank(u)[:, b, n - P:n], k.ident[:, :], k.causal[:, :], start=False, stop=True,
                                             skip_group_check=True)
                        last.then_inc(s["s_done"], 1)

                    def turn(u):
                        g, tt = UNITS[u]
                        pe.wait_ge(s["p_ready"], j * NU + (u + 1))
                        if u >= 2:
                            pe.wait_ge(s["t_ready"], j * NU + (u - 1))
                        for b in range(2):
                            for c in range(tt + 1):
                                last = pe.transpose(t_bank(u)[:, b, c, :], e[:, u % 3, b, c * P:(c + 1) * P], k.ident[:, :])
                        last.then_inc(s["t_done"], 1)

                    def values(u):
                        g, tt = UNITS[u]
                        if u == 0:
                            pe.wait_ge(s["o_used"], j * 2 + 2)
                            pe.wait_ge(s["ct_ready"], j + 1)
                        pe.wait_ge(s["t_ready"], j * NU + (u + 1))
                        o = o_bank(g)[:, tt * P:(tt + 1) * P]
                        pe.matmul(o, m.v_cmp[:, g, :], ptc[:, u, :], start=True, stop=False, skip_group_check=True)
                        for b, v in enumerate((m.v_slc, m.v_win)):
                            for c in range(tt + 1):
                                last = pe.matmul(o, v[:, c, g * HD:(g + 1) * HD], pt[:, u % 2, b, c, :], start=False,
                                                 stop=(b == 1 and c == tt), skip_group_check=True)
                        last.then_inc(s["pv_done"], 1)

                    compressed()
                    for u in range(NU + 3):
                        if u < NU:
                            scores(u)
                        if u == 2:
                            compressed_turn()
                        if 2 <= u < NU + 2:
                            turn(u - 2)
                        if u >= 3:
                            values(u - 3)

            @block.vector
            def _(dve):
                with dve.Fori(0, HPG) as j:
                    def compressed():
                        c = Chain(dve, s["c_step"], j * 4)
                        dve.wait_ge(s["c_exp"], j + 1)
                        c.link(dve.tensor_scalar(rs_c[:, :], sums_c[:, :], 1e-30, None, ALU.max))
                        c.link(dve.reciprocal(rs_c[:, :], rs_c[:, :]))
                        for g in range(NG):
                            part = rs_c[:, g * TT:(g + 1) * TT].unsqueeze(2)
                            c.link(dve.tensor_tensor(part, part, m.gates[:, :, ds((j + g * HPG) * 3, 1)], ALU.mult))
                        dve.tensor_tensor(ec[:, :, :], ec[:, :, :], rs_c[:, :].unsqueeze(2).broadcast_to([P, NU, NC]),
                                          ALU.mult).then_inc(s["c_ready"], 1)

                    dve.wait_ge(s["c_done"], j + 1)
                    dve.tensor_reduce(nmax_c[:, :], c_bank, AX.X, ALU.max, negate=True).then_inc(s["c_max"], 1)
                    for u in range(NU + 1):
                        if u < NU:
                            n = (UNITS[u][1] + 1) * P
                            dve.wait_ge(s["s_done"], j * NU + (u + 1))
                            dve.tensor_reduce(nmax[:, u % 3, :], s_bank(u)[:, :, 0:n], AX.X, ALU.max, negate=True).then_inc(s["max_ready"], 1)
                        if u == 1:
                            compressed()
                        if u >= 1:
                            v = u - 1
                            g, tt = UNITS[v]
                            n = (tt + 1) * P
                            c = Chain(dve, s["rs_step"], j * (3 * NU) + 3 * v)
                            dve.wait_ge(s["e_ready"], j * NU + (v + 1))
                            c.link(dve.tensor_scalar(rs[:, v % 3, :], sums[:, v % 3, :], 1e-30, None, ALU.max))
                            c.link(dve.reciprocal(rs[:, v % 3, :], rs[:, v % 3, :]))
                            c.link(dve.tensor_tensor(rs[:, v % 3, :], rs[:, v % 3, :], m.gates[:, tt, ds((j + g * HPG) * 3 + 1, 2)], ALU.mult))
                            for b in range(2):
                                last = dve.tensor_scalar(e[:, v % 3, b, 0:n], e[:, v % 3, b, 0:n], rs[:, v % 3, b:b + 1], None, ALU.mult)
                            last.then_inc(s["p_ready"], 1)

            @block.scalar
            def _(act):
                act.sem_inc(s["o_used"], 2)
                with act.Fori(0, HPG) as j:
                    act.wait_ge(s["c_max"], j + 1)
                    for u in range(NU):
                        last = act.activation(ec[:, u, :], c_bank[:, u, :], ACT.Exp, bias=nmax_c[:, u:u + 1], accum_out=sums_c[:, u:u + 1])
                    last.then_inc(s["c_exp"], 1)
                    for u in range(NU + 2):
                        if u < NU:
                            n = (UNITS[u][1] + 1) * P
                            act.wait_ge(s["max_ready"], j * NU + (u + 1))
                            if u >= 3:
                                act.wait_ge(s["t_done"], j * NU + (u - 2))
                            for b in range(2):
                                last = act.activation(e[:, u % 3, b, 0:n], s_bank(u)[:, b, 0:n], ACT.Exp, bias=nmax[:, u % 3, b:b + 1],
                                                      accum_out=sums[:, u % 3, b:b + 1])
                            last.then_inc(s["e_ready"], 1)
                        if u == 2:
                            act.wait_ge(s["ct_done"], j + 1)
                            act.activation(ptc[:, :, :], ct_bank, ACT.Copy).then_inc(s["ct_ready"], 1)
                        if u >= 2:
                            v = u - 2
                            g, tt = UNITS[v]
                            act.wait_ge(s["t_done"], j * NU + (v + 1))
                            if v >= 2:
                                act.wait_ge(s["pv_done"], j * NU + (v - 1))
                            act.activation(pt[:, v % 2, :, 0:tt + 1, :], t_bank(v)[:, :, 0:tt + 1, :], ACT.Copy).then_inc(s["t_ready"], 1)
                    for g in range(NG):
                        act.wait_ge(s["pv_done"], j * NU + NU)
                        act.activation(m.o_T[:, ds(j + g * HPG, 1), :].rearrange("d a t -> d (a t)"), o_bank(g), ACT.Copy).then_inc(s["o_used"], 1)


def mixer1(nc, k, w, l):
    with ExitStack() as ctx:
        def sb(name, shape):
            return ctx.enter_context(nc.sbuf_tensor(f"{name}_{nc.next_id()}", shape, F32))
        m = Buffers()
        m.q_T = sb("q_T", [HD, NH, S])
        m.ks_T = sb("ks_T", [HD, NG, S])
        m.kw_T = sb("kw_T", [HD, NG, S])
        m.kc_T = sb("kc_T", [HD, NG, NC])
        m.v_slc = sb("v_slc", [P, TT, KVW])
        m.v_win = sb("v_win", [P, TT, KVW])
        m.v_cmp = sb("v_cmp", [NC, NG, HD])
        m.gates = sb("gates", [P, TT, 3 * NH])
        m.y_pool = sb("y_pool", [P, 2, S])
        m.o_T = sb("o_T", [HD, NH, S])
        m.wo_pool = sb("wo_pool", [P, 2, D])
        m.wo_att = sb("wo_att", [HD, NH, D])
        mixer1_project(nc, k, m, w, l)
        mixer1_attend(nc, k, m, w, l)
        chunks = [(lambda tt, a=a: m.y_pool[:, a, tt * P:(tt + 1) * P], m.wo_pool[:, a, :]) for a in range(2)]
        chunks += [(lambda tt, h=h: m.o_T[:, h, tt * P:(tt + 1) * P], m.wo_att[:, h, :]) for h in range(NH)]
        out_phase(nc, k, chunks, ln=(lambda f: k.col("ln2_g", l * FT + f), lambda f: k.col("ln2_b", l * FT + f)))


def bias_phase(nc, k, b, w):
    names = ["rpb_in", "pick_in", "masked", "rpb_turned",
             "rpb_ready", "bias_done", "bias_used"]
    PER = 5
    NJ = 6
    with ExitStack() as ctx:
        def sb(name, shape):
            return ctx.enter_context(nc.sbuf_tensor(f"{name}_{nc.next_id()}", shape, F32))
        pick = sb("pick", [2 * 32, GW, P])
        rpb = sb("rpb_rows", [NJ * CH, 2, 32])
        rpb_T = sb("rpb_T", [2 * 32, NJ * CH])
        with phase(nc, names) as (block, s):
            @block.sync
            def _(sp):
                sp.dma_start(pick[:, :, :], w["c_pick"]).then_inc(s["pick_in"], 16)
                sp.wait_ge(s["masked"], 1)
                for r in range(2):
                    for j in range(NJ):
                        sp.dma_start(rpb[j * CH:(j + 1) * CH, r, 0:DX], w["odd_rpb_2"][0, :, j + 5 - r, :]).then_inc(s["rpb_in"], 16)

            @block.gpsimd
            def _(pool):
                pool.memset(rpb[:, :, :], NEG).then_inc(s["masked"], 1)

            @block.tensor
            def _(pe):
                pe.wait_ge(s["rpb_in"], 16 * 2 * NJ)
                pe.transpose(k.ps[0:64, 6, 0:NJ * CH], rpb[:, :, :].rearrange("a r x -> a (r x)"),
                             k.ident[0:NJ * CH, 0:NJ * CH]).then_inc(s["rpb_turned"], 1)
                pe.wait_ge(s["pick_in"], 16)
                pe.wait_ge(s["rpb_ready"], 1)
                for c in range(GW):
                    n = c // PER
                    if c % PER == 0 and n >= 4:
                        pe.wait_ge(s["bias_used"], n - 3)
                    last = pe.matmul(k.ps[:, 2 + n % 4, c % PER * NJ * CH:(c % PER + 1) * NJ * CH], pick[:, c, :], rpb_T[:, :],
                                     start=True, stop=True, skip_group_check=True)
                    if c % PER == PER - 1 or c == GW - 1:
                        last.then_inc(s["bias_done"], 1)

            @block.vector
            def _(dve):
                dve.wait_ge(s["rpb_turned"], 1)
                dve.tensor_copy(rpb_T[:, :], k.ps[0:64, 6, 0:NJ * CH]).then_inc(s["rpb_ready"], 1)
                for n in range((GW + PER - 1) // PER):
                    m = min(PER, GW - n * PER)
                    dve.wait_ge(s["bias_done"], n + 1)
                    for j in range(NJ):
                        last = dve.tensor_copy(b.bias[:, :, j, n * PER:n * PER + m].rearrange("p h c -> p c h"),
                                               k.ps[:, 2 + n % 4, 0:m * NJ * CH].rearrange("p (c j h) -> p c j h", j=NJ, h=CH)[:, :, j, :])
                    last.then_inc(s["bias_used"], 1)
                for l in range(DEPTH):
                    for at, name, plus in ((1, "pre_mix", 1.0), (2, "post_mix", 0.0), (4, "pre_ffn", 1.0), (5, "post_ffn", 0.0)):
                        part = b.mod[:, l, at * FT:(at + 1) * FT, :]
                        weight = k.par[:, PAR[name] + l * FT:PAR[name] + (l + 1) * FT].unsqueeze(2).broadcast_to([P, FT, 2])
                        dve.scalar_tensor_tensor(part, part, plus, weight, ALU.add, ALU.mult)


def prenorm_phase(nc, k, b, l, ffn, streams):
    names = ["sq_done", "sum_done", "std_done", "r_done", "n_done"]
    c0, n = streams[0] * S, len(streams) * S
    with ExitStack() as ctx:
        def sb(name, shape):
            return ctx.enter_context(nc.sbuf_tensor(f"{name}_{nc.next_id()}", shape, F32))
        sq = sb("squares", [P, FT, n])
        std = sb("pre_std", [P, n])
        r = sb("pre_r", [P, n])
        with phase(nc, names) as (block, s):
            def scale(f, st):
                return b.mod[:, l, (4 if ffn else 1) * FT + f, st:st + 1]

            def shift(f, st):
                return b.mod[:, l, (3 if ffn else 0) * FT + f, st:st + 1]

            @block.scalar
            def _(act):
                for f in range(FT):
                    act.activation(sq[:, f, :], k.x_T[:, f, c0:c0 + n], ACT.Square).then_inc(s["sq_done"], 1)
                act.wait_ge(s["sum_done"], 1)
                act.activation(std[:, :], k.ps[:, 0, 0:n], ACT.Sqrt, bias=k.eps[:, 1:2]).then_inc(s["std_done"], 1)
                for f in range(FT):
                    act.wait_ge(s["n_done"], f + 1)
                    for st in streams:
                        cols = slice(st * S, (st + 1) * S)
                        act.activation(b.h_T[:, f, cols], b.h_T[:, f, cols], ACT.Identity, bias=shift(f, st), scale=scale(f, st))

            @block.tensor
            def _(pe):
                for f in range(FT):
                    pe.wait_ge(s["sq_done"], f + 1)
                    last = pe.matmul(k.ps[:, 0, 0:n], k.mean[:, :], sq[:, f, :], start=(f == 0), stop=(f == FT - 1))
                last.then_inc(s["sum_done"], 1)

            @block.vector
            def _(dve):
                dve.wait_ge(s["std_done"], 1)
                dve.reciprocal(r[:, :], std[:, :]).then_inc(s["r_done"], 1)
                dve.wait_ge(s["r_done"], 1)
                for f in range(FT):
                    dve.tensor_tensor(b.h_T[:, f, c0:c0 + n], k.x_T[:, f, c0:c0 + n], r[:, :], ALU.mult).then_inc(s["n_done"], 1)


def gqa_project(nc, k, b, m, w):
    names = ["w_in", "tab_in", "p_done", "p_used", "copied", "sq_done", "ss_done", "std_done", "step", "rot_done", "turned"]
    NQK = GQ + GKV
    with ExitStack() as ctx:
        def sb(name, shape):
            return ctx.enter_context(nc.sbuf_tensor(f"{name}_{nc.next_id()}", shape, F32))
        wq = sb("gqa_w", [P, FT, BQ0])
        gain = sb("qk_gain", [P, NQK, HD2])
        cos, sin = sb("cos", [P, TT, HD2 // 2]), sb("sin", [P, TT, HD2 // 2])
        sq = sb("qk_sq", [P, NQK * HD2])
        ss, std, r = sb("qk_ss", [P, NQK]), sb("qk_std", [P, NQK]), sb("qk_r", [P, NQK])
        part = [sb(f"rot{n}", [P, NQK, HD2 // 2]) for n in range(4)]
        kd = sb("k_twice", [P, 2 * TT, GKV, 2, HD2])
        with phase(nc, names) as (block, s):

            @block.sync
            def _(sp):
                w_in = w["even_w_in_2"][0].rearrange("(f p) n -> p f n", p=P)
                for f in range(FT):
                    sp.dma_start(wq[:, f, :], w_in[:, f, 0:BQ0]).then_inc(s["w_in"], 16)
                for h in range(NQK):
                    g = w["even_q_norm_2"] if h < GQ else w["even_k_norm_2"]
                    sp.dma_start(gain[:, h, :], g.broadcast_to([P, HD2])).then_inc(s["tab_in"], 16)
                sp.dma_start(cos[:, :, :], w["c_cos"]).then_inc(s["tab_in"], 16)
                sp.dma_start(sin[:, :, :], w["c_sin"]).then_inc(s["tab_in"], 16)

            @block.tensor
            def _(pe):
                pe.wait_ge(s["w_in"], 16 * FT)
                for tt in range(2 * TT):
                    if tt >= 2:
                        pe.wait_ge(s["p_used"], tt - 1)
                    for bank, c0, c1 in ((0, 0, BANK), (1, BANK, BQ0)):
                        for f in range(FT):
                            last = pe.matmul(k.ps[:, 2 * (tt % 2) + bank, 0:c1 - c0], b.h_T[:, f, tt * P:(tt + 1) * P], wq[:, f, c0:c1],
                                             start=(f == 0), stop=(f == FT - 1))
                    last.then_inc(s["p_done"], 1)
                pe.wait_ge(s["rot_done"], 2 * TT)
                for g in range(GKV):
                    for tt in range(2 * TT):
                        last = pe.transpose(k.ps[:, 4 + g, tt * P:(tt + 1) * P], kd[:, tt, g, :, :].rearrange("p a d -> p (a d)"), k.ident[:, :])
                    last.then_inc(s["turned"], 1)

            @block.scalar
            def _(act):
                for tt in range(2 * TT):
                    act.wait_ge(s["p_done"], tt + 1)
                    both = k.ps[:, 2 * (tt % 2):2 * (tt % 2) + 2, :].rearrange("p b n -> p (b n)")
                    act.activation(m.qk[:, tt, :], both[:, 0:NQK * HD2], ACT.Copy).then_inc(s["copied"], 1)
                    act.activation(m.v[:, tt, :], both[:, NQK * HD2:BQ0], ACT.Copy).then_inc(s["p_used"], 1)
                    act.wait_ge(s["copied"], tt + 1)
                    if tt >= 1:
                        act.wait_ge(s["std_done"], tt)
                    act.activation(sq[:, :], m.qk[:, tt, :], ACT.Square).then_inc(s["sq_done"], 1)
                    act.wait_ge(s["ss_done"], tt + 1)
                    act.activation(std[:, :], ss[:, :], ACT.Sqrt, bias=k.eps[:, 1:2], scale=1.0 / HD2).then_inc(s["std_done"], 1)
                for g in range(GKV):
                    act.wait_ge(s["turned"], g + 1)
                    act.activation(m.k_T[:, g, :], k.ps[:, 4 + g, :], ACT.Copy)

            @block.vector
            def _(dve):
                c = Chain(dve, s["step"])
                dve.wait_ge(s["tab_in"], 16 * (NQK + 2))
                half = HD2 // 2
                for tt in range(2 * TT):
                    qk = m.qk[:, tt, :].rearrange("p (h d) -> p h d", d=HD2)
                    dve.wait_ge(s["sq_done"], tt + 1)
                    dve.reduce_sum(ss[:, :], sq[:, :].rearrange("p (h d) -> p h d", d=HD2), AX.X).then_inc(s["ss_done"], 1)
                    dve.wait_ge(s["std_done"], tt + 1)
                    c.link(dve.reciprocal(r[:, :], std[:, :]))
                    c.link(dve.tensor_tensor(qk, qk, r[:, :].unsqueeze(2).broadcast_to([P, NQK, HD2]), ALU.mult))
                    c.link(dve.tensor_tensor(qk, qk, gain[:, :, :], ALU.mult))
                    if tt < TT:
                        x1, x2 = qk[:, :, 0:half], qk[:, :, half:HD2]
                        ct, st = (a[:, tt, :].unsqueeze(1).broadcast_to([P, NQK, half]) for a in (cos, sin))
                        dve.tensor_tensor(part[0][:, :, :], x1, ct, ALU.mult)
                        dve.tensor_tensor(part[1][:, :, :], x2, st, ALU.mult)
                        dve.tensor_tensor(part[2][:, :, :], x1, st, ALU.mult)
                        c.link(dve.tensor_tensor(part[3][:, :, :], x2, ct, ALU.mult))
                        dve.tensor_tensor(x1, part[0][:, :, :], part[1][:, :, :], ALU.subtract)
                        c.link(dve.tensor_tensor(x2, part[2][:, :, :], part[3][:, :, :], ALU.add))
                    keys = m.qk[:, tt, GQ * HD2:NQK * HD2].rearrange("p (g d) -> p g d", d=HD2)
                    for a in range(2):
                        last = dve.tensor_copy(kd[:, tt, :, a, :], keys)
                    last.then_inc(s["rot_done"], 1)


def soft_tensor(pe, k, s, a, units, base, extra, first_value):
    def scores(u):
        if u >= 3:
            pe.wait_ge(s["e_ready"], base + (u - 2))
        pe.matmul(k.ps[:, a.banks[u % 3], 0:units[u].n], units[u].q, units[u].key, start=True, stop=True).then_inc(s["s_done"], 1)

    def turn(u):
        pe.wait_ge(s["p_ready"], base + (u + 1))
        if u >= 2:
            pe.wait_ge(s["t_ready"], base + (u - 1))
        for c in range(units[u].n // P):
            last = pe.transpose(k.ps[:, 2 + u % 2, c * P:(c + 1) * P], a.e[:, u % 3, c * P:(c + 1) * P], k.ident[:, :])
        last.then_inc(s["t_done"], 1)

    def values(u):
        if u == 0:
            first_value()
        pe.wait_ge(s["t_ready"], base + (u + 1))
        for c, v in enumerate(units[u].v):
            last = pe.matmul(units[u].out, v, a.pt[:, u % 2, c, :], start=(c == 0), stop=(c == len(units[u].v) - 1),
                             skip_group_check=True)
        last.then_inc(s["pv_done"], 1)

    nu = len(units)
    for u in range(nu + 3):
        if u < nu:
            extra(u)
            scores(u)
        if 2 <= u < nu + 2:
            turn(u - 2)
        if u >= 3:
            values(u - 3)


def soft_vector(dve, k, s, a, units, base):
    nu = len(units)
    for u in range(nu + 1):
        if u < nu:
            n, bias, bank = units[u].n, units[u].bias, a.banks[u % 3]
            dve.wait_ge(s["s_done"], base + (u + 1))
            if bias is not None:
                part = k.ps[:, bank, 0:S].rearrange("p (r c) -> p r c", c=GW)
                dve.tensor_tensor(part, part, bias, ALU.add).then_inc(s["bias_step"], 1)
                dve.wait_ge(s["bias_step"], base + (u + 1))
            dve.reduce_max(a.nmax[:, u % 3:u % 3 + 1], k.ps[:, bank, 0:n], AX.X, negate=True).then_inc(s["max_ready"], 1)
        if u >= 1:
            v = u - 1
            dve.wait_ge(s["e_ready"], base + (v + 1))
            dve.reciprocal(a.rs[:, v % 3:v % 3 + 1], a.sums[:, v % 3:v % 3 + 1]).then_inc(s["rs_step"], 1)
            dve.wait_ge(s["rs_step"], base + (v + 1))
            e = a.e[:, v % 3, 0:units[v].n]
            dve.tensor_scalar(e, e, a.rs[:, v % 3:v % 3 + 1], None, ALU.mult).then_inc(s["p_ready"], 1)


def soft_scalar(act, k, s, a, units, base):
    nu = len(units)
    for u in range(nu + 2):
        if u < nu:
            n = units[u].n
            act.wait_ge(s["max_ready"], base + (u + 1))
            if u >= 3:
                act.wait_ge(s["t_done"], base + (u - 2))
            act.activation(a.e[:, u % 3, 0:n], k.ps[:, a.banks[u % 3], 0:n], ACT.Exp, bias=a.nmax[:, u % 3:u % 3 + 1],
                           accum_out=a.sums[:, u % 3:u % 3 + 1]).then_inc(s["e_ready"], 1)
        if u >= 2:
            v = u - 2
            n = units[v].n
            act.wait_ge(s["t_done"], base + (v + 1))
            if v >= 2:
                act.wait_ge(s["pv_done"], base + (v - 1))
            act.activation(a.pt[:, v % 2, 0:n // P, :].rearrange("p c t -> p (c t)"), k.ps[:, 2 + v % 2, 0:n], ACT.Copy).then_inc(s["t_ready"], 1)


SOFT_SEMS = ["s_done", "bias_step", "max_ready", "e_ready", "rs_step", "p_ready", "t_done", "t_ready", "pv_done"]


def soft_buffers(nc, ctx, third_bank):
    def sb(name, shape):
        return ctx.enter_context(nc.sbuf_tensor(f"{name}_{nc.next_id()}", shape, F32))
    got = Buffers()
    got.banks = (0, 1, third_bank)
    got.e = sb("soft_e", [P, 3, 2 * S])
    got.pt = sb("soft_pt", [P, 2, 4, P])
    got.nmax = sb("soft_max", [P, 3])
    got.sums = sb("soft_sums", [P, 3])
    got.rs = sb("soft_rs", [P, 3])
    return got


def gqa_attend(nc, k, b, m, w):
    names = ["q_staged", "q_turned", "q_ready", "o_used"] + SOFT_SEMS
    NP = GQ // GKV // 2
    with ExitStack() as ctx:
        def sb(name, shape):
            return ctx.enter_context(nc.sbuf_tensor(f"{name}_{nc.next_id()}", shape, F32))
        q_st = sb("gqa_q_st", [P, GKV, 2 * TT, P])
        q_T = sb("gqa_q_T", [P, GKV, S + CTX])
        a = soft_buffers(nc, ctx, 6)
        with phase(nc, names) as (block, s):
            units = []
            for g in range(GKV):
                for hh in range(2):
                    rows = slice(HD2 * hh, HD2 * hh + HD2)
                    for tt in range(2 * TT):
                        first = 0 if tt < TT else TT
                        units.append(Unit(
                            q=q_T[rows, g, tt * P:(tt + 1) * P], key=m.k_T[rows, g, first * P:S + CTX], n=(2 * TT - first) * P, bias=None,
                            v=[m.v[:, c, g * HD2:(g + 1) * HD2] for c in range(first, 2 * TT)],
                            out=k.ps[rows, 4 + g, tt * P:(tt + 1) * P]))
            nu = len(units)

            @block.gpsimd
            def _(pool):
                with pool.Fori(0, NP) as j:
                    for g in range(GKV):
                        pool.tensor_copy(q_st[:, g, :, :], m.qk[:, :, ds((j + g * NP) * P, P)]).then_inc(s["q_staged"], 1)
                    pool.wait_ge(s["q_turned"], j * 2 + 2)

            @block.tensor
            def _(pe):
                with pe.Fori(0, NP) as j:
                    for g in range(GKV):
                        pe.wait_ge(s["q_staged"], j * 2 + (g + 1))
                        for tt in range(2 * TT):
                            last = pe.transpose(k.ps[:, 6 + g, tt * P:(tt + 1) * P], q_st[:, g, tt, :], k.ident[:, :])
                        last.then_inc(s["q_turned"], 1)

                    def queries(u):
                        if u % (nu // GKV) == 0:
                            pe.wait_ge(s["q_ready"], j * 2 + (u // (nu // GKV) + 1))

                    def outputs():
                        pe.wait_ge(s["o_used"], j * 2 + 2)
                    soft_tensor(pe, k, s, a, units, j * nu, queries, outputs)

            @block.vector
            def _(dve):
                with dve.Fori(0, NP) as j:
                    soft_vector(dve, k, s, a, units, j * nu)

            @block.scalar
            def _(act):
                act.sem_inc(s["o_used"], 2)
                with act.Fori(0, NP) as j:
                    for g in range(GKV):
                        act.wait_ge(s["q_turned"], j * 2 + (g + 1))
                        act.activation(q_T[:, g, :], k.ps[:, 6 + g, :], ACT.Copy, scale=HD2 ** -0.5).then_inc(s["q_ready"], 1)
                    soft_scalar(act, k, s, a, units, j * nu)
                    for g in range(GKV):
                        act.wait_ge(s["pv_done"], j * nu + (g + 1) * (nu // GKV))
                        act.activation(b.y_T[:, ds(j + g * NP, 1), :].rearrange("p a t -> p (a t)"), k.ps[:, 4 + g, :], ACT.Copy).then_inc(s["o_used"], 1)


def odd_attend(nc, k, b, w):
    names = ["w0_in", "w1_in", "proj_done", "proj_used", "o_used"] + SOFT_SEMS
    NPAIR = CH // 2
    with ExitStack() as ctx:
        def sb(name, shape):
            return ctx.enter_context(nc.sbuf_tensor(f"{name}_{nc.next_id()}", shape, F32))
        wq = [sb(f"odd_w{n}", [P, 3, FT, P]) for n in range(2)]
        q_T = sb("odd_q_T", [P, 2, S])
        k_T = sb("odd_k_T", [P, 2, S + CTX])
        v = sb("odd_v", [P, 2, 2 * TT, P])
        a = soft_buffers(nc, ctx, 5)
        with phase(nc, names) as (block, s):
            w_in = [s["w0_in"], s["w1_in"]]
            cols = w["odd_w_qkv_2"][0].rearrange("(f p) (a i n) -> i a p f n", p=P, a=3, n=P)

            def make_units(j):
                units = []
                for pp in range(2):
                    for hh in range(2):
                        rows = slice(HD2 * hh, HD2 * hh + HD2)
                        for tt in range(TT):
                            bias = None if j is None else b.bias[:, ds(j * 4 + (2 * pp + hh), 1), 2 - 2 * tt:2 - 2 * tt + NROW, :].rearrange(
                                "p a r c -> p (a r) c")
                            units.append(Unit(
                                q=q_T[rows, pp, tt * P:(tt + 1) * P], key=k_T[rows, pp, :], n=S + CTX, bias=bias,
                                v=[v[:, pp, c, rows] for c in range(2 * TT)],
                                out=k.ps[rows, 4, pp * S + tt * P:pp * S + (tt + 1) * P]))
                return units
            nu = len(make_units(None))

            @block.sync
            def _(sp):
                def load(i, n):
                    for part in range(3):
                        sp.dma_start(wq[n][:, part, :, :], cols[i, part]).then_inc(w_in[n], 16)
                for n in range(2):
                    load(n, n)
                with sp.Fori(0, NPAIR // 2 - 1) as j:
                    for n in range(2):
                        sp.wait_ge(s["proj_done"], j * 6 + (3 * n + 3))
                        load(j * 2 + (n + 2), n)

            @block.tensor
            def _(pe):
                with pe.Fori(0, NPAIR // 2) as j:
                    for n in range(2):
                        pe.wait_ge(w_in[n], j * 48 + 48)
                        if n == 1:
                            pe.wait_ge(s["proj_used"], j * 6 + 1)
                        for f in range(FT):
                            last = pe.matmul(k.ps[:, 6, 0:S], wq[n][:, 0, f, :], b.h_T[:, f, 0:S], start=(f == 0), stop=(f == FT - 1))
                        last.then_inc(s["proj_done"], 1)
                        if n == 1:
                            pe.wait_ge(s["proj_used"], j * 6 + 2)
                        for f in range(FT):
                            last = pe.matmul(k.ps[:, 7, :], wq[n][:, 1, f, :], b.h_T[:, f, :], start=(f == 0), stop=(f == FT - 1))
                        last.then_inc(s["proj_done"], 1)
                        if n == 1:
                            pe.wait_ge(s["proj_used"], j * 6 + 3)
                        for tt in range(2 * TT):
                            for f in range(FT):
                                last = pe.matmul(k.ps[:, 5, tt * P:(tt + 1) * P], b.h_T[:, f, tt * P:(tt + 1) * P], wq[n][:, 2, f, :],
                                                 start=(f == 0), stop=(f == FT - 1), skip_group_check=True)
                        last.then_inc(s["proj_done"], 1)

                    def pair(u):
                        if u == 0 or u == 2:
                            pe.wait_ge(s["proj_used"], j * 6 + (3, 6)[u // 2])

                    def outputs():
                        pe.wait_ge(s["o_used"], j + 1)
                    soft_tensor(pe, k, s, a, make_units(None), j * nu, pair, outputs)

            @block.vector
            def _(dve):
                with dve.Fori(0, NPAIR // 2) as j:
                    soft_vector(dve, k, s, a, make_units(j), j * nu)

            @block.scalar
            def _(act):
                act.sem_inc(s["o_used"], 1)
                with act.Fori(0, NPAIR // 2) as j:
                    for n in range(2):
                        act.wait_ge(s["proj_done"], j * 6 + (3 * n + 1))
                        act.activation(q_T[:, n, :], k.ps[:, 6, 0:S], ACT.Copy, scale=HD2 ** -0.5).then_inc(s["proj_used"], 1)
                        act.wait_ge(s["proj_done"], j * 6 + (3 * n + 2))
                        act.activation(k_T[:, n, :], k.ps[:, 7, :], ACT.Copy).then_inc(s["proj_used"], 1)
                        act.wait_ge(s["proj_done"], j * 6 + (3 * n + 3))
                        act.activation(v[:, n, :, :].rearrange("p t d -> p (t d)"), k.ps[:, 5, :], ACT.Copy).then_inc(s["proj_used"], 1)
                    soft_scalar(act, k, s, a, make_units(None), j * nu)
                    act.wait_ge(s["pv_done"], j * nu + nu)
                    act.activation(b.y_T[:, ds(j * 2, 2), 0:S], k.ps[:, 4, :].rearrange("p (a t) -> p a t", a=2), ACT.Copy).then_inc(s["o_used"], 1)


def hgrn_phase(nc, k, b, w):
    names = ["w_in", "tab_in", "proj_done", "q_ready", "q_scaled", "k_ready", "abs_ready", "soft_step", "g_ready", "v_ready", "g_turned",
             "g_tok", "cum_done", "e_ready", "qk_q", "qk_k", "sc_done", "masked", "p_ready", "pv_done", "x_ready", "x_done", "x_used",
             "o_done", "sq_done", "std_done", "r_step", "y_ready", "y_turned", "y_used"]
    TILES = 2 * TT
    NU = 2 * TILES
    UNITS = [(d, tt) for d in range(2) for tt in range(TILES)]
    N9 = NLV + 2
    N8 = NLV + 1
    with ExitStack() as ctx:
        def sb(name, shape):
            return ctx.enter_context(nc.sbuf_tensor(f"{name}_{nc.next_id()}", shape, F32))
        wh = sb("hgrn_w", [P, FT, 5, P])
        cum = sb("hgrn_cum", [P, 2, N9 * P])
        lvl = sb("hgrn_lvl", [P, 2, N8 * P])
        gain = sb("hgrn_gain", [P, P])
        q = sb("hgrn_q", [P, TILES, P])
        kk = sb("hgrn_k", [P, 2, TILES, P])
        ab = sb("hgrn_abs", [P, 2, TILES * P])
        g = sb("hgrn_g", [P, 2, TILES, P])
        g_tok = sb("hgrn_g_tok", [P, 2, TILES, P])
        v = sb("hgrn_v", [P, TILES, P])
        sg = sb("hgrn_gate", [P, TILES, P])
        e = sb("hgrn_e", [P, 2, N9, P])
        kd = sb("hgrn_kd", [P, 2, NLV, P])
        qd = sb("hgrn_qd", [P, 2, NLV, P])
        ke = sb("hgrn_ke", [P, NU, P])
        qs = sb("hgrn_qs", [P, NU, P])
        pm = sb("hgrn_pm", [P, 2, N8, P])
        pr = sb("hgrn_p", [P, 2, P])
        tot = sb("hgrn_tot", [P, NU])
        kx = sb("hgrn_kx", [P, 2, P])
        qx = sb("hgrn_qx", [P, 2, P])
        px = sb("hgrn_px", [P, 2, 6, P])
        sq = sb("hgrn_sq", [P, TILES, P])
        ss, std, r = sb("hgrn_ss", [P, TILES]), sb("hgrn_std", [P, TILES]), sb("hgrn_r", [P, TILES])
        y = sb("hgrn_y", [P, TILES, P])
        with phase(nc, names) as (block, s):
            cols = w["even_w_in_2"][0][:, BQ0:BQ0 + 5 * BH * P].rearrange("(f p) (a i n) -> i a p f n", p=P, a=5, n=P)
            flat = k.ps[:, :, :].rearrange("p b n -> p (b n)")
            CUM_PS = flat[:, 0:N9 * P]
            SC_PS = flat[:, 3 * BANK:3 * BANK + N8 * P]
            X_PS = flat[:, 5 * BANK:5 * BANK + 6 * P]
            O = 7

            def order(d, stream):
                tiles = (0, 1) if stream == 0 else (2, 3)
                return tiles if d == 0 else tiles[::-1]

            def cross(d):
                l0, l1 = order(d, 0)
                c0, c1 = order(d, 1)
                key = lambda tt: ke[:, d * TILES + tt, :]
                qry = lambda tt: qs[:, d * TILES + tt, :]
                return [(c0, c1, key(c0), qry(c1)), (l0, l1, key(l0), qry(l1)),
                        (c0, l0, kx[:, d, :], qry(l0)), (c0, l1, kx[:, d, :], qx[:, d, :]),
                        (c1, l0, key(c1), qry(l0)), (c1, l1, key(c1), qx[:, d, :])]

            @block.sync
            def _(sp):
                sp.dma_start(cum[:, :, :], w["c_cum"]).then_inc(s["tab_in"], 16)
                sp.dma_start(lvl[:, :, :], w["c_lvl"]).then_inc(s["tab_in"], 16)
                sp.dma_start(gain[:, :], w["hgrn_out_norm_2"].broadcast_to([P, P])).then_inc(s["tab_in"], 16)

                def load(i):
                    for part in range(5):
                        sp.dma_start(wh[:, :, part, :], cols[i, part]).then_inc(s["w_in"], 16)
                load(0)
                with sp.Fori(0, BH - 1) as i:
                    sp.wait_ge(s["proj_done"], i * 5 + 5)
                    load(i + 1)

            @block.tensor
            def _(pe):
                pe.wait_ge(s["tab_in"], 48)
                with pe.Fori(0, BH) as i:
                    pe.wait_ge(s["w_in"], i * 80 + 80)
                    for part in range(3):
                        for f in range(FT):
                            last = pe.matmul(k.ps[:, part, :], wh[:, f, part, :], b.h_T[:, f, :], start=(f == 0), stop=(f == FT - 1))
                        last.then_inc(s["proj_done"], 1)
                    for tt in range(TILES):
                        for f in range(FT):
                            last = pe.matmul(k.ps[:, 3 + tt // 2, tt % 2 * 2 * P:(tt % 2 + 1) * 2 * P], b.h_T[:, f, tt * P:(tt + 1) * P],
                                             wh[:, f, 3:5, :].rearrange("p a n -> p (a n)"), start=(f == 0), stop=(f == FT - 1),
                                             skip_group_check=True)
                        if tt % 2:
                            last.then_inc(s["proj_done"], 1)
                    for d in range(2):
                        pe.wait_ge(s["g_ready"], i * 2 + (d + 1))
                        for tt in range(TILES):
                            last = pe.transpose(k.ps[:, 5 + d, tt * P:(tt + 1) * P], g[:, d, tt, :], k.ident[:, :])
                        last.then_inc(s["g_turned"], 1)
                    pe.matmul(k.ps[:, O, :], k.zero[:, :], b.h_T[:, 0, :], start=True, stop=False, skip_group_check=True)
                    pe.wait_ge(s["g_tok"], i * 2 + 2)
                    pe.wait_ge(s["q_ready"], i + 1)
                    pe.wait_ge(s["k_ready"], i * 2 + 2)

                    def sums(u):
                        d, tt = UNITS[u]
                        if u >= 1:
                            pe.wait_ge(s["e_ready"], i * NU + u)
                        for c in range(0, N9 * P, BANK):
                            n = min(BANK, N9 * P - c)
                            last = pe.matmul(CUM_PS[:, c:c + n], g_tok[:, d, tt, :], cum[:, d, c:c + n], start=True, stop=True)
                        last.then_inc(s["cum_done"], 1)

                    def scores(u):
                        d, tt = UNITS[u]
                        pe.wait_ge(s["qk_q"], i * NU + (u + 1))
                        pe.wait_ge(s["qk_k"], i * NU + (u + 1))
                        if u >= 1:
                            pe.wait_ge(s["masked"], i * NU + u)
                        else:
                            pe.wait_ge(s["v_ready"], i * 2 + 2)
                        for n in range(NLV):
                            pe.matmul(SC_PS[:, n * P:(n + 1) * P], kd[:, u % 2, n, :], qd[:, u % 2, n, :], start=True, stop=True,
                                      skip_group_check=True)
                        pe.matmul(SC_PS[:, NLV * P:N8 * P], kk[:, d, tt, :], q[:, tt, :], start=True, stop=True,
                                  skip_group_check=True).then_inc(s["sc_done"], 1)

                    def values(u):
                        d, tt = UNITS[u]
                        pe.wait_ge(s["p_ready"], i * NU + (u + 1))
                        pe.matmul(k.ps[:, O, tt * P:(tt + 1) * P], pr[:, u % 2, :], v[:, tt, :], start=False, stop=False,
                                  skip_group_check=True).then_inc(s["pv_done"], 1)

                    for u in range(NU + 2):
                        if u < NU:
                            sums(u)
                        if 1 <= u <= NU:
                            scores(u - 1)
                        if u >= 2:
                            values(u - 2)
                    for d in range(2):
                        pe.wait_ge(s["x_ready"], i * 2 + (d + 1))
                        if d == 1:
                            pe.wait_ge(s["x_used"], i * 2 + 1)
                        for n, (_, _, key, qry) in enumerate(cross(d)):
                            last = pe.matmul(X_PS[:, n * P:(n + 1) * P], key, qry, start=True, stop=True, skip_group_check=True)
                        last.then_inc(s["x_done"], 1)
                    for d in range(2):
                        pe.wait_ge(s["x_used"], i * 2 + (d + 1))
                        for n, (src, dst, _, _) in enumerate(cross(d)):
                            last = pe.matmul(k.ps[:, O, dst * P:(dst + 1) * P], px[:, d, n, :], v[:, src, :], start=False,
                                             stop=(d == 1), skip_group_check=True)
                    last.then_inc(s["o_done"], 1)
                    pe.wait_ge(s["y_ready"], i + 1)
                    for tt in range(TILES):
                        last = pe.transpose(k.ps[:, 5, tt * P:(tt + 1) * P], y[:, tt, :], k.ident[:, :])
                    last.then_inc(s["y_turned"], 1)
                    pe.wait_ge(s["y_used"], i + 1)

            @block.scalar
            def _(act):
                with act.Fori(0, BH) as i:
                    act.wait_ge(s["proj_done"], i * 5 + 1)
                    act.activation(q[:, :, :].rearrange("p t d -> p (t d)"), k.ps[:, 0, :], ACT.Silu).then_inc(s["q_ready"], 1)
                    for n in range(2):
                        act.wait_ge(s["proj_done"], i * 5 + (4 + n))
                        both = k.ps[:, 3 + n, :].rearrange("p (t a d) -> p t a d", t=2, a=2)
                        act.activation(sg[:, 2 * n:2 * n + 2, :], both[:, :, 1, :], ACT.Silu)
                        act.activation(v[:, 2 * n:2 * n + 2, :], both[:, :, 0, :], ACT.Copy).then_inc(s["v_ready"], 1)
                    for d in range(2):
                        act.activation(kk[:, d, :, :].rearrange("p t d -> p (t d)"), k.ps[:, 1 + d, :], ACT.Sigmoid, scale=-1.0)
                        act.activation(ab[:, d, :], k.ps[:, 1 + d, :], ACT.Abs).then_inc(s["abs_ready"], 1)
                    act.wait_ge(s["abs_ready"], i * 2 + 2)
                    for d in range(2):
                        act.activation(ab[:, d, :], ab[:, d, :], ACT.Exp, scale=-1.0).then_inc(s["soft_step"], 1)
                    act.wait_ge(s["soft_step"], i * 4 + 2)
                    for d in range(2):
                        act.activation(ab[:, d, :], ab[:, d, :], ACT.Ln, bias=k.eps[:, 2:3]).then_inc(s["soft_step"], 1)
                    for d in range(2):
                        act.wait_ge(s["g_turned"], i * 2 + (d + 1))
                        act.activation(g_tok[:, d, :, :].rearrange("p t d -> p (t d)"), k.ps[:, 5 + d, :], ACT.Copy).then_inc(s["g_tok"], 1)
                    for u in range(NU):
                        act.wait_ge(s["cum_done"], i * NU + (u + 1))
                        if u >= 2:
                            act.wait_ge(s["qk_q"], i * NU + (u - 1))
                            act.wait_ge(s["qk_k"], i * NU + (u - 1))
                        act.activation(e[:, u % 2, :, :].rearrange("p n t -> p (n t)"), CUM_PS, ACT.Exp).then_inc(s["e_ready"], 1)
                    for d in range(2):
                        act.wait_ge(s["x_done"], i * 2 + (d + 1))
                        act.activation(px[:, d, :, :].rearrange("p n t -> p (n t)"), X_PS, ACT.Copy).then_inc(s["x_used"], 1)
                    act.wait_ge(s["o_done"], i + 1)
                    for tt in range(TILES):
                        last = act.activation(sq[:, tt, :], k.ps[:, O, tt * P:(tt + 1) * P], ACT.Square, accum_out=ss[:, tt:tt + 1])
                    last.then_inc(s["sq_done"], 1)
                    act.wait_ge(s["sq_done"], i + 1)
                    act.activation(std[:, :], ss[:, :], ACT.Sqrt, bias=k.eps[:, 1:2], scale=1.0 / P).then_inc(s["std_done"], 1)
                    act.wait_ge(s["y_turned"], i + 1)
                    act.activation(b.y_T[:, ds(i + BH, 1), :].rearrange("p a t -> p (a t)"), k.ps[:, 5, :], ACT.Copy).then_inc(s["y_used"], 1)

            @block.gpsimd
            def _(pool):
                with pool.Fori(0, BH) as i:
                    pool.wait_ge(s["abs_ready"], i * 2 + 2)
                    for u in range(NU):
                        d, tt = UNITS[u]
                        pool.wait_ge(s["e_ready"], i * NU + (u + 1))
                        if u >= 2:
                            pool.wait_ge(s["sc_done"], i * NU + (u - 1))
                        pool.tensor_tensor(ke[:, u, :], e[:, u % 2, 0, :], kk[:, d, tt, :], ALU.mult)
                        pool.tensor_tensor(kd[:, u % 2, :, :], e[:, u % 2, 1:N8, :], kk[:, d, tt, :].unsqueeze(1).broadcast_to([P, NLV, P]),
                                           ALU.mult).then_inc(s["qk_k"], 1)

            @block.vector
            def _(dve):
                with dve.Fori(0, BH) as i:
                    dve.wait_ge(s["q_ready"], i + 1)
                    q_all = q[:, :, :].rearrange("p t d -> p (t d)")
                    dve.tensor_scalar(q_all, q_all, HGRN_SCALE, None, ALU.mult).then_inc(s["q_scaled"], 1)
                    for d in range(2):
                        dve.wait_ge(s["soft_step"], i * 4 + (3 + d))
                        dve.scalar_tensor_tensor(g[:, d, :, :].rearrange("p t d -> p (t d)"), k.ps[:, 1 + d, :], 0.0, ab[:, d, :], ALU.min,
                                                 ALU.subtract).then_inc(s["g_ready"], 1)
                    dve.wait_ge(s["g_ready"], i * 2 + 2)
                    dve.wait_ge(s["v_ready"], i * 2 + 2)
                    dve.tensor_tensor(sg[:, :, :], sg[:, :, :], gain[:, :].unsqueeze(1).broadcast_to([P, TILES, P]), ALU.mult).then_inc(s["k_ready"], 2)
                    dve.wait_ge(s["q_scaled"], i + 1)

                    def probs(u):
                        dve.wait_ge(s["sc_done"], i * NU + (u + 1))
                        if u >= 2:
                            dve.wait_ge(s["p_ready"], i * NU + (u - 1))
                        dve.tensor_tensor(pm[:, u % 2, :, :].rearrange("p n t -> p (n t)"), SC_PS, lvl[:, UNITS[u][0], :], ALU.mult).then_inc(s["masked"], 1)
                        dve.wait_ge(s["masked"], i * NU + (u + 1))
                        if u >= 2:
                            dve.wait_ge(s["pv_done"], i * NU + (u - 1))
                        dve.reduce_sum(pr[:, u % 2, :], pm[:, u % 2, :, :].rearrange("p n t -> p t n"), AX.X).then_inc(s["p_ready"], 1)

                    for u in range(NU + 1):
                        if u < NU:
                            d, tt = UNITS[u]
                            dve.wait_ge(s["e_ready"], i * NU + (u + 1))
                            end = P - 1 if d == 0 else 0
                            dve.tensor_copy(tot[:, u:u + 1], e[:, u % 2, N9 - 1, end:end + 1])
                            dve.tensor_tensor(qs[:, u, :], e[:, u % 2, N8, :], q[:, tt, :], ALU.mult)
                            dve.tensor_tensor(qd[:, u % 2, :, :], e[:, u % 2, 1:N8, :], q[:, tt, :].unsqueeze(1).broadcast_to([P, NLV, P]),
                                              ALU.mult).then_inc(s["qk_q"], 1)
                        if u >= 1:
                            probs(u - 1)
                    dve.wait_ge(s["qk_q"], i * NU + NU)
                    dve.wait_ge(s["qk_k"], i * NU + NU)
                    for d in range(2):
                        l0, l1 = order(d, 0)
                        c0, c1 = order(d, 1)
                        dve.tensor_scalar(kx[:, d, :], ke[:, d * TILES + c0, :], tot[:, d * TILES + c1:d * TILES + c1 + 1], None, ALU.mult)
                        dve.tensor_scalar(qx[:, d, :], qs[:, d * TILES + l1, :], tot[:, d * TILES + l0:d * TILES + l0 + 1], None,
                                          ALU.mult).then_inc(s["x_ready"], 1)
                    dve.wait_ge(s["std_done"], i + 1)
                    dve.reciprocal(r[:, :], std[:, :]).then_inc(s["r_step"], 1)
                    dve.wait_ge(s["r_step"], i + 1)
                    for tt in range(TILES):
                        last = dve.scalar_tensor_tensor(y[:, tt, :], k.ps[:, O, tt * P:(tt + 1) * P], r[:, tt:tt + 1], sg[:, tt, :],
                                                        ALU.mult, ALU.mult)
                    last.then_inc(s["y_ready"], 1)


def load_out(nc, k, dst, src):
    with phase(nc, ["out_w"]) as (block, s):
        @block.sync
        def _(sp):
            sp.dma_start(dst[:, :, :], src.rearrange("(f p) n -> p f n", p=P)).then_inc(s["out_w"], 16)
            sp.wait_ge(s["out_w"], 16)


def second_block(nc, k, w):
    with ExitStack() as ctx:
        def sb(stack, name, shape):
            return stack.enter_context(nc.sbuf_tensor(f"{name}_{nc.next_id()}", shape, F32))
        b = Buffers()
        b.h_T = sb(ctx, "h_T", [P, FT, S + CTX])
        b.y_T = sb(ctx, "y_T", [P, FT, S + CTX])
        b.mod = k.mod
        b.bias = sb(ctx, "na_bias", [P, CH, 6, GW])
        bias_phase(nc, k, b, w)

        def ffn(l, st):
            prenorm_phase(nc, k, b, l, True, [st])
            up = w["ffn_w_up_2"][l].rearrange("(f p) (a i n) -> a i p f n", p=P, a=2, n=P)
            conv = Conv(
                tap=lambda n, i, a: k.par[:, ds(i + (conv_col(l, n) + a * NF), 1)],
                bias=lambda i, a: k.par[:, ds(i + (PAR["conv_b"] + l * CT + a * NF), 1)])
            ffn_phase(nc, k, up[0], up[1], w["ffn_w_down_2"][l].rearrange("(i p) n -> i p n", p=P),
                      lambda f: b.h_T[:, f, st * S:(st + 1) * S], conv=conv,
                      post=(lambda f: b.mod[:, l, 5 * FT + f, st:st + 1], st * S))

        def project_out(l, src, streams):
            with ExitStack() as inner:
                wo = sb(inner, "w_out2", [P, FT, D])
                load_out(nc, k, wo, src)
                for st in streams:
                    chunks = [(lambda tt, f=f: b.y_T[:, f, st * S + tt * P:st * S + (tt + 1) * P], wo[:, f, :]) for f in range(FT)]
                    out_phase(nc, k, chunks, post=(lambda f: b.mod[:, l, 2 * FT + f, st:st + 1], st * S))

        prenorm_phase(nc, k, b, 0, False, [0, 1])
        with ExitStack() as inner:
            m = Buffers()
            m.qk = sb(inner, "gqa_qk", [P, 2 * TT, (GQ + GKV) * HD2])
            m.v = sb(inner, "gqa_v", [P, 2 * TT, GKV * HD2])
            m.k_T = sb(inner, "gqa_k_T", [P, GKV, S + CTX])
            gqa_project(nc, k, b, m, w)
            gqa_attend(nc, k, b, m, w)
        hgrn_phase(nc, k, b, w)
        project_out(0, w["even_w_out_2"][0], [0, 1])
        ffn(0, 0)
        ffn(0, 1)
        prenorm_phase(nc, k, b, 1, False, [0, 1])
        odd_attend(nc, k, b, w)
        project_out(1, w["odd_w_out_2"][0], [0])
        ffn(1, 0)


def build(nc, w, out):
    with ExitStack() as ctx:
        def sb(name, shape):
            return ctx.enter_context(nc.sbuf_tensor(f"{name}_{nc.next_id()}", shape, F32))
        k = Buffers()
        k.ps = ctx.enter_context(nc.psum_tensor("ps", [P, 8, BANK], F32))
        k.c_silu = sb("c_silu", [P, FT, 2])
        k.mod = sb("mod", [P, DEPTH, 6 * FT, 2])
        k.x_T = sb("x_T", [P, FT, S + CTX])
        k.ident = sb("ident", [P, P])
        k.alpha = sb("alpha", [P, P])
        k.mean = sb("mean", [P, P])
        k.par = sb("par", [P, PAR_TILES * P])
        k.eps = sb("eps", [P, 3])
        k.zero = sb("zero", [P, P])
        k.one_row = sb("one_row", [1, P])
        k.b_gate = sb("b_gate_b", [1, 3 * NH])
        k.causal = sb("causal", [P, P])
        k.cmp_mask = sb("cmp_mask", [P, TT, NC])
        k.any_cmp = sb("any_cmp", [P, TT])
        k.col = lambda name, i: k.par[:, ds(i + PAR[name], 1)]
        params_phase(nc, k, w)

        def hidden_tiles(name):
            return w[name].rearrange("l (f p) (i n) -> l i p f n", p=P, n=P)

        def down_tiles(name):
            return w[name].rearrange("l (i p) n -> l i p n", p=P)

        with nc.Fori(0, DEPTH) as l:
            for n in (1, 2):
                cols = w["w_mod_2"][n - 1].rearrange("(f p) (c n) -> c p f n", p=P, n=3 * P)
                mod = (lambda j: cols[l * 8 + j],
                       lambda j: k.mod[:, n - 1, ds(l * 24 + j * 3, 3), :],
                       lambda j: k.par[:, ds(l * 24 + j * 3 + (PAR["b_mod"] + (n - 1) * 48), 3)].unsqueeze(2).broadcast_to([P, 3, 2]))
                ffn_phase(nc, k, hidden_tiles(f"ffn{n}_w_gate")[l], hidden_tiles(f"ffn{n}_w_up")[l], down_tiles(f"ffn{n}_w_down")[l],
                          lambda f: k.x_T[:, f, 0:S], ln=(lambda f, v=2 * n - 1: k.col(f"ln{v}_g", l * FT + f),
                                                          lambda f, v=2 * n - 1: k.col(f"ln{v}_b", l * FT + f)), mod=mod)
                if n == 1:
                    mixer1(nc, k, w, l)
        second_block(nc, k, w)
        store_phase(nc, k, out)


def store_phase(nc, k, out):
    with ExitStack() as ctx:
        rows = ctx.enter_context(nc.sbuf_tensor("out_rows", [P, TT, D], F32))
        with phase(nc, ["turned", "ready", "stored"]) as (block, s):

            @block.tensor
            def _(pe):
                for tt in range(TT):
                    for f in range(FT):
                        last = pe.transpose(k.ps[:, 2 * tt + f // 4, f % 4 * P:(f % 4 + 1) * P], k.x_T[:, f, tt * P:(tt + 1) * P],
                                            k.ident[:, :])
                    last.then_inc(s["turned"], 1)

            @block.vector
            def _(dve):
                for tt in range(TT):
                    dve.wait_ge(s["turned"], tt + 1)
                    dve.tensor_copy(rows[:, tt, :], k.ps[:, 2 * tt:2 * tt + 2, :].rearrange("p b n -> p (b n)")).then_inc(s["ready"], 1)

            @block.sync
            def _(sp):
                for tt in range(TT):
                    sp.wait_ge(s["ready"], tt + 1)
                    sp.dma_start(out[0, tt * P:(tt + 1) * P, :], rows[:, tt, :]).then_inc(s["stored"], 16)
                sp.wait_ge(s["stored"], 16 * TT)


_INS = ['x', 'ln1_g', 'ln1_b', 'ffn1_w_gate', 'ffn1_w_up', 'ffn1_w_down', 'w_in', 'b_gate', 'pool_w', 'pool_scale',
        'cmp_pos_k', 'cmp_k_w1', 'cmp_k_w2', 'cmp_pos_v', 'cmp_v_w1', 'cmp_v_w2', 'w_out', 'ln2_g', 'ln2_b',
        'ffn2_w_gate', 'ffn2_w_up', 'ffn2_w_down', 'ln3_g', 'ln3_b', 'c_2', 'ctx_2', 'c_ctx_2', 'w_mod_2', 'b_mod_2',
        'norm_pre_mix_2', 'norm_post_mix_2', 'norm_pre_ffn_2', 'norm_post_ffn_2', 'even_w_in_2', 'even_w_out_2',
        'even_q_norm_2', 'even_k_norm_2', 'hgrn_out_norm_2', 'odd_w_qkv_2', 'odd_w_out_2', 'odd_rpb_2', 'ffn_w_up_2',
        'ffn_conv_w_2', 'ffn_conv_b_2', 'ffn_w_down_2']


def kernel(**inputs):
    import concourse.bacc as _bacc
    from concourse.bass_utils import run_bass_kernel_spmd as _run

    nc = _bacc.Bacc("TRN2", target_bir_lowering=False, num_devices=1)
    arrays, w = {}, {}
    host = {name: np.ascontiguousarray(inputs[name]) for name in _INS}
    host.update(shape_constants())
    for name, a in host.items():
        arrays[f"in_{name}"] = a
        w[name] = nc.dram_tensor(f"in_{name}", a.shape, mybir.dt.from_np(a.dtype), kind="ExternalInput").ap()
    out = nc.dram_tensor("out", (1, S, D), F32, kind="ExternalOutput").ap()
    build(nc, w, out)
    r = _run(nc, [arrays], core_ids=[0])
    return r.results[0]["out"]
```

```python
from contextlib import ExitStack, contextmanager

import numpy as np

import concourse.bass as bass
from concourse import mybir

class Buffers:
    pass


class Unit:

    def __init__(self, q, key, n, bias, v, out):
        self.q, self.key, self.n, self.bias, self.v, self.out = q, key, n, bias, v, out


class Conv:

    def __init__(self, tap, bias):
        self.tap, self.bias = tap, bias


F32 = mybir.dt.float32
F32R = mybir.dt.float32r
ALU = mybir.AluOpType
ACT = mybir.ActivationFunctionType
AX = mybir.AxisListType
ds = bass.ds

P = 128
D = 1024
FT = D // P
S = 256
CTX = 256
TT = S // P
DEPTH = 2
D_FF = 2816
NF = D_FF // P
BANK = 512

ALPHA = (2.0 * DEPTH) ** 0.25
LN_EPS = 1e-5
RMS_EPS = 1e-6
NEG = -1e30

POOL_WINDOWS = (2, 4, 8, 16)
POOL_C = 64
HD = 96
NH = 8
NG = 2
HPG = NH // NG
KVW = NG * HD
STRIDE = 16
CBLK = 32
NC = S // STRIDE - 1
U0, Q0 = 0, 256
KC0, VC0, KS0, VS0, KW0, VW0, G0 = (1024 + i * KVW for i in range(7))
D_IN = G0 + 3 * NH

HD2 = 64
GQ, GKV = 8, 2
BH = 4
HGRN_SCALE = 128 ** -0.5
BQ0 = GQ * HD2 + 2 * GKV * HD2
LEVELS = (1, 2, 4, 8, 16, 32, 64)
NLV = len(LEVELS)
CUM = (NLV + 2) * P
NSC = (NLV + 1) * P
GW = 64
NROW = S // GW
CH = 16
NAC = 16
DY = 15
DX = 31
CONV = 3
CT = 2 * NF

PAR = dict(ln1_g=0, ln1_b=16, ln2_g=32, ln2_b=48, ln3_g=64, ln3_b=80, pre_mix=96, post_mix=112,
           pre_ffn=128, post_ffn=144, b_mod=160, conv_w=256, conv_b=640, pool_scale=768, c=772, c_ctx=780)
PAR_TILES = 7


def conv_col(l, j):
    row = (l * CONV + j) * CT
    return PAR["conv_w"] + row // 88 * P + row % 88


def shape_constants():
    c = {}
    eye = np.eye(P, dtype=np.float32)
    c["c_ident"] = eye
    c["c_alpha"] = (np.float32(ALPHA) * eye).astype(np.float32)
    i = np.arange(P)
    c["c_causal"] = np.where(i[None, :] <= i[:, None], 0.0, NEG).astype(np.float32)
    t = np.arange(S)
    ends = np.arange(NC) * STRIDE + CBLK - 1
    cm = np.where(ends[None, :] <= t[:, None], 0.0, NEG).astype(np.float32)
    c["c_cmp"] = cm.reshape(TT, P, NC).transpose(1, 0, 2).copy()
    c["c_any"] = (t >= ends[0]).astype(np.float32).reshape(TT, P).T.copy()
    band = np.zeros((S, len(POOL_WINDOWS), S), np.float32)
    for g, w in enumerate(POOL_WINDOWS):
        for tt in range(S):
            band[max(tt + 1 - w, 0):tt + 1, g, tt] = 1.0 / min(tt + 1, w)
        band[t, g, t] -= 1.0
    c["c_band"] = band.reshape(TT, P, len(POOL_WINDOWS), S).transpose(1, 0, 2, 3).copy()
    nf = HD2 // 4
    inv = 10000.0 ** (-np.arange(nf, dtype=np.float32) / np.float32(nf))
    ang = np.concatenate([(t // GW)[:, None] * inv, (t % GW)[:, None] * inv], axis=1).astype(np.float32)
    for name, f in (("c_cos", np.cos), ("c_sin", np.sin)):
        c[name] = f(ang).astype(np.float32).reshape(TT, P, 2 * nf).transpose(1, 0, 2).copy()
    u, tc = i[:, None], i[None, :]
    cum = np.zeros((2, P, NLV + 2, P), np.float32)
    msk = np.zeros((2, P, NLV + 1, P), np.float32)
    for n, h in enumerate(LEVELS):
        mid = tc // (2 * h) * 2 * h + h
        late = tc % (2 * h) >= h
        cum[0, :, n + 1] = np.where(late, (u >= mid) & (u <= tc), (u > tc) & (u < mid))
        cum[1, :, n + 1] = np.where(late, (u >= mid) & (u < tc), (u >= tc) & (u < mid))
        same = u // (2 * h) == tc // (2 * h)
        msk[0, :, n] = same & (u % (2 * h) < h) & late
        msk[1, :, n] = same & (u % (2 * h) >= h) & ~late
    cum[0, :, 0], cum[0, :, NLV + 1] = u > tc, u <= tc
    cum[1, :, 0], cum[1, :, NLV + 1] = u < tc, u >= tc
    msk[:, :, NLV] = eye
    c["c_cum"] = cum.transpose(1, 0, 2, 3).reshape(P, 2, CUM).copy()
    c["c_lvl"] = msk.transpose(1, 0, 2, 3).reshape(P, 2, NSC).copy()
    start = np.clip(np.arange(GW) - NAC // 2, 0, GW - NAC)
    pick = np.zeros((2, 32, GW, 2, GW), np.float32)
    for q in range(GW):
        for k in range(GW):
            x = k - q + NAC - 1 if start[q] <= k < start[q] + NAC else DX
            for r in range(2):
                pick[r, x, k, r, q] = 1.0
    c["c_pick"] = pick.reshape(2 * 32, GW, P).copy()
    return c


@contextmanager
def phase(nc, names):
    with ExitStack() as ctx:
        handles = [ctx.enter_context(nc.semaphore(f"{n}_{nc.next_id()}")) for n in names]
        s = dict(zip(names, handles))
        with nc.Block() as block:
            yield block, s
        for h in handles:
            nc.gpsimd.sem_clear(h)
        nc.all_engine_barrier()


class Chain:

    def __init__(self, eng, sem, base=0):
        self.eng, self.sem, self.base, self.n = eng, sem, base, 0

    def link(self, ins):
        self.n += 1
        ins.then_inc(self.sem, 1)
        self.eng.wait_ge(self.sem, self.base + self.n)


def load_ahead(sp, s, ahead):
    for dst, src in ahead:
        sp.dma_start(dst, src).then_inc(s["ahead_in"], 16)
    if ahead:
        sp.wait_ge(s["ahead_in"], 16 * len(ahead))




def params_phase(nc, k, w, ahead):
    names = ["ahead_in", "zeroed", "rows_in", "consts_in", "turned", "x_in", "x_turned", "x_used", "par_ready"]
    with ExitStack() as ctx:
        rows = ctx.enter_context(nc.sbuf_tensor("par_rows", [P, PAR_TILES, P], F32))
        x_rows = ctx.enter_context(nc.sbuf_tensor("x_rows", [P, 4, D], F32))
        vectors = [("ln1_g", 0, 0), ("ln1_b", 0, 16), ("ln2_g", 0, 32), ("ln2_b", 0, 48), ("ln3_g", 0, 64),
                   ("ln3_b", 0, 80), ("norm_pre_mix_2", 0, 96), ("norm_post_mix_2", 0, 112),
                   ("norm_pre_ffn_2", 1, 0), ("norm_post_ffn_2", 1, 16), ("b_mod_2", 1, 32),
                   ("ffn_conv_b_2", 5, 0), ("pool_scale", 6, 0), ("c_2", 6, 4), ("c_ctx_2", 6, 12)]
        consts = [(k.ident[:, :], w["c_ident"]), (k.alpha[:, :], w["c_alpha"]), (k.causal[:, :], w["c_causal"]),
                  (k.cmp_mask[:, :, :], w["c_cmp"]), (k.any_cmp[:, :], w["c_any"])]
        n_rows = len(vectors) + CONV
        with phase(nc, names) as (block, s):

            @block.sync
            def _(sp):
                for dst, src in consts:
                    sp.dma_start(dst, src).then_inc(s["consts_in"], 16)
                for tt in range(TT):
                    sp.dma_start(x_rows[:, tt, :], w["x"][0, tt * P:(tt + 1) * P, :]).then_inc(s["x_in"], 16)
                    sp.dma_start(x_rows[:, TT + tt, :], w["ctx_2"][0, tt * P:(tt + 1) * P, :]).then_inc(s["x_in"], 16)
                load_ahead(sp, s, ahead)

            @block.gpsimd
            def _(pool):
                pool.memset(rows[:, :, :], 0.0).then_inc(s["zeroed"], 1)
                pool.memset(k.eps[:, 0:1], LN_EPS)
                pool.memset(k.eps[:, 1:2], RMS_EPS)
                pool.memset(k.eps[:, 2:3], 1.0)
                pool.memset(k.zero[:, :], 0.0)
                pool.memset(k.ones[:, :], 1.0)
                pool.memset(k.one_row[:, :], 1.0)

            @block.tensor
            def _(pe):
                pe.wait_ge(s["consts_in"], 16 * len(consts))
                pe.wait_ge(s["x_in"], 16 * 2 * TT)
                for f in range(FT):
                    if f >= 4:
                        pe.wait_ge(s["x_used"], f - 3)
                    for tt in range(2 * TT):
                        last = pe.transpose(k.ps[:, f % 4, tt * P:(tt + 1) * P], x_rows[:, tt, f * P:(f + 1) * P],
                                            k.ident[:, :])
                    last.then_inc(s["x_turned"], 1)
                pe.wait_ge(s["rows_in"], 16 * n_rows)
                for n in range(PAR_TILES):
                    last = pe.transpose(k.ps[:, 4 + n // 4, n % 4 * P:(n % 4 + 1) * P], rows[:, n, :], k.ident[:, :])
                last.then_inc(s["turned"], 1)

            @block.scalar
            def _(act):
                act.wait_ge(s["zeroed"], 1)
                for name, tile, r in vectors:
                    a = w[name]
                    src = a.rearrange("(r p) -> r p", p=P) if len(a.shape) == 1 else a.rearrange("l (r p) -> (l r) p", p=P)
                    act.dma_start(rows[r:r + src.shape[0], tile, :], src).then_inc(s["rows_in"], 16)
                taps = w["ffn_conv_w_2"].rearrange("l j (r p) -> (l j r) p", p=P)
                for n in range(CONV):
                    act.dma_start(rows[0:88, 2 + n, :], taps[88 * n:88 * n + 88, :]).then_inc(s["rows_in"], 16)
                act.wait_ge(s["par_ready"], 1)
                for n, name in enumerate(("c", "c_ctx")):
                    act.activation(k.c_silu[:, :, n], k.par[:, PAR[name]:PAR[name] + FT], ACT.Silu)

            @block.vector
            def _(dve):
                for f in range(FT):
                    dve.wait_ge(s["x_turned"], f + 1)
                    dve.tensor_copy(k.x_T[:, f, :], k.ps[:, f % 4, :]).then_inc(s["x_used"], 1)
                dve.wait_ge(s["turned"], 1)
                dve.tensor_copy(k.par[:, 0:512], k.ps[:, 4, :])
                dve.tensor_copy(k.par[:, 512:PAR_TILES * P], k.ps[:, 5, 0:(PAR_TILES - 4) * P]).then_inc(s["par_ready"], 1)


LN_SEMS = ["tile_done", "ln_stats", "ln_mv", "ln_std", "ln_rstd", "ln_shift", "z0_ready", "z1_ready", "ln_turned"]


def ln_vector(dve, k, s, t, par_g, par_b):
    for tt in range(TT):
        dve.wait_ge(s["tile_done"], tt + 1)
        for n in range(2):
            dve.bn_stats(t.stats[:, tt, n, :], k.ps[:, 2 * tt + n, :]).then_inc(s["ln_stats"], 1)
        dve.wait_ge(s["ln_stats"], 2 * tt + 2)
        dve.bn_aggr(t.mv[:, tt, :], t.stats[:, tt, :, :]).then_inc(s["ln_mv"], 1)
        dve.wait_ge(s["ln_std"], tt + 1)
        dve.reciprocal(t.rstd[:, tt:tt + 1], t.std[:, tt:tt + 1]).then_inc(s["ln_rstd"], 1)
        dve.wait_ge(s["ln_rstd"], tt + 1)
        dve.scalar_tensor_tensor(t.shift[:, tt:tt + 1], t.mv[:, tt, 0:1], -1.0, t.rstd[:, tt:tt + 1], ALU.mult, ALU.mult).then_inc(s["ln_shift"], 1)
        dve.tensor_scalar(t.z[:, tt, 0:BANK], k.ps[:, 2 * tt, :], t.mv[:, tt, 0:1], t.rstd[:, tt:tt + 1], ALU.subtract,
                          ALU.mult).then_inc(s["z0_ready"], 1)
    for f in (2, 3, 6, 7):
        dve.wait_ge(s["ln_turned"], f // 2 + 1)
        dve.tensor_scalar(k.x_T[:, f, 0:S], turned(k, f), par_g(f), par_b(f), ALU.mult, ALU.add)


def ln_scalar(act, k, s, t, par_g, par_b):
    for tt in range(TT):
        act.wait_ge(s["ln_mv"], tt + 1)
        act.activation(t.std[:, tt:tt + 1], t.mv[:, tt, 1:2], ACT.Sqrt, bias=k.eps[:, 0:1]).then_inc(s["ln_std"], 1)
        act.wait_ge(s["ln_shift"], tt + 1)
        act.activation(t.z[:, tt, BANK:D], k.ps[:, 2 * tt + 1, :], ACT.Identity, bias=t.shift[:, tt:tt + 1],
                       scale=t.rstd[:, tt:tt + 1]).then_inc(s["z1_ready"], 1)
    for f in (0, 1, 4, 5):
        act.wait_ge(s["ln_turned"], f // 2 + 1)
        act.activation(k.x_T[:, f, 0:S], turned(k, f), ACT.Identity, bias=par_b(f), scale=par_g(f))


def turned(k, f, bank=4):
    return k.ps[:, bank + f // 2, f % 2 * S:(f % 2 + 1) * S]


def turn_tensor(pe, k, s, z, sem, st=0, bank=4):
    for tt in range(TT):
        for f in range(FT):
            if f % 4 == 0:
                pe.wait_ge(s["z0_ready" if f == 0 else "z1_ready"], st * TT + tt + 1)
            last = pe.transpose(turned(k, f, bank)[:, tt * P:(tt + 1) * P], z[:, tt, f * P:(f + 1) * P], k.ident[:, :])
            if tt == TT - 1 and f % 2:
                last.then_inc(sem, 1)


def ln_buffers(nc, ctx):
    def sb(name, shape):
        return ctx.enter_context(nc.sbuf_tensor(f"{name}_{nc.next_id()}", shape, F32))
    got = Buffers()
    got.stats = sb("ln_stats_b", [P, TT, 2, 6])
    got.mv = sb("ln_mv_b", [P, TT, 2])
    got.std = sb("ln_std_b", [P, TT])
    got.rstd = sb("ln_rstd_b", [P, TT])
    got.shift = sb("ln_shift_b", [P, TT])
    got.z = sb("ln_z_b", [P, TT, D])
    return got


POST_SEMS = ["tile_done", "po_sq", "po_std", "po_r", "z0_ready", "z1_ready", "po_turned"]


def post_scalar(act, k, s, t, st=0):
    if st == 0:
        act.activation(t.shift[:, 0:1], k.eps[:, 1:2], ACT.Sqrt)
    for tt in range(TT):
        made, at = st * TT + tt + 1, 4 * st + 2 * tt
        act.wait_ge(s["tile_done"], made)
        act.activation(t.z[:, tt, :], k.ps[:, at:at + 2, :].rearrange("p b n -> p (b n)"), ACT.Square,
                       accum_out=t.mv[:, tt, 0:1]).then_inc(s["po_sq"], 1)
        act.wait_ge(s["po_sq"], made)
        act.activation(t.std[:, tt:tt + 1], t.mv[:, tt, 0:1], ACT.Sqrt, bias=k.eps[:, 1:2], scale=1.0 / D).then_inc(s["po_std"], 1)
        act.wait_ge(s["po_r"], made)
        act.activation(t.z[:, tt, BANK:D], k.ps[:, at + 1, :], ACT.Copy, scale=t.rstd[:, tt:tt + 1]).then_inc(s["z1_ready"], 1)


def post_scale(dve, k, s, t, st=0):
    for tt in range(TT):
        made, at = st * TT + tt + 1, 4 * st + 2 * tt
        dve.wait_ge(s["po_std"], made)
        dve.reciprocal(t.rstd[:, tt:tt + 1], t.std[:, tt:tt + 1]).then_inc(s["po_r"], 1)
        dve.wait_ge(s["po_r"], made)
        dve.tensor_scalar(t.z[:, tt, 0:BANK], k.ps[:, at, :], t.rstd[:, tt:tt + 1], None, ALU.mult).then_inc(s["z0_ready"], 1)


def post_add(dve, k, s, gain, cols, st=0, bank=4):
    for f in range(FT):
        dve.wait_ge(s["po_turned"], st * (FT // 2) + f // 2 + 1)
        dve.scalar_tensor_tensor(k.x_T[:, f, cols:cols + S], turned(k, f, bank), gain(f), k.x_T[:, f, cols:cols + S],
                                 ALU.mult, ALU.add)


def post_vector(dve, k, s, t, gain, cols, st=0, bank=4):
    post_scale(dve, k, s, t, st)
    post_add(dve, k, s, gain, cols, st, bank)


def first_tiles(nc, ctx):
    got = Buffers()
    got.gu = [ctx.enter_context(nc.sbuf_tensor(f"w_gu{n}_{nc.next_id()}", [P, 2, FT, P], F32)) for n in range(2)]
    got.dn = [ctx.enter_context(nc.sbuf_tensor(f"w_dn{n}_{nc.next_id()}", [P, D], F32)) for n in range(2)]
    return got


def first_loads(tiles, w_gate, w_up, w_down):
    got = []
    for n in range(2):
        got += [(tiles.gu[n][:, 0, :, :], w_gate[n]), (tiles.gu[n][:, 1, :, :], w_up[n]), (tiles.dn[n][:, :], w_down[n])]
    return got


def ffn_phase(nc, k, w_gate, w_up, w_down, src, ln=None, conv=None, post=None, mod=None, loaded=None, ahead=(), reloads=False):
    names = ["gu0_in", "gu1_in", "dn0_in", "dn1_in", "x_hi", "x_lo", "w_hi", "gate0_split", "gu_split", "dn_split", "gu_done", "mid_ready",
             "mid_step", "act_done", "h_full", "h_hi", "h_ready", "down_done", "ahead_in", "wm0_in", "wm1_in", "acc_step", "prod_step", "mod_done", "mod_used"]
    names += LN_SEMS if ln else POST_SEMS
    LAST = NF - 1
    TURNS = (NF - 6) // 2
    MT = 3
    with ExitStack() as ctx:
        def sb(name, shape, dt=F32):
            return ctx.enter_context(nc.sbuf_tensor(f"{name}_{nc.next_id()}", shape, dt))
        x_hi, x_lo = sb("x_hi", [P, FT, S], F32R), sb("x_lo", [P, FT, S], F32R)
        tiles_in = loaded or first_tiles(nc, ctx)
        wgu, wdn = tiles_in.gu, tiles_in.dn
        gu_hi = [sb(f"gu_hi{n}", [P, 2, FT, P], F32R) for n in range(2)]
        gu_lo = [sb(f"gu_lo{n}", [P, 2, FT, P], F32R) for n in range(2)]
        dn_hi = [sb(f"dn_hi{n}", [P, D], F32R) for n in range(2)]
        dn_lo = [sb(f"dn_lo{n}", [P, D], F32R) for n in range(2)]
        sil = [sb(f"silu{n}", [P, S]) for n in range(2)]
        hid = [sb(f"hid{n}", [P, S]) for n in range(2)]
        h_hi = [sb(f"h_hi{n}", [P, S], F32R) for n in range(2)]
        h_lo = [sb(f"h_lo{n}", [P, S], F32R) for n in range(2)]
        cv = [sb(f"conv{n}", [P, 2, S]) for n in range(2)] if conv else None
        wm = sb("w_mod", [P, FT, MT * P]) if mod else None
        acc = sb("mod_acc", [P, MT * P]) if mod else None
        prod = sb("mod_prod", [P, FT, MT * P]) if mod else None
        t_ln = ln_buffers(nc, ctx)
        with phase(nc, names) as (block, s):
            gu_in, dn_in = [s["gu0_in"], s["gu1_in"]], [s["dn0_in"], s["dn1_in"]]

            def gu(n):
                return k.ps[:, 4 + n, :].rearrange("p (a t) -> p a t", a=2)

            def tiles(eng, step):
                for t in range(4):
                    step(t, t % 2, t)
                with eng.Fori(0, TURNS - 1) as j:
                    for n in range(2):
                        step(j * 2 + (4 + n), n, None)
                    step(j, None, "turn")
                for t in range(NF - 4, NF):
                    step(t, t % 2, t)
                    if t == NF - 3:
                        step(TURNS - 1, None, "turn")

            @block.sync
            def _(sp):
                def load_gu(i, n):
                    sp.dma_start(wgu[n][:, 0, :, :], w_gate[i]).then_inc(gu_in[n], 16)
                    sp.dma_start(wgu[n][:, 1, :, :], w_up[i]).then_inc(gu_in[n], 16)

                def load_dn(i, n):
                    sp.dma_start(wdn[n][:, :], w_down[i]).then_inc(dn_in[n], 16)

                for n in range(2):
                    if loaded:
                        sp.sem_inc(gu_in[n], 32)
                        sp.sem_inc(dn_in[n], 16)
                    else:
                        load_gu(n, n)
                        load_dn(n, n)
                with sp.Fori(0, NF // 2 - 1) as j:
                    for n in range(2):
                        sp.wait_ge(s["gu_split"], j * 2 + n + 1)
                        load_gu(j * 2 + (n + 2), n)
                        sp.wait_ge(s["dn_split"], j * 2 + n + 1)
                        load_dn(j * 2 + (n + 2), n)
                if reloads:
                    sp.wait_ge(s["gu_split"], NF)
                    sp.wait_ge(s["dn_split"], NF)
                load_ahead(sp, s, ahead)

            @block.tensor
            def _(pe):
                def gate_up(t, n):
                    pe.wait_ge(s["gu_split"], t + 1)
                    for a in range(2):
                        for f in range(FT):
                            for p, (wt, x) in enumerate(((gu_hi, x_hi), (gu_hi, x_lo), (gu_lo, x_hi))):
                                last = pe.matmul(gu(n)[:, a, :], wt[n][:, a, f, :], x[:, f, :], start=(f == 0 and p == 0),
                                                 stop=(f == FT - 1 and p == 2), skip_group_check=True)
                    last.then_inc(s["gu_done"], 1)

                def first_gate_up():
                    for p, (wt, x) in enumerate(((gu_hi, x_hi), (gu_lo, x_hi), (gu_hi, x_lo))):
                        for a in range(2):
                            if p == 0:
                                pe.wait_ge(s["w_hi"], a + 1)
                            if p == 1:
                                pe.wait_ge(s["gate0_split"] if a == 0 else s["gu_split"], 1)
                            for f in range(FT):
                                if a == 0 and p != 1:
                                    pe.wait_ge(s["x_hi"] if p == 0 else s["x_lo"], f + 1)
                                last = pe.matmul(gu(0)[:, a, :], wt[0][:, a, f, :], x[:, f, :], start=(p == 0 and a == 0 and f == 0),
                                                 stop=(f == FT - 1 and p == 2), skip_group_check=True)
                    last.then_inc(s["gu_done"], 1)

                def down(t, n, first=False, end=False):
                    pe.wait_ge(s["dn_split"], t + 1)
                    pe.wait_ge(s["h_ready"], t + 1)
                    for tt in range(TT):
                        for c in range(2):
                            for p, (h, wt) in enumerate(((h_hi, dn_hi), (h_hi, dn_lo), (h_lo, dn_hi))):
                                last = pe.matmul(k.ps[:, 2 * tt + c, :], h[n][:, tt * P:(tt + 1) * P], wt[n][:, c * BANK:(c + 1) * BANK],
                                                 start=(first and p == 0), stop=(end and p == 2), skip_group_check=True)
                        if end:
                            last.then_inc(s["tile_done"], 1)
                    if not end:
                        last.then_inc(s["down_done"], 1)

                def step(t, n, fixed):
                    if fixed == "turn":
                        if mod:
                            pe.wait_ge(s["acc_step"], t * FT + FT)
                            pe.wait_ge(s["prod_step"], t * 5 + 5)
                            pe.wait_ge(s["mod_used"], t + 1)
                            for m in range(MT):
                                for st in range(2):
                                    last = pe.matmul(k.ps[:, 6, 2 * m + st:2 * m + st + 1], (acc[:, m * P:(m + 1) * P], prod[:, 0, m * P:(m + 1) * P])[st], k.eps[:, 2:3],
                                                     start=True, stop=True, skip_group_check=True)
                            last.then_inc(s["mod_done"], 1)
                        return
                    if fixed is None or fixed >= 2:
                        pe.wait_ge(s["h_full"], t - 1)
                    if fixed == 0:
                        first_gate_up()
                    else:
                        gate_up(t, n)
                    if fixed is None or fixed >= 1:
                        down(t - 1, 1 - n, first=(fixed == 1 and not ln))

                if ln:
                    for tt in range(TT):
                        for f in range(FT):
                            pe.matmul(k.ps[:, 2 * tt + f // 4, f % 4 * P:(f % 4 + 1) * P], k.x_T[:, f, tt * P:(tt + 1) * P],
                                      k.alpha[:, :], start=(f % 4 == 0), stop=False, skip_group_check=True)
                tiles(pe, step)
                down(LAST, LAST % 2, end=True)
                turn_tensor(pe, k, s, t_ln.z, s["ln_turned"] if ln else s["po_turned"])

            @block.scalar
            def _(act):
                def hi_gu(t, n, a, fixed):
                    if a == 0:
                        act.wait_ge(gu_in[n], 16 * (fixed - n) + 32 if fixed is not None else (t - n) * 16 + 32)
                    act.activation(gu_hi[n][:, a, :, :], wgu[n][:, a, :, :], ACT.Copy).then_inc(s["w_hi"], 1)

                def hi_dn(t, n, fixed):
                    act.wait_ge(dn_in[n], 8 * (fixed - n) + 16 if fixed is not None else (t - n) * 8 + 16)
                    act.activation(dn_hi[n][:, :], wdn[n][:, :], ACT.Copy).then_inc(s["w_hi"], 1)

                def step(t, n, fixed):
                    if fixed == "turn":
                        return
                    more_gu = fixed is None or fixed + 2 <= LAST
                    more_dn = fixed is None or 1 <= fixed < LAST
                    act.wait_ge(s["gu_done"], t + 1)
                    if conv is None:
                        act.activation(sil[n][:, :], gu(n)[:, 0, :], ACT.Silu).then_inc(s["act_done"], 1)
                    else:
                        for a in range(2):
                            act.activation(cv[n][:, a, :], gu(n)[:, a, :], ACT.Identity, bias=conv.bias(t, a),
                                           scale=conv.tap(1, t, a)).then_inc(s["mid_ready"], 1)
                    if mod and ((fixed is None and n == 1) or fixed == 3):
                        if fixed is None:
                            act.wait_ge(s["acc_step"], (t - 3) * (FT // 2))
                            act.wait_ge(s["prod_step"], (t - 5) // 2 * 5 + 2)
                        load_mod(1, (t - 3) // 2)
                    if more_gu:
                        hi_gu(t + 2, n, 0, None if fixed is None else fixed + 2)
                    if conv is not None:
                        act.wait_ge(s["mid_step"], t * 4 + 4)
                        act.activation(sil[n][:, :], cv[n][:, 1, :], ACT.Silu).then_inc(s["act_done"], 1)
                    if more_gu:
                        hi_gu(t + 2, n, 1, None if fixed is None else fixed + 2)
                    act.wait_ge(s["h_full"], t + 1)
                    act.activation(h_hi[n][:, :], hid[n][:, :], ACT.Copy).then_inc(s["h_hi"], 1)
                    if more_dn:
                        act.wait_ge(s["down_done"], t)
                        hi_dn(t + 1, 1 - n, None if fixed is None else fixed + 1)
                    if mod and fixed is None and n == 0:
                        act.wait_ge(s["acc_step"], (t - 3) * (FT // 2))
                        act.wait_ge(s["prod_step"], (t - 4) // 2 * 5 + 1)
                        load_mod(0, (t - 4) // 2 + 1)

                def load_mod(half, j):
                    f0 = half * (FT // 2)
                    act.dma_start(wm[:, f0:f0 + FT // 2, :], mod[0](j)[:, f0:f0 + FT // 2, :]).then_inc(s[f"wm{half}_in"], 16)

                if mod:
                    load_mod(0, 0)
                for n in range(2):
                    hi_gu(n, n, 0, n)
                    hi_gu(n, n, 1, n)
                for n in range(2):
                    hi_dn(n, n, n)
                tiles(act, step)
                if ln:
                    ln_scalar(act, k, s, t_ln, *ln)
                else:
                    post_scalar(act, k, s, t_ln)

            @block.gpsimd
            def _(pool):
                H = FT // 2

                def turn(j):
                    pool.wait_ge(s["mod_used"], j + 1)
                    for n in range(2):
                        pool.wait_ge(s[f"wm{n}_in"], j * 16 + 16)
                        half = slice(n * H, (n + 1) * H)
                        pool.tensor_tensor(prod[:, half, :], wm[:, half, :], k.c_silu[:, half, 1:2].broadcast_to([P, H, MT * P]),
                                           ALU.mult).then_inc(s["prod_step"], 1)
                    for n, half in enumerate((4, 2, 1)):
                        pool.wait_ge(s["prod_step"], j * 5 + (2 + n))
                        pool.tensor_tensor(prod[:, 0:half, :], prod[:, 0:half, :], prod[:, half:2 * half, :], ALU.add).then_inc(s["prod_step"], 1)

                for f in range(FT):
                    pool.wait_ge(s["x_hi"], f + 1)
                    pool.tensor_tensor(x_lo[:, f, :], src(f), x_hi[:, f, :].bitcast(F32), ALU.subtract).then_inc(s["x_lo"], 1)
                if mod:
                    with pool.Fori(0, TURNS - 1) as j:
                        turn(j)
                    turn(TURNS - 1)

            @block.vector
            def _(dve):
                def lo_gu(n, a, made, first=False):
                    dve.wait_ge(s["w_hi"], made)
                    last = dve.tensor_tensor(gu_lo[n][:, a, :, :], wgu[n][:, a, :, :], gu_hi[n][:, a, :, :].bitcast(F32), ALU.subtract)
                    if a == 1:
                        last.then_inc(s["gu_split"], 1)
                    if first:
                        last.then_inc(s["gate0_split"], 1)

                def lo_dn(n, made):
                    dve.wait_ge(s["w_hi"], made)
                    dve.tensor_tensor(dn_lo[n][:, :], wdn[n][:, :], dn_hi[n][:, :].bitcast(F32), ALU.subtract).then_inc(s["dn_split"], 1)

                def step(t, n, fixed):
                    if fixed == "turn":
                        if mod:
                            dve.wait_ge(s["mod_done"], t + 1)
                            dve.tensor_tensor(mod[1](t), k.ps[:, 6, 0:2 * MT].rearrange("p (m s) -> p m s", s=2), mod[2](t),
                                              ALU.add).then_inc(s["mod_used"], 1)
                            if not (isinstance(t, int) and t == TURNS - 1):
                                latent_mod(t * 2 + 5, 0)
                        return
                    more_gu = fixed is None or fixed + 2 <= LAST
                    more_dn = fixed is None or 1 <= fixed < LAST
                    made = 6 if fixed == 0 else t * 3 + 5
                    if conv is not None:
                        dve.wait_ge(s["mid_ready"], t * 2 + 2)
                        for a in range(2):
                            dve.scalar_tensor_tensor(cv[n][:, a, 1:S], gu(n)[:, a, 0:S - 1], conv.tap(0, t, a),
                                                     cv[n][:, a, 1:S], ALU.mult, ALU.add).then_inc(s["mid_step"], 1)
                        for a in range(2):
                            dve.wait_ge(s["mid_step"], t * 4 + (a + 1))
                            dve.scalar_tensor_tensor(cv[n][:, a, 0:S - 1], gu(n)[:, a, 1:S], conv.tap(2, t, a),
                                                     cv[n][:, a, 0:S - 1], ALU.mult, ALU.add).then_inc(s["mid_step"], 1)
                    else:
                        dve.wait_ge(s["act_done"], t + 1)
                        dve.scalar_tensor_tensor(hid[n][:, :], sil[n][:, :], 0.5, gu(n)[:, 1, :], ALU.mult, ALU.mult).then_inc(s["h_full"], 1)
                    if more_gu:
                        lo_gu(n, 0, made + 1)
                    if conv is not None:
                        dve.wait_ge(s["act_done"], t + 1)
                        dve.tensor_tensor(hid[n][:, :], sil[n][:, :], cv[n][:, 0, :], ALU.mult).then_inc(s["h_full"], 1)
                    if more_gu:
                        lo_gu(n, 1, made + 2)
                    dve.wait_ge(s["h_hi"], t + 1)
                    dve.tensor_tensor(h_lo[n][:, :], hid[n][:, :], h_hi[n][:, :].bitcast(F32), ALU.subtract).then_inc(s["h_ready"], 1)
                    if more_dn:
                        lo_dn(1 - n, made + (3 if more_gu else 1))
                    if mod and (fixed == 3 or (n == 0 and (fixed is None or fixed == NF - 4))):
                        latent_mod(t, 1 - n)

                def latent_mod(t, half):
                    dve.wait_ge(s[f"wm{half}_in"], (t - 3 - half) * 8 + 16)
                    if half == 0:
                        dve.wait_ge(s["mod_used"], (t - 3) // 2 + 1)
                    for i in range(FT // 2):
                        f = half * (FT // 2) + i
                        if f == 0:
                            part = dve.tensor_scalar(acc[:, :], wm[:, f, :], k.c_silu[:, f, 0:1], None, ALU.mult)
                        else:
                            dve.wait_ge(s["acc_step"], (t - 3) * (FT // 2) + i)
                            part = dve.scalar_tensor_tensor(acc[:, :], wm[:, f, :], k.c_silu[:, f, 0:1], acc[:, :], ALU.mult, ALU.add)
                        part.then_inc(s["acc_step"], 1)

                if mod:
                    dve.sem_inc(s["mod_used"], 1)
                for f in range(FT):
                    dve.tensor_copy(x_hi[:, f, :], src(f)).then_inc(s["x_hi"], 1)
                for n in range(2):
                    lo_gu(n, 0, 2 * n + 1, first=(n == 0))
                    lo_gu(n, 1, 2 * n + 2)
                for n in range(2):
                    lo_dn(n, n + 5)
                tiles(dve, step)
                if ln:
                    ln_vector(dve, k, s, t_ln, *ln)
                else:
                    post_vector(dve, k, s, t_ln, *post)


def out_phase(nc, k, chunks, ln=None, post=None, ahead=(), stream=None, raw=None):
    names = ["w0_in", "w1_in", "w2_in", "hi_made", "lo_made", "chunk_done", "ahead_in"] + (LN_SEMS if ln else POST_SEMS)
    LAST = len(chunks) - 1
    SLOTS = 3
    with ExitStack() as ctx:
        def sb(name, shape):
            return ctx.enter_context(nc.sbuf_tensor(f"{name}_{nc.next_id()}", shape, F32R))
        w_hi, w_lo = sb("out_w_hi", [P, SLOTS, D]), sb("out_w_lo", [P, SLOTS, D])
        y_hi, y_lo = sb("out_y_hi", [P, SLOTS, S]), sb("out_y_lo", [P, SLOTS, S])
        t = ln_buffers(nc, ctx)
        if stream is not None:
            chunks = [(y, raw[:, n % SLOTS, :]) for n, y in enumerate(chunks)]
        with phase(nc, names) as (block, s):

            @block.sync
            def _(sp):
                if stream is not None:
                    for n in range(SLOTS):
                        sp.sem_inc(s[f"w{n}_in"], 16)
                    for n in range(SLOTS, len(chunks)):
                        sp.wait_ge(s["lo_made"], n - SLOTS + 1)
                        sp.dma_start(raw[:, n % SLOTS, :], stream[n]).then_inc(s[f"w{n % SLOTS}_in"], 16)
                load_ahead(sp, s, ahead)

            @block.tensor
            def _(pe):
                if ln:
                    for tt in range(TT):
                        for f in range(FT):
                            pe.matmul(k.ps[:, 2 * tt + f // 4, f % 4 * P:(f % 4 + 1) * P], k.x_T[:, f, tt * P:(tt + 1) * P],
                                      k.alpha[:, :], start=(f % 4 == 0), stop=False, skip_group_check=True)
                for n, (y, _) in enumerate(chunks):
                    rows, m = y.shape[0], n % SLOTS
                    pe.wait_ge(s["lo_made"], n + 1)
                    for tt in range(TT):
                        for c in range(2):
                            for p, (a, b) in enumerate(((y_hi, w_hi), (y_hi, w_lo), (y_lo, w_hi))):
                                last = pe.matmul(k.ps[:, 2 * tt + c, :], a[0:rows, m, tt * P:(tt + 1) * P], b[0:rows, m, c * BANK:(c + 1) * BANK],
                                                 start=(n == 0 and p == 0 and not ln), stop=(n == LAST and p == 2), skip_group_check=True)
                        if n == LAST:
                            last.then_inc(s["tile_done"], 1)
                    if n < LAST:
                        last.then_inc(s["chunk_done"], 1)
                turn_tensor(pe, k, s, t.z, s["ln_turned"] if ln else s["po_turned"])

            @block.scalar
            def _(act):
                for n, (y, moving) in enumerate(chunks):
                    rows, m = y.shape[0], n % SLOTS
                    if n >= SLOTS:
                        act.wait_ge(s["chunk_done"], n - SLOTS + 1)
                    act.activation(y_hi[0:rows, m, :], y, ACT.Copy)
                    if stream is not None:
                        act.wait_ge(s[f"w{m}_in"], n // SLOTS * 16 + 16)
                    act.activation(w_hi[0:rows, m, :], moving, ACT.Copy).then_inc(s["hi_made"], 1)
                if ln:
                    ln_scalar(act, k, s, t, *ln)
                else:
                    post_scalar(act, k, s, t)

            @block.vector
            def _(dve):
                for n, (y, moving) in enumerate(chunks):
                    rows, m = y.shape[0], n % SLOTS
                    dve.wait_ge(s["hi_made"], n + 1)
                    dve.tensor_tensor(y_lo[0:rows, m, :], y, y_hi[0:rows, m, :].bitcast(F32), ALU.subtract)
                    dve.tensor_tensor(w_lo[0:rows, m, :], moving, w_hi[0:rows, m, :].bitcast(F32), ALU.subtract).then_inc(s["lo_made"], 1)
                if ln:
                    ln_vector(dve, k, s, t, *ln)
                else:
                    post_vector(dve, k, s, t, *post)


def mixer1_columns():
    tok = [(U0, U0 + 256, 0), (VS0, VS0 + KVW, 256), (VW0, D_IN, 256 + KVW)]
    keys = [(KC0, KC0 + 2 * KVW, 0), (KS0, KS0 + KVW, 2 * KVW), (KW0, KW0 + KVW, 3 * KVW)]
    return tok, keys, [(Q0, Q0 + NH * HD, 0)]


def column_loads(dst, src, columns):
    return [(dst[:, :, at:at + c1 - c0], src[:, :, c0:c1]) for c0, c1, at in columns]


PIECES = 4 + NH // 2


def mixer1_project(nc, k, m, w, l):
    names = ["x_hi", "piece_hi", "piece_lo", "w_in", "pool_in", "cmp_in", "pos_in", "tok_done", "tok_used", "feat_done", "feat_used", "q_done", "q_used",
             "pos_turned", "pos_ready", "blocks_ready", "hid_done", "hid_ready", "cmp_done", "band_done", "band_used",
             "mix_done", "gate_ready"]
    with ExitStack() as ctx:
        def sb(name, shape, dt=F32):
            return ctx.enter_context(nc.sbuf_tensor(f"{name}_{nc.next_id()}", shape, dt))
        w_q = sb("w_in_q", [P, FT, NH * HD])
        x_hi, x_lo = sb("mix_x_hi", [P, FT, S], F32R), sb("mix_x_lo", [P, FT, S], F32R)
        w_hi, w_lo = sb("mix_w_hi", [P, 2, FT, KVW], F32R), sb("mix_w_lo", [P, 2, FT, KVW], F32R)
        spare = m.w_tok[:, :, :].rearrange("p f n -> p (f n)")
        w1 = [sb("cmp_w1_b", [HD, CBLK, HD]), spare[0:HD, 0:CBLK * HD].rearrange("d (c j) -> d c j", j=HD)]
        w2 = sb("cmp_w2_b", [HD, 2, HD])
        pos_rows = sb("pos_rows", [CBLK, 2, HD])
        pos = sb("pos_T", [HD, 2, CBLK])
        blocks = sb("cmp_blocks", [HD, 2, CBLK, NG, NC])
        hidden = sb("cmp_hidden", [HD, 2, NG, NC])
        pool_w = sb("pool_w_b", [P, 2, POOL_C])
        band = spare[:, CBLK * HD:CBLK * HD + TT * len(POOL_WINDOWS) * S].rearrange("p (a g t) -> p a g t", a=TT, t=S)
        u_tok = sb("u_tok", [P, TT, 256])
        pooled = sb("pooled", [P, 2, S])
        with phase(nc, names) as (block, s):
            def piece(i):
                return m.w_keys[:, :, i * KVW:(i + 1) * KVW] if i < 4 else w_q[:, :, (i - 4) * KVW:(i - 3) * KVW]

            def piece_used(eng, i):
                eng.wait_ge(s["feat_done"] if i < 4 else s["q_done"], i + 1 if i < 4 else i - 3)

            @block.sync
            def _(sp):
                for n, kv in enumerate("kv"):
                    sp.dma_start(pos_rows[:, n, :], w[f"cmp_pos_{kv}"][l]).then_inc(s["pos_in"], 16)
                for dst, src in column_loads(w_q, w["w_in"].rearrange("l (f p) n -> l p f n", p=P)[l], mixer1_columns()[2]):
                    sp.dma_start(dst, src).then_inc(s["w_in"], 16)
                w1_in = [w[f"cmp_{kv}_w1"].rearrange("l (c d) j -> l d c j", d=HD)[l] for kv in "kv"]
                sp.dma_start(w1[0][:, :, :], w1_in[0]).then_inc(s["cmp_in"], 16)
                for n, kv in enumerate("kv"):
                    sp.dma_start(w2[:, n, :], w[f"cmp_{kv}_w2"][l]).then_inc(s["cmp_in"], 16)
                pw = w["pool_w"].rearrange("l (a b) c d -> l b c a d", b=2)
                for b in range(2):
                    sp.dma_start(pool_w[64 * b:64 * b + 64, :, :], pw[l, b]).then_inc(s["pool_in"], 16)
                sp.wait_ge(s["tok_done"], TT)
                sp.dma_start(band, w["c_band"]).then_inc(s["pool_in"], 16)
                sp.dma_start(w1[1], w1_in[1]).then_inc(s["cmp_in"], 16)

            @block.tensor
            def _(pe):
                def project(i, a, out):
                    for f in range(FT):
                        for p, (wt, x) in enumerate(((w_hi, x_hi), (w_hi, x_lo), (w_lo, x_hi))):
                            last = pe.matmul(out, wt[:, i % 2, f, a * HD:(a + 1) * HD], x[:, f, :], start=(f == 0 and p == 0),
                                             stop=(f == FT - 1 and p == 2), skip_group_check=True)
                    return last

                pe.wait_ge(s["pos_in"], 32)
                for n in range(2):
                    last = pe.transpose(k.ps[0:HD, 7, n * CBLK:(n + 1) * CBLK], pos_rows[:, n, :], k.ident[0:CBLK, 0:CBLK])
                last.then_inc(s["pos_turned"], 1)
                for tt in range(TT):
                    for bank, col, n in ((tt, 0, 256 + KVW), (2 + tt, 256 + KVW, KVW + 3 * NH)):
                        for f in range(FT):
                            last = pe.matmul(k.ps[:, bank, 0:n], k.x_T[:, f, tt * P:(tt + 1) * P], m.w_tok[:, f, col:col + n],
                                             start=(f == 0), stop=(f == FT - 1), skip_group_check=True)
                    last = pe.matmul(k.ps[:, 2 + tt, KVW:KVW + 3 * NH], k.one_row[0:1, :], k.b_gate[0:1, :], start=False,
                                     stop=True, skip_group_check=True)
                    last.then_inc(s["tok_done"], 1)
                for n in range(4):
                    if n == 3:
                        pe.wait_ge(s["pos_ready"], 1)
                    pe.wait_ge(s["piece_lo"], n + 1)
                    for g in range(NG):
                        last = project(n, g, k.ps[0:HD, 4 + n, g * S:(g + 1) * S])
                    last.then_inc(s["feat_done"], 1)
                for n in range(NH // 2):
                    if n < 2:
                        pe.wait_ge(s["tok_used"], 4 * TT)
                    else:
                        pe.wait_ge(s["q_used"], n - 1)
                    pe.wait_ge(s["piece_lo"], n + 5)
                    for a in range(2):
                        last = project(n + 4, a, k.ps[0:HD, n % 2, a * S:(a + 1) * S])
                    last.then_inc(s["q_done"], 1)
                pe.wait_ge(s["pool_in"], 48)
                for g in range(4):
                    for tt in range(TT):
                        last = pe.matmul(k.ps[64 * (g % 2):64 * (g % 2) + 64, 2 + g // 2, 0:S], u_tok[:, tt, g * POOL_C:(g + 1) * POOL_C],
                                         band[:, tt, g, :], start=(tt == 0), stop=(tt == TT - 1), skip_group_check=True)
                last.then_inc(s["band_done"], 1)
                pe.wait_ge(s["cmp_in"], 64)
                for n in range(2):
                    pe.wait_ge(s["blocks_ready"], 4 * n + 4)
                    for c in range(CBLK):
                        last = pe.matmul(k.ps[0:HD, 4 + n, 0:NG * NC], w1[n][:, c, :], blocks[:, n, c, :, :].rearrange("d g b -> d (g b)"),
                                         start=(c == 0), stop=(c == CBLK - 1))
                    last.then_inc(s["hid_done"], 1)
                pe.wait_ge(s["band_used"], 2)
                for g in range(4):
                    r = 64 * (g % 2)
                    last = pe.matmul(k.ps[r:r + 64, 2 + g // 2, S:2 * S], pool_w[r:r + 64, g // 2, :], pooled[r:r + 64, g // 2, :],
                                     start=True, stop=True, skip_group_check=True)
                last.then_inc(s["mix_done"], 1)
                pe.wait_ge(s["feat_used"], 2)
                pe.wait_ge(s["hid_ready"], 2)
                pe.matmul(k.ps[0:HD, 6, 0:NG * NC], w2[:, 0, :], hidden[:, 0, :, :].rearrange("d g b -> d (g b)"), start=True, stop=True)
                for g in range(NG):
                    last = pe.matmul(k.ps[0:NC, 7, g * HD:(g + 1) * HD], hidden[:, 1, g, :], w2[:, 1, :], start=True, stop=True,
                                     skip_group_check=True)
                last.then_inc(s["cmp_done"], 1)

            @block.scalar
            def _(act):
                def hi(i):
                    if i >= 2:
                        piece_used(act, i - 2)
                    act.activation(w_hi[:, i % 2, :, :], piece(i), ACT.Copy).then_inc(s["piece_hi"], 1)

                for f in range(FT):
                    act.activation(x_hi[:, f, :], k.x_T[:, f, 0:S], ACT.Copy).then_inc(s["x_hi"], 1)
                for i in range(2):
                    hi(i)
                for tt in range(TT):
                    act.wait_ge(s["tok_done"], tt + 1)
                    act.activation(m.gates[:, tt, :], k.ps[:, 2 + tt, KVW:KVW + 3 * NH], ACT.Sigmoid).then_inc(s["gate_ready"], 1)
                    act.activation(m.v_win[:, tt, :], k.ps[:, 2 + tt, 0:KVW], ACT.Copy).then_inc(s["tok_used"], 2)
                def kept(i):
                    if i in (2, 3):
                        act.wait_ge(s["feat_done"], i + 1)
                        act.activation((m.ks_T, m.kw_T)[i - 2][:, :, :].rearrange("d g t -> d (g t)"), k.ps[0:HD, 4 + i, :], ACT.Copy).then_inc(s["feat_used"], 1)
                    elif i >= 4:
                        n = i - 4
                        act.wait_ge(s["q_done"], n + 1)
                        act.activation(m.q_T[:, 2 * n:2 * n + 2, :].rearrange("d h t -> d (h t)"), k.ps[0:HD, n % 2, :], ACT.Copy,
                                       scale=HD ** -0.5).then_inc(s["q_used"], 1)

                act.wait_ge(s["w_in"], 16)
                for i in range(2, PIECES + 2):
                    if i < PIECES:
                        hi(i)
                    kept(i - 2)
                act.wait_ge(s["band_done"], 1)
                for a in range(2):
                    act.activation(pooled[:, a, :], k.ps[:, 2 + a, 0:S], ACT.Copy).then_inc(s["band_used"], 1)
                for n in range(2):
                    act.wait_ge(s["hid_done"], n + 1)
                    act.activation(hidden[:, n, :, :].rearrange("d g b -> d (g b)"), k.ps[0:HD, 4 + n, 0:NG * NC], ACT.Gelu_apprx_tanh).then_inc(s["hid_ready"], 1)
                act.wait_ge(s["cmp_done"], 1)
                act.activation(m.kc_T[:, :, :].rearrange("d g b -> d (g b)"), k.ps[0:HD, 6, 0:NG * NC], ACT.Copy)
                act.activation(m.v_cmp[:, :, :].rearrange("b g d -> b (g d)"), k.ps[0:NC, 7, 0:KVW], ACT.Copy)

            @block.vector
            def _(dve):
                def lo(i):
                    dve.wait_ge(s["piece_hi"], i + 1)
                    dve.tensor_tensor(w_lo[:, i % 2, :, :], piece(i), w_hi[:, i % 2, :, :].bitcast(F32), ALU.subtract).then_inc(s["piece_lo"], 1)

                for f in range(FT):
                    dve.wait_ge(s["x_hi"], f + 1)
                    dve.tensor_tensor(x_lo[:, f, :], k.x_T[:, f, 0:S], x_hi[:, f, :].bitcast(F32), ALU.subtract)
                for i in range(2):
                    lo(i)
                dve.wait_ge(s["pos_turned"], 1)
                dve.tensor_copy(pos[:, :, :].rearrange("d n c -> d (n c)"), k.ps[0:HD, 7, 0:2 * CBLK]).then_inc(s["pos_ready"], 1)
                for tt in range(TT):
                    dve.wait_ge(s["tok_done"], tt + 1)
                    dve.tensor_copy(u_tok[:, tt, :], k.ps[:, tt, 0:256])
                    dve.tensor_copy(m.v_slc[:, tt, :], k.ps[:, tt, 256:256 + KVW]).then_inc(s["tok_used"], 2)
                    dve.wait_ge(s["gate_ready"], tt + 1)
                    g_cmp = m.gates[:, tt, :].rearrange("p (h b) -> p h b", b=3)[:, :, 0]
                    dve.tensor_scalar(g_cmp, g_cmp, k.any_cmp[:, tt:tt + 1], None, ALU.mult)
                dve.wait_ge(s["pos_ready"], 1)
                for n in range(2):
                    lo(2 + n)
                    dve.wait_ge(s["feat_done"], n + 1)
                    for g in range(NG):
                        toks = k.ps[0:HD, 4 + n, g * S:(g + 1) * S].rearrange("d (b c) -> d c b", c=STRIDE)
                        for half in range(2):
                            c0 = half * STRIDE
                            dve.tensor_tensor(blocks[:, n, c0:c0 + STRIDE, g, :], toks[:, :, half:half + NC],
                                              pos[:, n, c0:c0 + STRIDE].unsqueeze(2).broadcast_to([HD, STRIDE, NC]),
                                              ALU.add).then_inc(s["blocks_ready"], 1)
                for i in range(4, PIECES):
                    lo(i)
                dve.wait_ge(s["mix_done"], 1)
                for a in range(2):
                    dve.tensor_scalar(m.y_pool[:, a, :], k.ps[:, 2 + a, S:2 * S], k.col("pool_scale", l * 2 + a), None, ALU.mult)


def mixer1_attend(nc, k, m, w, l):
    names = ["q_staged", "c_done", "c_max", "c_exp", "c_step", "c_ready", "ct_done", "ct_ready",
             "s_done", "max_ready", "e_ready", "rs_step", "p_ready", "t_done", "t_ready", "pv_done", "o_used", "out_w"]
    SET = [(g, tt) for g in range(NG) for tt in range(TT)]
    NS = len(SET)
    UNITS = SET * 2
    NU = len(UNITS)
    with ExitStack() as ctx:
        def sb(name, shape):
            return ctx.enter_context(nc.sbuf_tensor(f"{name}_{nc.next_id()}", shape, F32))
        q_st = sb("q_staged_b", [HD, 2, NG, S])
        nmax = sb("nmax", [P, 3, 2])
        sums = sb("sums", [P, 3, 2])
        rs = sb("rs", [P, 3, 2])
        e = sb("e_b", [P, 3, 2, S])
        pt = sb("pt_b", [P, 2, 2, TT, P])
        nmax_c, sums_c, rs_c = sb("nmax_c", [P, NS]), sb("sums_c", [P, NS]), sb("rs_c", [P, NS])
        ec = sb("ec_b", [P, NS, NC])
        ptc = sb("ptc_b", [NC, 2, NS, P])
        with phase(nc, names) as (block, s):

            @block.sync
            def _(sp):
                sp.dma_start(m.wo_pool[:, :, :], w["w_out"].rearrange("l (a p) n -> l p a n", p=P)[l, :, 0:2, :]).then_inc(s["out_w"], 16)
                sp.dma_start(m.wo_att[:, :, :], w["w_out"][l, 256:D, :].rearrange("(h d) n -> d h n", d=HD)).then_inc(s["out_w"], 16)
                sp.wait_ge(s["out_w"], 32)

            @block.gpsimd
            def _(pool):
                with pool.Fori(0, HPG // 2) as j:
                    for h in range(2):
                        for g in range(NG):
                            pool.tensor_copy(q_st[:, h, g, :], m.q_T[:, ds(j * 2 + (h + g * HPG), 1), :].rearrange("d a t -> d (a t)")).then_inc(s["q_staged"], 1)
                    pool.wait_ge(s["s_done"], j * NU + NU)

            def s_bank(u):
                return k.ps[:, (0, 1, 3)[u % 3], :].rearrange("p (b t) -> p b t", b=2)

            c_bank = k.ps[:, 2, 0:NS * NC].rearrange("p (u n) -> p u n", u=NS)
            ct_bank = k.ps[0:NC, 7, :].rearrange("n (u t) -> n u t", u=NS)

            def t_bank(u):
                return k.ps[:, 4 + u % 2, :].rearrange("p (b c t) -> p b c t", b=2, c=TT)

            def o_bank(g):
                return k.ps[0:HD, 6, g * S:(g + 1) * S]

            @block.tensor
            def _(pe):
                with pe.Fori(0, HPG // 2) as j:
                    def compressed(h):
                        pe.wait_ge(s["q_staged"], j * 4 + (2 * h + 2))
                        if h == 1:
                            pe.wait_ge(s["c_exp"], j * 2 + 1)
                        for u, (g, tt) in enumerate(SET):
                            pe.matmul(c_bank[:, u, :], q_st[:, h, g, tt * P:(tt + 1) * P], m.kc_T[:, g, :], start=True, stop=False,
                                      skip_group_check=True)
                            last = pe.matmul(c_bank[:, u, :], k.ident[:, :], k.cmp_mask[:, tt, :], start=False, stop=True, skip_group_check=True)
                        last.then_inc(s["c_done"], 1)

                    def compressed_turn(h):
                        pe.wait_ge(s["c_ready"], j * 2 + (h + 1))
                        if h == 1:
                            pe.wait_ge(s["ct_ready"], j * 2 + 1)
                        for u in range(NS):
                            last = pe.transpose(ct_bank[:, u, :], ec[:, u, :], k.ident[:, :])
                        last.then_inc(s["ct_done"], 1)

                    def scores(u):
                        g, tt = UNITS[u]
                        n = (tt + 1) * P
                        if u >= 3:
                            pe.wait_ge(s["e_ready"], j * NU + (u - 2))
                        for b, key in enumerate((m.ks_T, m.kw_T)):
                            pe.matmul(s_bank(u)[:, b, 0:n], q_st[:, u // NS, g, tt * P:(tt + 1) * P], key[:, g, 0:n], start=True, stop=False,
                                      skip_group_check=True)
                            last = pe.matmul(s_bank(u)[:, b, n - P:n], k.ident[:, :], k.causal[:, :], start=False, stop=True,
                                             skip_group_check=True)
                        last.then_inc(s["s_done"], 1)

                    def turn(u):
                        g, tt = UNITS[u]
                        pe.wait_ge(s["p_ready"], j * NU + (u + 1))
                        if u >= 2:
                            pe.wait_ge(s["t_ready"], j * NU + (u - 1))
                        for b in range(2):
                            for c in range(tt + 1):
                                last = pe.transpose(t_bank(u)[:, b, c, :], e[:, u % 3, b, c * P:(c + 1) * P], k.ident[:, :])
                        last.then_inc(s["t_done"], 1)

                    def values(u):
                        g, tt = UNITS[u]
                        if u % NS == 0:
                            pe.wait_ge(s["o_used"], j * 4 + (2 * (u // NS) + 2))
                            pe.wait_ge(s["ct_ready"], j * 2 + (u // NS + 1))
                        pe.wait_ge(s["t_ready"], j * NU + (u + 1))
                        o = o_bank(g)[:, tt * P:(tt + 1) * P]
                        pe.matmul(o, m.v_cmp[:, g, :], ptc[:, u // NS, u % NS, :], start=True, stop=False, skip_group_check=True)
                        for b, v in enumerate((m.v_slc, m.v_win)):
                            for c in range(tt + 1):
                                last = pe.matmul(o, v[:, c, g * HD:(g + 1) * HD], pt[:, u % 2, b, c, :], start=False,
                                                 stop=(b == 1 and c == tt), skip_group_check=True)
                        last.then_inc(s["pv_done"], 1)

                    for u in range(NU + 3):
                        if u < NU and u % NS == 0:
                            compressed(u // NS)
                        if u < NU:
                            scores(u)
                        if u < NU and u % NS == 2:
                            compressed_turn(u // NS)
                        if 2 <= u < NU + 2:
                            turn(u - 2)
                        if u >= 3:
                            values(u - 3)

            @block.vector
            def _(dve):
                with dve.Fori(0, HPG // 2) as j:
                    def compressed(h):
                        c = Chain(dve, s["c_step"], j * 8 + 4 * h)
                        dve.wait_ge(s["c_exp"], j * 2 + (h + 1))
                        c.link(dve.tensor_scalar(rs_c[:, :], sums_c[:, :], 1e-30, None, ALU.max))
                        c.link(dve.reciprocal(rs_c[:, :], rs_c[:, :]))
                        for g in range(NG):
                            part = rs_c[:, g * TT:(g + 1) * TT].unsqueeze(2)
                            c.link(dve.tensor_tensor(part, part, m.gates[:, :, ds((j * 2 + (h + g * HPG)) * 3, 1)], ALU.mult))
                        dve.tensor_tensor(ec[:, :, :], ec[:, :, :], rs_c[:, :].unsqueeze(2).broadcast_to([P, NS, NC]),
                                          ALU.mult).then_inc(s["c_ready"], 1)

                    for u in range(NU + 1):
                        if u < NU and u % NS == 0:
                            dve.wait_ge(s["c_done"], j * 2 + (u // NS + 1))
                            dve.tensor_reduce(nmax_c[:, :], c_bank, AX.X, ALU.max, negate=True).then_inc(s["c_max"], 1)
                        if u < NU:
                            n = (UNITS[u][1] + 1) * P
                            dve.wait_ge(s["s_done"], j * NU + (u + 1))
                            dve.tensor_reduce(nmax[:, u % 3, :], s_bank(u)[:, :, 0:n], AX.X, ALU.max, negate=True).then_inc(s["max_ready"], 1)
                        if u < NU and u % NS == 1:
                            compressed(u // NS)
                        if u >= 1:
                            v = u - 1
                            g, tt = UNITS[v]
                            n = (tt + 1) * P
                            c = Chain(dve, s["rs_step"], j * (3 * NU) + 3 * v)
                            dve.wait_ge(s["e_ready"], j * NU + (v + 1))
                            c.link(dve.tensor_scalar(rs[:, v % 3, :], sums[:, v % 3, :], 1e-30, None, ALU.max))
                            c.link(dve.reciprocal(rs[:, v % 3, :], rs[:, v % 3, :]))
                            c.link(dve.tensor_tensor(rs[:, v % 3, :], rs[:, v % 3, :], m.gates[:, tt, ds((j * 2 + (v // NS + g * HPG)) * 3 + 1, 2)], ALU.mult))
                            for b in range(2):
                                last = dve.tensor_scalar(e[:, v % 3, b, 0:n], e[:, v % 3, b, 0:n], rs[:, v % 3, b:b + 1], None, ALU.mult)
                            last.then_inc(s["p_ready"], 1)

            @block.scalar
            def _(act):
                act.sem_inc(s["o_used"], 2)
                with act.Fori(0, HPG // 2) as j:
                    def outputs(h):
                        for g in range(NG):
                            act.wait_ge(s["pv_done"], j * NU + (h + 1) * NS)
                            act.activation(m.o_T[:, ds(j * 2 + (h + g * HPG), 1), :].rearrange("d a t -> d (a t)"), o_bank(g), ACT.Copy).then_inc(s["o_used"], 1)

                    for u in range(NU + 2):
                        if u < NU and u % NS == 0:
                            h = u // NS
                            act.wait_ge(s["c_max"], j * 2 + (h + 1))
                            if h == 1:
                                act.wait_ge(s["ct_done"], j * 2 + 1)
                            for i in range(NS):
                                last = act.activation(ec[:, i, :], c_bank[:, i, :], ACT.Exp, bias=nmax_c[:, i:i + 1], accum_out=sums_c[:, i:i + 1])
                            last.then_inc(s["c_exp"], 1)
                        if u < NU:
                            n = (UNITS[u][1] + 1) * P
                            act.wait_ge(s["max_ready"], j * NU + (u + 1))
                            if u >= 3:
                                act.wait_ge(s["t_done"], j * NU + (u - 2))
                            for b in range(2):
                                last = act.activation(e[:, u % 3, b, 0:n], s_bank(u)[:, b, 0:n], ACT.Exp, bias=nmax[:, u % 3, b:b + 1],
                                                      accum_out=sums[:, u % 3, b:b + 1])
                            last.then_inc(s["e_ready"], 1)
                        if u < NU and u % NS == 2:
                            act.wait_ge(s["ct_done"], j * 2 + (u // NS + 1))
                            act.activation(ptc[:, u // NS, :, :], ct_bank, ACT.Copy).then_inc(s["ct_ready"], 1)
                        if u >= 2:
                            v = u - 2
                            g, tt = UNITS[v]
                            act.wait_ge(s["t_done"], j * NU + (v + 1))
                            if v >= 2:
                                act.wait_ge(s["pv_done"], j * NU + (v - 1))
                            act.activation(pt[:, v % 2, :, 0:tt + 1, :], t_bank(v)[:, :, 0:tt + 1, :], ACT.Copy).then_inc(s["t_ready"], 1)
                        if u == NS + 2:
                            outputs(0)
                    outputs(1)


def mixer1(nc, k, w, l, m, ffn_ahead):
    with ExitStack() as ctx:
        def sb(name, shape):
            return ctx.enter_context(nc.sbuf_tensor(f"{name}_{nc.next_id()}", shape, F32))
        m.q_T = sb("q_T", [HD, NH, S])
        m.ks_T = sb("ks_T", [HD, NG, S])
        m.kw_T = sb("kw_T", [HD, NG, S])
        m.kc_T = sb("kc_T", [HD, NG, NC])
        m.v_slc = sb("v_slc", [P, TT, KVW])
        m.v_win = sb("v_win", [P, TT, KVW])
        m.v_cmp = sb("v_cmp", [NC, NG, HD])
        m.gates = sb("gates", [P, TT, 3 * NH])
        m.y_pool = sb("y_pool", [P, 2, S])
        mixer1_project(nc, k, m, w, l)
        m.o_T = sb("o_T", [HD, NH, S])
        m.wo_pool = sb("wo_pool", [P, 2, D])
        m.wo_att = sb("wo_att", [HD, NH, D])
        mixer1_attend(nc, k, m, w, l)
        chunks = [(m.y_pool[:, a, :], m.wo_pool[:, a, :]) for a in range(2)]
        chunks += [(m.o_T[:, h, :], m.wo_att[:, h, :]) for h in range(NH)]
        out_phase(nc, k, chunks, ln=(lambda f: k.col("ln2_g", l * FT + f), lambda f: k.col("ln2_b", l * FT + f)), ahead=ffn_ahead)


def scale_modulation(dve, k, b):
    for l in range(DEPTH):
        for at, name, plus in ((1, "pre_mix", 1.0), (2, "post_mix", 0.0), (4, "pre_ffn", 1.0), (5, "post_ffn", 0.0)):
            part = b.mod[:, l, at * FT:(at + 1) * FT, :]
            weight = k.par[:, PAR[name] + l * FT:PAR[name] + (l + 1) * FT].unsqueeze(2).broadcast_to([P, FT, 2])
            last = dve.scalar_tensor_tensor(part, part, plus, weight, ALU.add, ALU.mult)
    return last


BIAS_ROWS = 6


def bias_rows(nc, ctx, w):
    rpb = ctx.enter_context(nc.sbuf_tensor(f"rpb_rows_{nc.next_id()}", [BIAS_ROWS * CH, 2, 32], F32))
    return rpb, [(rpb[j * CH:(j + 1) * CH, r, 0:DX], w["odd_rpb_2"][0, :, j + 5 - r, :]) for r in range(2) for j in range(BIAS_ROWS)]


class Bias:
    PER = 5
    BANKS = (GW + 4) // 5
    BY_SCALAR = 9
    SEMS = ["bias_masked", "rpb_turned", "rpb_ready", "bias_done", "bias_used"]

    def __init__(self, out, pick, rows, rows_T):
        self.out, self.pick, self.rows, self.rows_T = out, pick, rows, rows_T

    def mask(self, pool, s):
        pool.memset(self.rows[:, :, DX:32], NEG).then_inc(s["bias_masked"], 1)

    def turn(self, pe, k, s):
        pe.wait_ge(s["bias_masked"], 1)
        pe.transpose(k.ps[0:64, 6, 0:BIAS_ROWS * CH], self.rows[:, :, :].rearrange("a r x -> a (r x)"),
                     k.ident[0:BIAS_ROWS * CH, 0:BIAS_ROWS * CH]).then_inc(s["rpb_turned"], 1)

    def keep_turned(self, act, k, s):
        act.wait_ge(s["rpb_turned"], 1)
        act.activation(self.rows_T[:, :], k.ps[0:64, 6, 0:BIAS_ROWS * CH], ACT.Copy).then_inc(s["rpb_ready"], 1)

    def products(self, pe, k, s, banks):
        pe.wait_ge(s["rpb_ready"], 1)
        m = BIAS_ROWS * CH
        for n in banks:
            if n >= 4:
                pe.wait_ge(s["bias_used"], n - 3)
            for c in range(n * self.PER, min((n + 1) * self.PER, GW)):
                at = c % self.PER * m
                last = pe.matmul(k.ps[:, 2 + n % 4, at:at + m], self.pick(c), self.rows_T[:, :], start=True, stop=True, skip_group_check=True)
            last.then_inc(s["bias_done"], 1)

    def keep(self, eng, copy, k, s, banks):
        for n in banks:
            m = min(self.PER, GW - n * self.PER)
            eng.wait_ge(s["bias_done"], n + 1)
            for j in range(BIAS_ROWS):
                last = copy(self.out[:, :, j, n * self.PER:n * self.PER + m].rearrange("p h c -> p c h"),
                            k.ps[:, 2 + n % 4, 0:m * BIAS_ROWS * CH].rearrange("p (c j h) -> p c j h", j=BIAS_ROWS, h=CH)[:, :, j, :])
            if n < self.BY_SCALAR:
                last.then_inc(s["bias_used"], 1)


def prenorm_phase(nc, k, b, l, ffn, streams, ahead=(), first=False, bias=None):
    names = ["sq_done", "side_step", "acc_step", "acc_done", "sum_done", "std_done", "r_done", "diag_done", "spread", "scaled", "n_done", "ahead_in"]
    names += Bias.SEMS if bias else []
    c0, n = streams[0] * S, len(streams) * S
    NT = n // P
    BY_ACT = (2, 3, 0, 1, 5, 4)
    with ExitStack() as ctx:
        def sb(name, shape):
            return ctx.enter_context(nc.sbuf_tensor(f"{name}_{nc.next_id()}", shape, F32))
        sq = sb("squares", [P, FT, n])
        std, r = sb("pre_std", [P, NT]), sb("pre_r", [P, NT])
        diag = sb("pre_diag", [P, NT, P])
        with phase(nc, names) as (block, s):
            by_vector = {(f, streams[-1]) for f in ((1, 3, 5) if len(streams) == 1 else (0, 1, 2, 3, 4))}

            if bias:
                by_vector |= {(f, streams[0]) for f in range(4, FT)} | {(f, streams[-1]) for f in range(FT)}

            def affine(f, st):
                at = (3 if ffn else 0) * FT + f
                return b.h_T[:, f, st * S:(st + 1) * S], b.mod[:, l, at + FT, st:st + 1], b.mod[:, l, at, st:st + 1]

            @block.sync
            def _(sp):
                load_ahead(sp, s, ahead)

            @block.scalar
            def _(act):
                for f in BY_ACT:
                    act.activation(sq[:, f, :], k.x_T[:, f, c0:c0 + n], ACT.Square).then_inc(s["sq_done"], 1)
                    if bias and f == BY_ACT[0]:
                        bias.keep_turned(act, k, s)
                act.wait_ge(s["sum_done"], 1)
                act.activation(std[:, :], k.ps[:, 0, 0:NT], ACT.Sqrt, bias=k.eps[:, 1:2], scale=1.0 / D).then_inc(s["std_done"], 1)
                if first:
                    act.wait_ge(s["scaled"], 1)
                act_copy = lambda to, frm: act.activation(to, frm, ACT.Copy)
                if bias:
                    bias.keep(act, act_copy, k, s, range(4))
                for f in range(FT):
                    act.wait_ge(s["n_done"], f + 1)
                    for st in streams:
                        if (f, st) not in by_vector:
                            h, scale, shift = affine(f, st)
                            act.activation(h, h, ACT.Identity, bias=shift, scale=scale)
                if bias:
                    bias.keep(act, act_copy, k, s, range(4, Bias.BY_SCALAR))

            @block.gpsimd
            def _(pool):
                if bias:
                    bias.mask(pool, s)
                pool.wait_ge(s["sq_done"], 2)
                pool.tensor_tensor(sq[:, 2, :], sq[:, 2, :], sq[:, 3, :], ALU.add).then_inc(s["side_step"], 1)
                pool.wait_ge(s["sq_done"], 5)
                pool.wait_ge(s["side_step"], 1)
                pool.tensor_tensor(sq[:, 2, :], sq[:, 2, :], sq[:, 5, :], ALU.add).then_inc(s["side_step"], 1)

            @block.tensor
            def _(pe):
                if bias:
                    bias.turn(pe, k, s)
                    bias.products(pe, k, s, range(1))
                pe.wait_ge(s["acc_done"], 1)
                for tt in range(NT):
                    last = pe.matmul(k.ps[:, 0, tt:tt + 1], sq[:, 6, tt * P:(tt + 1) * P], k.eps[:, 2:3], start=True, stop=True,
                                     skip_group_check=True)
                last.then_inc(s["sum_done"], 1)
                if bias:
                    bias.products(pe, k, s, range(1, 2))
                pe.wait_ge(s["diag_done"], NT)
                for tt in range(NT):
                    last = pe.matmul(k.ps[:, 1, tt * P:(tt + 1) * P], k.ones[:, :], diag[:, tt, :], start=True, stop=True, skip_group_check=True)
                last.then_inc(s["spread"], 1)
                if bias:
                    bias.products(pe, k, s, range(2, Bias.BANKS))

            @block.vector
            def _(dve):
                c = Chain(dve, s["acc_step"])
                for f in (6, 7):
                    last = dve.tensor_tensor(sq[:, f, :], k.x_T[:, f, c0:c0 + n], k.x_T[:, f, c0:c0 + n], ALU.mult)
                c.link(last)
                c.link(dve.tensor_tensor(sq[:, 6, :], sq[:, 6, :], sq[:, 7, :], ALU.add))
                for f, made in ((0, 3), (1, 4), (4, 6)):
                    dve.wait_ge(s["sq_done"], made)
                    c.link(dve.tensor_tensor(sq[:, 6, :], sq[:, 6, :], sq[:, f, :], ALU.add))
                dve.wait_ge(s["side_step"], 2)
                dve.tensor_tensor(sq[:, 6, :], sq[:, 6, :], sq[:, 2, :], ALU.add).then_inc(s["acc_done"], 1)
                if first:
                    scale_modulation(dve, k, b).then_inc(s["scaled"], 1)
                dve.wait_ge(s["std_done"], 1)
                dve.reciprocal(r[:, :], std[:, :]).then_inc(s["r_done"], 1)
                dve.wait_ge(s["r_done"], 1)
                for tt in range(NT):
                    dve.tensor_scalar(diag[:, tt, :], k.ident[:, :], r[:, tt:tt + 1], None, ALU.mult).then_inc(s["diag_done"], 1)
                dve.wait_ge(s["spread"], 1)
                if first:
                    dve.wait_ge(s["scaled"], 1)
                for f in range(FT + 1):
                    if f < FT:
                        dve.tensor_tensor(b.h_T[:, f, c0:c0 + n], k.x_T[:, f, c0:c0 + n], k.ps[:, 1, 0:n], ALU.mult).then_inc(s["n_done"], 1)
                    for st in streams:
                        if (f - 1, st) in by_vector:
                            dve.wait_ge(s["n_done"], f)
                            h, scale, shift = affine(f - 1, st)
                            dve.tensor_scalar(h, h, scale, shift, ALU.mult, ALU.add)
                if bias:
                    bias.keep(dve, dve.tensor_copy, k, s, range(Bias.BY_SCALAR, Bias.BANKS))


def gqa_buffers(nc, ctx, w):
    def sb(name, shape):
        return ctx.enter_context(nc.sbuf_tensor(f"{name}_{nc.next_id()}", shape, F32))
    m = Buffers()
    m.qk = sb("gqa_qk", [P, 2 * TT, (GQ + GKV) * HD2])
    m.v = sb("gqa_v", [P, 2 * TT, GKV * HD2])
    m.k_T = sb("gqa_k_T", [P, GKV, S + CTX])
    m.w_in = sb("gqa_w", [P, FT, BQ0])
    m.gain = sb("qk_gain", [P, GQ + GKV, HD2])
    m.cos, m.sin = sb("cos", [P, TT, HD2 // 2]), sb("sin", [P, TT, HD2 // 2])
    loads = [(m.w_in[:, :, :], w["even_w_in_2"][0].rearrange("(f p) n -> p f n", p=P)[:, :, 0:BQ0])]
    for h in range(GQ + GKV):
        g = w["even_q_norm_2"] if h < GQ else w["even_k_norm_2"]
        loads.append((m.gain[:, h, :], g.broadcast_to([P, HD2])))
    loads += [(m.cos[:, :, :], w["c_cos"]), (m.sin[:, :, :], w["c_sin"])]
    return m, loads


def gqa_project(nc, k, b, m, hgrn):
    names = ["h_hi", "p_done", "p_used", "copied", "sq_done", "ss_done", "std_done", "step", "rot_done", "turned"]
    NQK = GQ + GKV
    SPLITS = ((0, 1, 2), (3, 4, 5), (6, 7))
    with ExitStack() as ctx:
        def sb(name, shape):
            return ctx.enter_context(nc.sbuf_tensor(f"{name}_{nc.next_id()}", shape, F32))
        sq = sb("qk_sq", [P, NQK * HD2])
        ss, std, r = sb("qk_ss", [P, NQK]), sb("qk_std", [P, NQK]), sb("qk_r", [P, NQK])
        part = [sb(f"rot{n}", [P, NQK, HD2 // 2]) for n in range(4)]
        kd = sb("k_twice", [P, 2 * TT, GKV, 2, HD2])
        with phase(nc, names) as (block, s):

            @block.tensor
            def _(pe):
                for tt in range(2 * TT):
                    if tt >= 2:
                        pe.wait_ge(s["p_used"], tt - 1)
                    for bank, c0, c1 in ((0, 0, BANK), (1, BANK, BQ0)):
                        for f in range(FT):
                            last = pe.matmul(k.ps[:, 2 * (tt % 2) + bank, 0:c1 - c0], b.h_T[:, f, tt * P:(tt + 1) * P], m.w_in[:, f, c0:c1],
                                             start=(f == 0), stop=(f == FT - 1))
                    last.then_inc(s["p_done"], 1)
                pe.wait_ge(s["rot_done"], 2 * TT)
                for g in range(GKV):
                    for tt in range(2 * TT):
                        last = pe.transpose(k.ps[:, 4 + g, tt * P:(tt + 1) * P], kd[:, tt, g, :, :].rearrange("p a d -> p (a d)"), k.ident[:, :])
                    last.then_inc(s["turned"], 1)

            @block.scalar
            def _(act):
                for tt in range(2 * TT):
                    act.wait_ge(s["p_done"], tt + 1)
                    both = k.ps[:, 2 * (tt % 2):2 * (tt % 2) + 2, :].rearrange("p b n -> p (b n)")
                    act.activation(m.qk[:, tt, :], both[:, 0:NQK * HD2], ACT.Copy).then_inc(s["copied"], 1)
                    act.activation(m.v[:, tt, :], both[:, NQK * HD2:BQ0], ACT.Copy).then_inc(s["p_used"], 1)
                    act.wait_ge(s["copied"], tt + 1)
                    if tt >= 1:
                        act.wait_ge(s["std_done"], tt)
                    act.activation(sq[:, :], m.qk[:, tt, :], ACT.Square).then_inc(s["sq_done"], 1)
                    act.wait_ge(s["ss_done"], tt + 1)
                    act.activation(std[:, :], ss[:, :], ACT.Sqrt, bias=k.eps[:, 1:2], scale=1.0 / HD2).then_inc(s["std_done"], 1)
                    if tt < 2 * TT - 1:
                        for f in SPLITS[tt]:
                            act.activation(hgrn.h_hi[:, f, :], b.h_T[:, f, :], ACT.Copy).then_inc(s["h_hi"], 1)
                for g in range(GKV):
                    act.wait_ge(s["turned"], g + 1)
                    act.activation(m.k_T[:, g, :], k.ps[:, 4 + g, :], ACT.Copy)

            @block.vector
            def _(dve):
                c = Chain(dve, s["step"])
                half = HD2 // 2
                for tt in range(2 * TT):
                    qk = m.qk[:, tt, :].rearrange("p (h d) -> p h d", d=HD2)
                    dve.wait_ge(s["sq_done"], tt + 1)
                    dve.reduce_sum(ss[:, :], sq[:, :].rearrange("p (h d) -> p h d", d=HD2), AX.X).then_inc(s["ss_done"], 1)
                    dve.wait_ge(s["std_done"], tt + 1)
                    c.link(dve.reciprocal(r[:, :], std[:, :]))
                    c.link(dve.tensor_tensor(qk, qk, r[:, :].unsqueeze(2).broadcast_to([P, NQK, HD2]), ALU.mult))
                    c.link(dve.tensor_tensor(qk, qk, m.gain[:, :, :], ALU.mult))
                    if tt < TT:
                        x1, x2 = qk[:, :, 0:half], qk[:, :, half:HD2]
                        ct, st = (a[:, tt, :].unsqueeze(1).broadcast_to([P, NQK, half]) for a in (m.cos, m.sin))
                        dve.tensor_tensor(part[0][:, :, :], x1, ct, ALU.mult)
                        dve.tensor_tensor(part[1][:, :, :], x2, st, ALU.mult)
                        dve.tensor_tensor(part[2][:, :, :], x1, st, ALU.mult)
                        c.link(dve.tensor_tensor(part[3][:, :, :], x2, ct, ALU.mult))
                        dve.tensor_tensor(x1, part[0][:, :, :], part[1][:, :, :], ALU.subtract)
                        c.link(dve.tensor_tensor(x2, part[2][:, :, :], part[3][:, :, :], ALU.add))
                    keys = m.qk[:, tt, GQ * HD2:NQK * HD2].rearrange("p (g d) -> p g d", d=HD2)
                    for a in range(2):
                        last = dve.tensor_copy(kd[:, tt, :, a, :], keys)
                    last.then_inc(s["rot_done"], 1)
                    if tt < 2 * TT - 1:
                        for f in SPLITS[tt]:
                            dve.wait_ge(s["h_hi"], f + 1)
                            dve.tensor_tensor(hgrn.h_lo[:, f, :], b.h_T[:, f, :], hgrn.h_hi[:, f, :].bitcast(F32), ALU.subtract)


def soft_tensor(pe, k, s, a, units, base, extra, first_value):
    def scores(u):
        if u >= 3:
            pe.wait_ge(s["e_ready"], base + (u - 2))
        pe.matmul(k.ps[:, a.banks[u % 3], 0:units[u].n], units[u].q, units[u].key, start=True, stop=True).then_inc(s["s_done"], 1)

    def turn(u):
        pe.wait_ge(s["p_ready"], base + (u + 1))
        if u >= 2:
            pe.wait_ge(s["t_ready"], base + (u - 1))
        for c in range(units[u].n // P):
            last = pe.transpose(k.ps[:, 2 + u % 2, c * P:(c + 1) * P], a.e[:, u % 3, c * P:(c + 1) * P], k.ident[:, :])
        last.then_inc(s["t_done"], 1)

    def values(u):
        if u == 0:
            first_value()
        pe.wait_ge(s["t_ready"], base + (u + 1))
        for c, v in enumerate(units[u].v):
            last = pe.matmul(units[u].out, v, a.pt[:, u % 2, c, :], start=(c == 0), stop=(c == len(units[u].v) - 1),
                             skip_group_check=True)
        last.then_inc(s["pv_done"], 1)

    nu = len(units)
    for u in range(nu + 3):
        if u < nu:
            extra(u)
            scores(u)
        if 2 <= u < nu + 2:
            turn(u - 2)
        if u >= 3:
            values(u - 3)


def soft_vector(dve, k, s, a, units, base, side=lambda u: None):
    nu = len(units)
    for u in range(nu + 1):
        if u < nu:
            n, bias, bank = units[u].n, units[u].bias, a.banks[u % 3]
            dve.wait_ge(s["s_done"], base + (u + 1))
            if bias is not None:
                part = k.ps[:, bank, 0:S].rearrange("p (r c) -> p r c", c=GW)
                dve.tensor_tensor(part, part, bias, ALU.add).then_inc(s["bias_step"], 1)
                dve.wait_ge(s["bias_step"], base + (u + 1))
            dve.reduce_max(a.nmax[:, u % 3:u % 3 + 1], k.ps[:, bank, 0:n], AX.X, negate=True).then_inc(s["max_ready"], 1)
        if u >= 1:
            v = u - 1
            dve.wait_ge(s["e_ready"], base + (v + 1))
            dve.reciprocal(a.rs[:, v % 3:v % 3 + 1], a.sums[:, v % 3:v % 3 + 1]).then_inc(s["rs_step"], 1)
            dve.wait_ge(s["rs_step"], base + (v + 1))
            e = a.e[:, v % 3, 0:units[v].n]
            dve.tensor_scalar(e, e, a.rs[:, v % 3:v % 3 + 1], None, ALU.mult).then_inc(s["p_ready"], 1)
            side(v)


def soft_scalar(act, k, s, a, units, base, side=lambda u: None):
    nu = len(units)
    for u in range(nu + 2):
        if u < nu:
            n = units[u].n
            act.wait_ge(s["max_ready"], base + (u + 1))
            if u >= 3:
                act.wait_ge(s["t_done"], base + (u - 2))
            act.activation(a.e[:, u % 3, 0:n], k.ps[:, a.banks[u % 3], 0:n], ACT.Exp, bias=a.nmax[:, u % 3:u % 3 + 1],
                           accum_out=a.sums[:, u % 3:u % 3 + 1]).then_inc(s["e_ready"], 1)
        if u >= 2:
            v = u - 2
            n = units[v].n
            act.wait_ge(s["t_done"], base + (v + 1))
            if v >= 2:
                act.wait_ge(s["pv_done"], base + (v - 1))
            act.activation(a.pt[:, v % 2, 0:n // P, :].rearrange("p c t -> p (c t)"), k.ps[:, 2 + v % 2, 0:n], ACT.Copy).then_inc(s["t_ready"], 1)
            side(v)


SOFT_SEMS = ["s_done", "bias_step", "max_ready", "e_ready", "rs_step", "p_ready", "t_done", "t_ready", "pv_done"]


def soft_buffers(nc, ctx, third_bank, e=None):
    def sb(name, shape):
        return ctx.enter_context(nc.sbuf_tensor(f"{name}_{nc.next_id()}", shape, F32))
    got = Buffers()
    got.banks = (0, 1, third_bank)
    got.e = sb("soft_e", [P, 3, 2 * S]) if e is None else e
    got.pt = sb("soft_pt", [P, 2, 4, P])
    got.nmax = sb("soft_max", [P, 3])
    got.sums = sb("soft_sums", [P, 3])
    got.rs = sb("soft_rs", [P, 3])
    return got


def gqa_attend(nc, k, b, m, ahead):
    names = ["q_staged", "q_turned", "q_ready", "o_used", "ahead_in"] + SOFT_SEMS
    NP = GQ // GKV // 2
    with ExitStack() as ctx:
        def sb(name, shape):
            return ctx.enter_context(nc.sbuf_tensor(f"{name}_{nc.next_id()}", shape, F32))
        q_st = sb("gqa_q_st", [P, GKV, 2 * TT, P])
        q_T = sb("gqa_q_T", [P, GKV, S + CTX])
        a = soft_buffers(nc, ctx, 6)
        with phase(nc, names) as (block, s):
            units = []
            for g in range(GKV):
                for hh in range(2):
                    rows = slice(HD2 * hh, HD2 * hh + HD2)
                    for tt in range(2 * TT):
                        first = 0 if tt < TT else TT
                        units.append(Unit(
                            q=q_T[rows, g, tt * P:(tt + 1) * P], key=m.k_T[rows, g, first * P:S + CTX], n=(2 * TT - first) * P, bias=None,
                            v=[m.v[:, c, g * HD2:(g + 1) * HD2] for c in range(first, 2 * TT)],
                            out=k.ps[rows, 4 + g, tt * P:(tt + 1) * P]))
            nu = len(units)

            @block.sync
            def _(sp):
                load_ahead(sp, s, ahead)

            @block.gpsimd
            def _(pool):
                with pool.Fori(0, NP) as j:
                    for g in range(GKV):
                        pool.tensor_copy(q_st[:, g, :, :], m.qk[:, :, ds((j + g * NP) * P, P)]).then_inc(s["q_staged"], 1)
                    pool.wait_ge(s["q_turned"], j * 2 + 2)

            @block.tensor
            def _(pe):
                with pe.Fori(0, NP) as j:
                    for g in range(GKV):
                        pe.wait_ge(s["q_staged"], j * 2 + (g + 1))
                        for tt in range(2 * TT):
                            last = pe.transpose(k.ps[:, 6 + g, tt * P:(tt + 1) * P], q_st[:, g, tt, :], k.ident[:, :])
                        last.then_inc(s["q_turned"], 1)

                    def queries(u):
                        if u % (nu // GKV) == 0:
                            pe.wait_ge(s["q_ready"], j * 2 + (u // (nu // GKV) + 1))

                    def outputs():
                        pe.wait_ge(s["o_used"], j * 2 + 2)
                    soft_tensor(pe, k, s, a, units, j * nu, queries, outputs)

            @block.vector
            def _(dve):
                with dve.Fori(0, NP) as j:
                    soft_vector(dve, k, s, a, units, j * nu)

            @block.scalar
            def _(act):
                act.sem_inc(s["o_used"], 2)
                with act.Fori(0, NP) as j:
                    for g in range(GKV):
                        act.wait_ge(s["q_turned"], j * 2 + (g + 1))
                        act.activation(q_T[:, g, :], k.ps[:, 6 + g, :], ACT.Copy, scale=HD2 ** -0.5).then_inc(s["q_ready"], 1)
                    soft_scalar(act, k, s, a, units, j * nu)
                    for g in range(GKV):
                        act.wait_ge(s["pv_done"], j * nu + (g + 1) * (nu // GKV))
                        act.activation(b.y_T[:, ds(j + g * NP, 1), :].rearrange("p a t -> p (a t)"), k.ps[:, 4 + g, :], ACT.Copy).then_inc(s["o_used"], 1)


def odd_columns(w):
    return w["odd_w_qkv_2"][0].rearrange("(f p) (a i n) -> i a p f n", p=P, a=3, n=P)


def odd_attend(nc, k, b, w, wq, spare, ahead):
    names = ["ahead_in", "h_hi", "h_lo", "w0_in", "w1_in", "w_hi", "w_lo", "proj_done", "proj_used", "o_used"] + SOFT_SEMS
    NPAIR = CH // 2
    TURNS = NPAIR // 2
    PARTS = [(0, 0), (0, 1), (1, 0), (1, 1), (0, 2), (1, 2)]
    with ExitStack() as ctx:
        def sb(name, shape, dt=F32):
            return ctx.enter_context(nc.sbuf_tensor(f"{name}_{nc.next_id()}", shape, dt))
        h_hi, h_lo = sb("odd_h_hi", [P, FT, S + CTX], F32R), sb("odd_h_lo", [P, FT, S + CTX], F32R)
        w_hi, w_lo = (sb(f"odd_w_{x}", [P, 3, FT, 2, P], F32R) for x in ("hi", "lo"))
        q_T, k_T, v, e = (spare[:, at:at + n].rearrange("p (a n) -> p a n", n=width) for at, n, width in (
            (0, 2 * S, S), (2 * S, 2 * (S + CTX), S + CTX), (4 * S + 2 * CTX, 4 * TT * P, P),
            (4 * S + 2 * CTX + 4 * TT * P, 6 * S, 2 * S)))
        v = v.rearrange("p (a c) n -> p a c n", a=2)
        a = soft_buffers(nc, ctx, 5, e)
        with phase(nc, names) as (block, s):
            w_in = [s["w0_in"], s["w1_in"]]
            cols = odd_columns(w)

            def make_units(j):
                units = []
                for pp in range(2):
                    for hh in range(2):
                        rows = slice(HD2 * hh, HD2 * hh + HD2)
                        for tt in range(TT):
                            bias = None if j is None else b.bias[:, ds(j * 4 + (2 * pp + hh), 1), 2 - 2 * tt:2 - 2 * tt + NROW, :].rearrange(
                                "p a r c -> p (a r) c")
                            units.append(Unit(
                                q=q_T[rows, pp, tt * P:(tt + 1) * P], key=k_T[rows, pp, :], n=S + CTX, bias=bias,
                                v=[v[:, pp, c, rows] for c in range(2 * TT)],
                                out=k.ps[rows, 4, pp * S + tt * P:pp * S + (tt + 1) * P]))
                return units
            nu = len(make_units(None))

            def turns(eng, body):
                with eng.Fori(0, TURNS - 1) as j:
                    body(j, True)
                body(TURNS - 1, False)

            @block.sync
            def _(sp):
                for n in range(2):
                    sp.sem_inc(w_in[n], 48)
                with sp.Fori(0, TURNS - 1) as j:
                    for n in range(2):
                        sp.wait_ge(s["w_lo"], j * 6 + (5 + n))
                        for part in range(3):
                            sp.dma_start(wq[n][:, part, :, :], cols[j * 2 + (n + 2), part]).then_inc(w_in[n], 16)
                sp.wait_ge(s["h_lo"], FT)
                load_ahead(sp, s, ahead)

            @block.tensor
            def _(pe):
                def body(j, more):
                    hl = ((w_hi, h_hi), (w_hi, h_lo), (w_lo, h_hi))
                    for i, (n, part) in enumerate(PARTS[:4]):
                        pe.wait_ge(s["w_lo"], j * 6 + (i + 1))
                        if n == 1:
                            pe.wait_ge(s["proj_used"], j * 6 + (part + 1))
                        to = S + part * CTX
                        for f in range(FT):
                            if i == 0:
                                pe.wait_ge(s["h_lo"], f + 1)
                            for p, (wt, h) in enumerate(hl):
                                last = pe.matmul(k.ps[:, 6 + part, 0:to], wt[:, part, f, n, :], h[:, f, 0:to],
                                                 start=(f == 0 and p == 0), stop=(f == FT - 1 and p == 2))
                        last.then_inc(s["proj_done"], 1)
                    def values():
                        pe.wait_ge(s["w_lo"], j * 6 + 6)
                        for tt in range(2 * TT):
                            for f in range(FT):
                                for p, (wt, h) in enumerate(hl):
                                    last = pe.matmul(k.ps[:, (1, 5)[tt // 2], tt % 2 * 2 * P:(tt % 2 + 1) * 2 * P], h[:, f, tt * P:(tt + 1) * P],
                                                     wt[:, 2, f, :, :].rearrange("p a n -> p (a n)"), start=(f == 0 and p == 0),
                                                     stop=(f == FT - 1 and p == 2), skip_group_check=True)
                            if tt % 2:
                                last.then_inc(s["proj_done"], 1)

                    def pair(u):
                        if u == 0:
                            pe.wait_ge(s["proj_used"], j * 6 + 2)
                        if u == 1:
                            values()
                            pe.wait_ge(s["proj_used"], j * 6 + 5)
                        if u == 2:
                            pe.wait_ge(s["proj_used"], j * 6 + 6)

                    def outputs():
                        pe.wait_ge(s["o_used"], j + 1)
                    soft_tensor(pe, k, s, a, make_units(None), j * nu, pair, outputs)

                turns(pe, body)

            @block.vector
            def _(dve):
                def split(i, turn):
                    n, part = PARTS[i]
                    dve.wait_ge(s["w_hi"], turn * 6 + (i + 1))
                    dve.tensor_tensor(w_lo[:, part, :, n, :], wq[n][:, part, :, :], w_hi[:, part, :, n, :].bitcast(F32),
                                      ALU.subtract).then_inc(s["w_lo"], 1)

                def body(j, more):
                    soft_vector(dve, k, s, a, make_units(j), j * nu, lambda u: split(u - 2, j + 1) if more and u >= 2 else None)

                split(0, 0)
                for f in range(FT):
                    dve.wait_ge(s["h_hi"], f + 1)
                    dve.tensor_tensor(h_lo[:, f, :], b.h_T[:, f, :], h_hi[:, f, :].bitcast(F32), ALU.subtract).then_inc(s["h_lo"], 1)
                for i in range(1, len(PARTS)):
                    split(i, 0)
                turns(dve, body)

            @block.scalar
            def _(act):
                def split(i, turn):
                    n, part = PARTS[i]
                    act.wait_ge(w_in[n], turn * 48 + 48)
                    act.activation(w_hi[:, part, :, n, :], wq[n][:, part, :, :], ACT.Copy).then_inc(s["w_hi"], 1)

                def body(j, more):
                    for n in range(2):
                        act.wait_ge(s["proj_done"], j * 6 + (2 * n + 1))
                        act.activation(q_T[:, n, :], k.ps[:, 6, 0:S], ACT.Copy, scale=HD2 ** -0.5).then_inc(s["proj_used"], 1)
                        act.wait_ge(s["proj_done"], j * 6 + (2 * n + 2))
                        act.activation(k_T[:, n, :], k.ps[:, 7, :], ACT.Copy).then_inc(s["proj_used"], 1)
                    for half in range(2):
                        act.wait_ge(s["proj_done"], j * 6 + (5 + half))
                        act.activation(v[:, :, 2 * half:2 * half + 2, :], k.ps[:, (1, 5)[half], :].rearrange("p (t a d) -> p a t d", t=2, a=2),
                                       ACT.Copy).then_inc(s["proj_used"], 1)
                    soft_scalar(act, k, s, a, make_units(None), j * nu, lambda u: split(u, j + 1) if more and u < len(PARTS) else None)
                    act.wait_ge(s["pv_done"], j * nu + nu)
                    act.activation(b.y_T[:, ds(j * 2, 2), 0:S], k.ps[:, 4, :].rearrange("p (a t) -> p a t", a=2), ACT.Copy).then_inc(s["o_used"], 1)

                act.sem_inc(s["o_used"], 1)
                split(0, 0)
                for f in range(FT):
                    act.activation(h_hi[:, f, :], b.h_T[:, f, :], ACT.Copy).then_inc(s["h_hi"], 1)
                for i in range(1, len(PARTS)):
                    split(i, 0)
                turns(act, body)


def hgrn_buffers(nc, ctx, w):
    def sb(name, shape):
        return ctx.enter_context(nc.sbuf_tensor(f"{name}_{nc.next_id()}", shape, F32))
    m = Buffers()
    m.h_hi, m.h_lo = (ctx.enter_context(nc.sbuf_tensor(f"hgrn_h_{x}_{nc.next_id()}", [P, FT, S + CTX], F32R)) for x in ("hi", "lo"))
    m.wh = sb("hgrn_w", [P, FT, 5, P])
    m.e = sb("hgrn_e", [P, 2, CUM])
    m.lvl = sb("hgrn_lvl", [P, 2, NSC])
    m.gain = sb("hgrn_gain", [P, P])
    loads = [(m.e[:, :, :], w["c_cum"]), (m.lvl[:, :, :], w["c_lvl"]), (m.gain[:, :], w["hgrn_out_norm_2"].broadcast_to([P, P]))]
    return m, loads + hgrn_loads(m, w, 0)


def hgrn_loads(m, w, i):
    cols = w["even_w_in_2"][0][:, BQ0:BQ0 + 5 * BH * P].rearrange("(f p) (a i n) -> i a p f n", p=P, a=5, n=P)
    return [(m.wh[:, :, part, :], cols[i, part]) for part in range(5)]


def hgrn_phase(nc, k, b, w, m, ahead):
    names = ["ahead_in", "cum_ready", "w_in", "w_hi", "w_lo01", "w_lo234", "side_done", "proj_done", "q_ready", "q_scaled", "gate_ready", "abs_ready", "soft_step", "g_ready", "v_ready", "g_turned",
             "g_hi", "g_lo", "cum_done", "e_ready", "qk_q", "qk_k", "sc_done", "masked", "p_ready", "pv_done", "x_ready", "x_done", "x_used",
             "o_done", "sq_done", "std_done", "r_step", "y_ready", "y_turned", "y_used"]
    TILES = 2 * TT
    NU = 2 * TILES
    UNITS = [(d, tt) for d in range(2) for tt in range(TILES)]
    N9 = NLV + 2
    N8 = NLV + 1
    with ExitStack() as ctx:
        def sb(name, shape, dt=F32):
            return ctx.enter_context(nc.sbuf_tensor(f"{name}_{nc.next_id()}", shape, dt))
        wh, lvl, gain = m.wh, m.lvl, m.gain
        e = m.e[:, :, :].rearrange("p u (n t) -> p u n t", t=P)
        h_hi, h_lo = m.h_hi, m.h_lo
        w_hi, w_lo = sb("hgrn_w_hi", [P, FT, 2, P], F32R), sb("hgrn_w_lo", [P, FT, 2, P], F32R)
        cum = sb("hgrn_cum", [P, 2, 3, CUM // 3], F32R)
        g_hi, g_lo = sb("hgrn_g_hi", [P, 2, TILES, P], F32R), sb("hgrn_g_lo", [P, 2, TILES, P], F32R)
        q = sb("hgrn_q", [P, TILES, P])
        kk = sb("hgrn_k", [P, 2, TILES, P])
        ab = sb("hgrn_abs", [P, 2, TILES * P])
        g = ab[:, :, :].rearrange("p d (t n) -> p d t n", n=P)
        v = sb("hgrn_v", [P, TILES, P])
        sg = sb("hgrn_gate", [P, TILES, P])
        kd = sb("hgrn_kd", [P, 2, NLV, P])
        qd = sb("hgrn_qd", [P, 2, NLV, P])
        ke = sb("hgrn_ke", [P, NU, P])
        qs = sb("hgrn_qs", [P, NU, P])
        pm = sb("hgrn_pm", [P, 2, N8, P])
        pr = sb("hgrn_p", [P, 2, P])
        tot = sb("hgrn_tot", [P, NU])
        kx = sb("hgrn_kx", [P, 2, P])
        qx = sb("hgrn_qx", [P, 2, P])
        px = pm[:, :, 0:6, :]
        ss, std, r = sb("hgrn_ss", [P, TILES]), sb("hgrn_std", [P, TILES]), sb("hgrn_r", [P, TILES])
        y = sb("hgrn_y", [P, TILES, P])
        with phase(nc, names) as (block, s):
            flat = k.ps[:, :, :].rearrange("p b n -> p (b n)")
            CUM_PS = k.ps[:, 0:3, 0:CUM // 3]
            SPLIT = 5
            SC_PS = flat[:, 3 * BANK:3 * BANK + N8 * P]
            X_PS = flat[:, 5 * BANK:5 * BANK + 6 * P]
            O = 7

            def order(d, stream):
                tiles = (0, 1) if stream == 0 else (2, 3)
                return tiles if d == 0 else tiles[::-1]

            def cross(d):
                l0, l1 = order(d, 0)
                c0, c1 = order(d, 1)
                key = lambda tt: ke[:, d * TILES + tt, :]
                qry = lambda tt: qs[:, d * TILES + tt, :]
                return [(c0, c1, key(c0), qry(c1)), (l0, l1, key(l0), qry(l1)),
                        (c0, l0, kx[:, d, :], qry(l0)), (c0, l1, kx[:, d, :], qx[:, d, :]),
                        (c1, l0, key(c1), qry(l0)), (c1, l1, key(c1), qx[:, d, :])]

            @block.sync
            def _(sp):
                with sp.Fori(0, BH - 1) as i:
                    sp.wait_ge(s["w_lo01"], i * 2 + 2)
                    sp.wait_ge(s["w_lo234"], i * 3 + 3)
                    for dst, src in hgrn_loads(m, w, i + 1):
                        sp.dma_start(dst, src).then_inc(s["w_in"], 16)
                load_ahead(sp, s, ahead)

            def heads(eng, body):
                with eng.Fori(0, BH - 1) as i:
                    body(i, True)
                body(BH - 1, False)

            @block.tensor
            def _(pe):
                SPLITS = ((w_hi, h_hi), (w_hi, h_lo), (w_lo, h_hi))

                def part(h, n):
                    if n < 2:
                        pe.wait_ge(s["w_lo01"], h * 2 + (n + 1))
                    else:
                        pe.wait_ge(s["w_lo234"], h * 3 + 1)
                    for f in range(FT):
                        for p, (wt, x) in enumerate(SPLITS):
                            last = pe.matmul(k.ps[:, n, :], wt[:, f, n % 2, :], x[:, f, :], start=(f == 0 and p == 0), stop=(f == FT - 1 and p == 2))
                    last.then_inc(s["proj_done"], 1)

                def values_and_gates(h):
                    pe.wait_ge(s["w_lo234"], h * 3 + 3)
                    for tt in range(TILES):
                        for f in range(FT):
                            for p, (wt, x) in enumerate(SPLITS):
                                last = pe.matmul(k.ps[:, 3 + tt // 2, tt % 2 * 2 * P:(tt % 2 + 1) * 2 * P], x[:, f, tt * P:(tt + 1) * P],
                                                 wt[:, f, :, :].rearrange("p a n -> p (a n)"), start=(f == 0 and p == 0),
                                                 stop=(f == FT - 1 and p == 2), skip_group_check=True)
                        if tt % 2:
                            last.then_inc(s["proj_done"], 1)

                def decays_to_token_major(h):
                    for d in range(2):
                        pe.wait_ge(s["g_ready"], h * 2 + (d + 1))
                        for tt in range(TILES):
                            last = pe.transpose(k.ps[:, 5 + d, tt * P:(tt + 1) * P], g[:, d, tt, :], k.ident[:, :])
                        last.then_inc(s["g_turned"], 1)

                def tiles(i, more):
                    pe.matmul(k.ps[:, O, :], k.zero[:, :], k.x_T[:, 0, :], start=True, stop=False, skip_group_check=True)
                    pe.wait_ge(s["g_lo"], i * 2 + 2)
                    pe.wait_ge(s["q_ready"], i + 1)
                    pe.wait_ge(s["abs_ready"], i * 2 + 2)

                    def sums(u):
                        d, tt = UNITS[u]
                        if u >= 1:
                            pe.wait_ge(s["e_ready"], i * NU + u)
                        for c in range(3):
                            for p, part in enumerate((g_hi, g_lo)):
                                last = pe.matmul(CUM_PS[:, c, :], part[:, d, tt, :], cum[:, d, c, :], start=(p == 0), stop=(p == 1))
                        last.then_inc(s["cum_done"], 1)

                    def scores(u):
                        d, tt = UNITS[u]
                        pe.wait_ge(s["qk_q"], i * NU + (u + 1))
                        pe.wait_ge(s["qk_k"], i * NU + (u + 1))
                        if u >= 1:
                            pe.wait_ge(s["masked"], i * NU + u)
                        else:
                            pe.wait_ge(s["v_ready"], i * 2 + 2)
                        for n in range(NLV):
                            pe.matmul(SC_PS[:, n * P:(n + 1) * P], kd[:, u % 2, n, :], qd[:, u % 2, n, :], start=True, stop=True,
                                      skip_group_check=True)
                        pe.matmul(SC_PS[:, NLV * P:N8 * P], kk[:, d, tt, :], q[:, tt, :], start=True, stop=True,
                                  skip_group_check=True).then_inc(s["sc_done"], 1)

                    def values(u):
                        d, tt = UNITS[u]
                        pe.wait_ge(s["p_ready"], i * NU + (u + 1))
                        pe.matmul(k.ps[:, O, tt * P:(tt + 1) * P], pr[:, u % 2, :], v[:, tt, :], start=False, stop=False,
                                  skip_group_check=True).then_inc(s["pv_done"], 1)

                    for u in range(NU + 2):
                        if u < NU:
                            sums(u)
                        if 1 <= u <= NU:
                            scores(u - 1)
                        if u == NU and more:
                            pe.wait_ge(s["e_ready"], i * NU + NU)
                            part(i + 1, 0)
                        if u >= 2:
                            values(u - 2)

                def cross_scores(i, d):
                    pe.wait_ge(s["x_ready"], i * 2 + (d + 1))
                    if d == 1:
                        pe.wait_ge(s["x_used"], i * 2 + 1)
                    for n, (_, _, key, qry) in enumerate(cross(d)):
                        last = pe.matmul(X_PS[:, n * P:(n + 1) * P], key, qry, start=True, stop=True, skip_group_check=True)
                    last.then_inc(s["x_done"], 1)

                def cross_values(i):
                    for d in range(2):
                        pe.wait_ge(s["x_used"], i * 2 + (d + 1))
                        for n, (src, dst, _, _) in enumerate(cross(d)):
                            last = pe.matmul(k.ps[:, O, dst * P:(dst + 1) * P], px[:, d, n, :], v[:, src, :], start=False,
                                             stop=(d == 1), skip_group_check=True)
                    last.then_inc(s["o_done"], 1)

                def turn_out(i):
                    pe.wait_ge(s["y_ready"], i + 1)
                    for tt in range(TILES):
                        last = pe.transpose(k.ps[:, O, tt * P:(tt + 1) * P], y[:, tt, :], k.ident[:, :])
                    last.then_inc(s["y_turned"], 1)

                def body(i, more):
                    tiles(i, more)
                    cross_scores(i, 0)
                    if more:
                        part(i + 1, 1)
                    cross_scores(i, 1)
                    if more:
                        part(i + 1, 2)
                    cross_values(i)
                    if more:
                        pe.wait_ge(s["masked"], i * NU + NU)
                        values_and_gates(i + 1)
                    turn_out(i)
                    if more:
                        decays_to_token_major(i + 1)
                    pe.wait_ge(s["y_used"], i + 1)

                for n in range(3):
                    part(0, n)
                values_and_gates(0)
                pe.wait_ge(s["cum_ready"], 1)
                decays_to_token_major(0)
                heads(pe, body)

            @block.scalar
            def _(act):
                def split(h, part):
                    if part >= 2:
                        act.wait_ge(s["proj_done"], h * 5 + (part - 1))
                    act.activation(w_hi[:, :, part % 2, :], wh[:, :, part, :], ACT.Copy).then_inc(s["w_hi"], 1)

                def queries(h):
                    act.wait_ge(s["proj_done"], h * 5 + 1)
                    act.activation(q[:, :, :].rearrange("p t d -> p (t d)"), k.ps[:, 0, :], ACT.Silu).then_inc(s["q_ready"], 1)

                def keys(h, d):
                    act.wait_ge(s["proj_done"], h * 5 + (2 + d))
                    act.activation(kk[:, d, :, :].rearrange("p t d -> p (t d)"), k.ps[:, 1 + d, :], ACT.Sigmoid, scale=-1.0)
                    act.activation(ab[:, d, :], k.ps[:, 1 + d, :], ACT.Abs).then_inc(s["abs_ready"], 1)

                def softplus(h):
                    act.wait_ge(s["abs_ready"], h * 2 + 2)
                    for d in range(2):
                        act.activation(ab[:, d, :], ab[:, d, :], ACT.Exp, scale=-1.0).then_inc(s["soft_step"], 1)
                    act.wait_ge(s["soft_step"], h * 4 + 2)
                    for d in range(2):
                        act.activation(ab[:, d, :], ab[:, d, :], ACT.Ln, bias=k.eps[:, 2:3]).then_inc(s["soft_step"], 1)

                def values_and_gates(h):
                    for n in range(2):
                        act.wait_ge(s["proj_done"], h * 5 + (4 + n))
                        both = k.ps[:, 3 + n, :].rearrange("p (t a d) -> p t a d", t=2, a=2)
                        act.activation(sg[:, 2 * n:2 * n + 2, :], both[:, :, 0, :], ACT.Silu)
                        act.activation(v[:, 2 * n:2 * n + 2, :], both[:, :, 1, :], ACT.Copy).then_inc(s["v_ready"], 1)

                def decays(h):
                    for d in range(2):
                        act.wait_ge(s["g_turned"], h * 2 + (d + 1))
                        act.activation(g_hi[:, d, :, :].rearrange("p t d -> p (t d)"), k.ps[:, 5 + d, :], ACT.Copy).then_inc(s["g_hi"], 1)

                def tiles(i, more):
                    for u in range(NU):
                        act.wait_ge(s["cum_done"], i * NU + (u + 1))
                        if u >= 2:
                            act.wait_ge(s["qk_q"], i * NU + (u - 1))
                            act.wait_ge(s["side_done"], i * NU + (u - 1))
                        act.activation(m.e[:, u % 2, :].rearrange("p (b n) -> p b n", b=3), CUM_PS, ACT.Exp).then_inc(s["e_ready"], 1)
                        if more and u == 5:
                            act.wait_ge(s["w_in"], i * 80 + 80)
                            for part in range(2):
                                split(i + 1, part)

                def cross_scores(i, d):
                    act.wait_ge(s["x_done"], i * 2 + (d + 1))
                    act.activation(px[:, d, :, :].rearrange("p n t -> p (n t)"), X_PS, ACT.Copy).then_inc(s["x_used"], 1)

                def norm(i):
                    act.wait_ge(s["o_done"], i + 1)
                    for tt in range(TILES):
                        last = act.activation(y[:, tt, :], k.ps[:, O, tt * P:(tt + 1) * P], ACT.Square, accum_out=ss[:, tt:tt + 1])
                    last.then_inc(s["sq_done"], 1)
                    act.wait_ge(s["sq_done"], i + 1)
                    act.activation(std[:, :], ss[:, :], ACT.Sqrt, bias=k.eps[:, 1:2], scale=1.0 / P).then_inc(s["std_done"], 1)

                def body(i, more):
                    tiles(i, more)
                    if more:
                        queries(i + 1)
                        split(i + 1, 2)
                    cross_scores(i, 0)
                    if more:
                        keys(i + 1, 0)
                        split(i + 1, 3)
                    cross_scores(i, 1)
                    if more:
                        keys(i + 1, 1)
                        split(i + 1, 4)
                    norm(i)
                    if more:
                        softplus(i + 1)
                        act.wait_ge(s["y_ready"], i + 1)
                        values_and_gates(i + 1)
                    act.wait_ge(s["y_turned"], i + 1)
                    act.activation(b.y_T[:, ds(i + BH, 1), :].rearrange("p a t -> p (a t)"), k.ps[:, O, :], ACT.Copy).then_inc(s["y_used"], 1)
                    if more:
                        decays(i + 1)

                for part in range(2):
                    split(0, part)
                for d in range(2):
                    last = act.activation(cum[:, d, :, :].rearrange("p b n -> p (b n)"), m.e[:, d, :], ACT.Copy)
                last.then_inc(s["cum_ready"], 1)
                queries(0)
                split(0, 2)
                for d in range(2):
                    split(0, 3 + d)
                    keys(0, d)
                softplus(0)
                values_and_gates(0)
                decays(0)
                heads(act, body)

            @block.gpsimd
            def _(pool):
                def split(h):
                    for part in range(2):
                        pool.wait_ge(s["w_hi"], h * SPLIT + (part + 1))
                        pool.tensor_tensor(w_lo[:, :, part, :], wh[:, :, part, :], w_hi[:, :, part, :].bitcast(F32), ALU.subtract).then_inc(s["w_lo01"], 1)

                def body(i, more):
                    pool.wait_ge(s["abs_ready"], i * 2 + 2)
                    pool.wait_ge(s["q_scaled"], i + 1)
                    for u in range(NU):
                        d, tt = UNITS[u]
                        pool.wait_ge(s["e_ready"], i * NU + (u + 1))
                        if u >= 2:
                            pool.wait_ge(s["sc_done"], i * NU + (u - 1))
                        pool.tensor_tensor(kd[:, u % 2, :, :], e[:, u % 2, 1:N8, :], kk[:, d, tt, :].unsqueeze(1).broadcast_to([P, NLV, P]),
                                           ALU.mult).then_inc(s["qk_k"], 1)
                        pool.tensor_tensor(ke[:, u, :], e[:, u % 2, 0, :], kk[:, d, tt, :], ALU.mult)
                        pool.tensor_tensor(qs[:, u, :], e[:, u % 2, N8, :], q[:, tt, :], ALU.mult).then_inc(s["side_done"], 1)
                    if more:
                        split(i + 1)

                split(0)
                heads(pool, body)

            @block.vector
            def _(dve):
                def split(h, part):
                    dve.wait_ge(s["w_hi"], h * SPLIT + (part + 1))
                    dve.tensor_tensor(w_lo[:, :, part % 2, :], wh[:, :, part, :], w_hi[:, :, part % 2, :].bitcast(F32), ALU.subtract).then_inc(s["w_lo234"], 1)

                def decays_lo(h):
                    for d in range(2):
                        dve.wait_ge(s["g_hi"], h * 2 + (d + 1))
                        flat_d = lambda a: a[:, d, :, :].rearrange("p t d -> p (t d)")
                        dve.tensor_tensor(flat_d(g_lo), k.ps[:, 5 + d, :], flat_d(g_hi).bitcast(F32), ALU.subtract).then_inc(s["g_lo"], 1)

                def queries(h):
                    dve.wait_ge(s["q_ready"], h + 1)
                    q_all = q[:, :, :].rearrange("p t d -> p (t d)")
                    dve.tensor_scalar(q_all, q_all, HGRN_SCALE, None, ALU.mult).then_inc(s["q_scaled"], 1)

                def decays(h):
                    for d in range(2):
                        dve.wait_ge(s["soft_step"], h * 4 + (3 + d))
                        dve.scalar_tensor_tensor(g[:, d, :, :].rearrange("p t d -> p (t d)"), k.ps[:, 1 + d, :], 0.0, ab[:, d, :], ALU.min,
                                                 ALU.subtract).then_inc(s["g_ready"], 1)

                def gates(h):
                    dve.wait_ge(s["v_ready"], h * 2 + 2)
                    dve.tensor_tensor(sg[:, :, :], sg[:, :, :], gain[:, :].unsqueeze(1).broadcast_to([P, TILES, P]), ALU.mult).then_inc(s["gate_ready"], 1)

                def tiles(i):
                    dve.wait_ge(s["q_scaled"], i + 1)

                    def probs(u):
                        dve.wait_ge(s["sc_done"], i * NU + (u + 1))
                        if u >= 2:
                            dve.wait_ge(s["p_ready"], i * NU + (u - 1))
                        dve.tensor_tensor(pm[:, u % 2, :, :].rearrange("p n t -> p (n t)"), SC_PS, lvl[:, UNITS[u][0], :], ALU.mult).then_inc(s["masked"], 1)
                        dve.wait_ge(s["masked"], i * NU + (u + 1))
                        if u >= 2:
                            dve.wait_ge(s["pv_done"], i * NU + (u - 1))
                        dve.reduce_sum(pr[:, u % 2, :], pm[:, u % 2, :, :].rearrange("p n t -> p t n"), AX.X).then_inc(s["p_ready"], 1)

                    for u in range(NU + 1):
                        if u < NU:
                            d, tt = UNITS[u]
                            dve.wait_ge(s["e_ready"], i * NU + (u + 1))
                            end = P - 1 if d == 0 else 0
                            dve.tensor_copy(tot[:, u:u + 1], e[:, u % 2, N9 - 1, end:end + 1])
                            dve.tensor_tensor(qd[:, u % 2, :, :], e[:, u % 2, 1:N8, :], q[:, tt, :].unsqueeze(1).broadcast_to([P, NLV, P]),
                                              ALU.mult).then_inc(s["qk_q"], 1)
                        if u >= 1:
                            probs(u - 1)

                def cross_operands(i):
                    dve.wait_ge(s["qk_q"], i * NU + NU)
                    dve.wait_ge(s["side_done"], i * NU + NU)
                    for d in range(2):
                        l0, l1 = order(d, 0)
                        c0, c1 = order(d, 1)
                        dve.tensor_scalar(kx[:, d, :], ke[:, d * TILES + c0, :], tot[:, d * TILES + c1:d * TILES + c1 + 1], None, ALU.mult)
                        dve.tensor_scalar(qx[:, d, :], qs[:, d * TILES + l1, :], tot[:, d * TILES + l0:d * TILES + l0 + 1], None,
                                          ALU.mult).then_inc(s["x_ready"], 1)

                def norm(i):
                    dve.wait_ge(s["std_done"], i + 1)
                    dve.reciprocal(r[:, :], std[:, :]).then_inc(s["r_step"], 1)
                    dve.wait_ge(s["r_step"], i + 1)
                    dve.wait_ge(s["gate_ready"], i + 1)
                    for tt in range(TILES):
                        last = dve.scalar_tensor_tensor(y[:, tt, :], k.ps[:, O, tt * P:(tt + 1) * P], r[:, tt:tt + 1], sg[:, tt, :],
                                                        ALU.mult, ALU.mult)
                    last.then_inc(s["y_ready"], 1)

                def body(i, more):
                    tiles(i)
                    cross_operands(i)
                    if more:
                        queries(i + 1)
                        for part in range(2, SPLIT):
                            split(i + 1, part)
                    norm(i)
                    if more:
                        decays(i + 1)
                        gates(i + 1)
                        decays_lo(i + 1)

                queries(0)
                for part in range(2, SPLIT):
                    split(0, part)
                decays(0)
                gates(0)
                decays_lo(0)
                heads(dve, body)


OUT_SLOTS = 4


def out_both_phase(nc, k, b, l, stream, raw):
    names = ["w0_in", "w1_in", "w2_in", "w3_in", "hi_made", "lo_made"] + POST_SEMS
    SLOTS = OUT_SLOTS
    BEHIND = 3
    with ExitStack() as ctx:
        def sb(name, shape, dt=F32R):
            return ctx.enter_context(nc.sbuf_tensor(f"{name}_{nc.next_id()}", shape, dt))
        w_hi, w_lo = sb("both_w_hi", [P, FT, D]), sb("both_w_lo", [P, FT, D])
        y_hi, y_lo = sb("both_y_hi", [P, FT, S + CTX]), sb("both_y_lo", [P, FT, S + CTX])
        t = [ln_buffers(nc, ctx) for st in range(2)]

        def gain(st):
            return lambda f: b.mod[:, l, 2 * FT + f, st:st + 1]
        with phase(nc, names) as (block, s):

            @block.sync
            def _(sp):
                for n in range(SLOTS):
                    sp.sem_inc(s[f"w{n}_in"], 16)
                for n in range(SLOTS, FT):
                    sp.wait_ge(s["lo_made"], n - SLOTS + 1)
                    sp.dma_start(raw[:, n % SLOTS, :], stream[n]).then_inc(s[f"w{n % SLOTS}_in"], 16)

            @block.tensor
            def _(pe):
                for st in range(2):
                    for n in range(FT):
                        if st == 0:
                            pe.wait_ge(s["lo_made"], n + 1)
                        elif n == BEHIND:
                            pe.wait_ge(s["z0_ready"], TT)
                            pe.wait_ge(s["z1_ready"], TT)
                            turn_tensor(pe, k, s, t[0].z, s["po_turned"], 0, 0)
                        for tt in range(TT):
                            at = st * S + tt * P
                            for c in range(2):
                                for p, (y, wt) in enumerate(((y_hi, w_hi), (y_hi, w_lo), (y_lo, w_hi))):
                                    last = pe.matmul(k.ps[:, 4 * st + 2 * tt + c, :], y[:, n, at:at + P], wt[:, n, c * BANK:(c + 1) * BANK],
                                                     start=(n == 0 and p == 0), stop=(n == FT - 1 and p == 2), skip_group_check=True)
                            if n == FT - 1:
                                last.then_inc(s["tile_done"], 1)
                turn_tensor(pe, k, s, t[1].z, s["po_turned"], 1, 0)

            @block.scalar
            def _(act):
                for n in range(FT):
                    act.activation(y_hi[:, n, :], b.y_T[:, n, :], ACT.Copy)
                    act.wait_ge(s[f"w{n % SLOTS}_in"], n // SLOTS * 16 + 16)
                    act.activation(w_hi[:, n, :], raw[:, n % SLOTS, :], ACT.Copy).then_inc(s["hi_made"], 1)
                for st in range(2):
                    post_scalar(act, k, s, t[st], st)

            @block.vector
            def _(dve):
                for n in range(FT):
                    dve.wait_ge(s["hi_made"], n + 1)
                    dve.tensor_tensor(y_lo[:, n, :], b.y_T[:, n, :], y_hi[:, n, :].bitcast(F32), ALU.subtract)
                    dve.tensor_tensor(w_lo[:, n, :], raw[:, n % SLOTS, :], w_hi[:, n, :].bitcast(F32), ALU.subtract).then_inc(s["lo_made"], 1)
                for st in range(2):
                    post_vector(dve, k, s, t[st], gain(st), st * S, st, 0)


def second_block(nc, k, w):
    with ExitStack() as ctx:
        def sb(stack, name, shape):
            return stack.enter_context(nc.sbuf_tensor(f"{name}_{nc.next_id()}", shape, F32))
        b = Buffers()
        b.h_T = sb(ctx, "h_T", [P, FT, S + CTX])
        b.y_T = sb(ctx, "y_T", [P, FT, S + CTX])
        b.mod = k.mod

        def ffn(l, streams, ahead=()):
            up = w["ffn_w_up_2"][l].rearrange("(f p) (a i n) -> a i p f n", p=P, a=2, n=P)
            weights = up[0], up[1], w["ffn_w_down_2"][l].rearrange("(i p) n -> i p n", p=P)
            conv = Conv(
                tap=lambda n, i, a: k.par[:, ds(i + (conv_col(l, n) + a * NF), 1)],
                bias=lambda i, a: k.par[:, ds(i + (PAR["conv_b"] + l * CT + a * NF), 1)])
            with ExitStack() as inner:
                tiles = first_tiles(nc, inner)
                prenorm_phase(nc, k, b, l, True, streams, first_loads(tiles, *weights))
                for st in streams:
                    more = st != streams[-1]
                    ffn_phase(nc, k, *weights, lambda f: b.h_T[:, f, st * S:(st + 1) * S], conv=conv,
                              post=(lambda f: b.mod[:, l, 5 * FT + f, st:st + 1], st * S), loaded=tiles,
                              ahead=first_loads(tiles, *weights) if more else ahead, reloads=more)

        out_raw = b.h_T[:, :, :].rearrange("p f t -> p (f t)").rearrange("p (n d) -> p n d", d=D)

        def out_rows(name):
            return w[name][0].rearrange("(f p) n -> f p n", p=P)

        with ExitStack() as outer:
            hgrn, hgrn_ahead = hgrn_buffers(nc, outer, w)
            with ExitStack() as inner:
                m, gqa_ahead = gqa_buffers(nc, inner, w)
                prenorm_phase(nc, k, b, 0, False, [0, 1], gqa_ahead, first=True)
                gqa_project(nc, k, b, m, hgrn)
                gqa_attend(nc, k, b, m, hgrn_ahead)
            rows = out_rows("even_w_out_2")
            hgrn_phase(nc, k, b, w, hgrn, [(out_raw[:, n, :], rows[n]) for n in range(OUT_SLOTS)])
        out_both_phase(nc, k, b, 0, rows, out_raw)
        with ExitStack() as outer:
            b.bias = sb(outer, "na_bias", [P, CH, BIAS_ROWS, GW])
            half = GW // 2
            spare = sb(outer, "bias_pick", [P, half * P])
            pick = [b.y_T[0:2 * 32, :, :].rearrange("p f t -> p (f t)").rearrange("p (c n) -> p c n", n=P),
                    spare[0:2 * 32, :].rearrange("p (c n) -> p c n", n=P)]
            rpb, rpb_loads = bias_rows(nc, outer, w)
            ffn(0, [0, 1], rpb_loads + [(pick[n], w["c_pick"][:, n * half:(n + 1) * half, :]) for n in range(2)])
            bias = Bias(b.bias, lambda c: pick[c // half][:, c % half, :], rpb, sb(outer, "rpb_T", [2 * 32, BIAS_ROWS * CH]))
            wq = [sb(outer, f"odd_w{n}", [P, 3, FT, P]) for n in range(2)]
            prenorm_phase(nc, k, b, 1, False, [0, 1], [(wq[n][:, part, :, :], odd_columns(w)[n, part]) for n in range(2) for part in range(3)],
                          bias=bias)
            rows = out_rows("odd_w_out_2")
            odd_attend(nc, k, b, w, wq, spare, [(out_raw[:, n, :], rows[n]) for n in range(3)])
        out_phase(nc, k, [b.y_T[:, f, 0:S] for f in range(FT)], stream=rows, raw=out_raw,
                  post=(lambda f: b.mod[:, 1, 2 * FT + f, 0:1], 0))
        ffn(1, [0])


def build(nc, w, out):
    with ExitStack() as ctx:
        def sb(name, shape):
            return ctx.enter_context(nc.sbuf_tensor(f"{name}_{nc.next_id()}", shape, F32))
        k = Buffers()
        k.ps = ctx.enter_context(nc.psum_tensor("ps", [P, 8, BANK], F32))
        k.c_silu = sb("c_silu", [P, FT, 2])
        k.mod = sb("mod", [P, DEPTH, 6 * FT, 2])
        k.x_T = sb("x_T", [P, FT, S + CTX])
        k.ident = sb("ident", [P, P])
        k.alpha = sb("alpha", [P, P])
        k.par = sb("par", [P, PAR_TILES * P])
        k.eps = sb("eps", [P, 3])
        k.zero = sb("zero", [P, P])
        k.ones = sb("ones", [P, P])
        k.one_row = sb("one_row", [1, P])
        k.b_gate = sb("b_gate_b", [1, 3 * NH])
        k.causal = sb("causal", [P, P])
        k.cmp_mask = sb("cmp_mask", [P, TT, NC])
        k.any_cmp = sb("any_cmp", [P, TT])
        k.col = lambda name, i: k.par[:, ds(i + PAR[name], 1)]

        def hidden_tiles(name):
            return w[name].rearrange("l (f p) (i n) -> l i p f n", p=P, n=P)

        def down_tiles(name):
            return w[name].rearrange("l (i p) n -> l i p n", p=P)

        def ffn_weights(n, l):
            return hidden_tiles(f"ffn{n}_w_gate")[l], hidden_tiles(f"ffn{n}_w_up")[l], down_tiles(f"ffn{n}_w_down")[l]

        def mod_part(l, n):
            cols = w["w_mod_2"][n - 1].rearrange("(f p) (c n) -> c p f n", p=P, n=3 * P)
            return (lambda j: cols[l * 8 + j],
                    lambda j: k.mod[:, n - 1, ds(l * 24 + j * 3, 3), :],
                    lambda j: k.par[:, ds(l * 24 + j * 3 + (PAR["b_mod"] + (n - 1) * 48), 3)].unsqueeze(2).broadcast_to([P, 3, 2]))

        block1 = ExitStack()
        tiles = first_tiles(nc, block1)
        params_phase(nc, k, w, first_loads(tiles, *ffn_weights(1, 0)))
        with nc.Fori(0, DEPTH) as l:
            def norm(n):
                return lambda f: k.col(f"ln{n}_g", l * FT + f), lambda f: k.col(f"ln{n}_b", l * FT + f)

            x = lambda f: k.x_T[:, f, 0:S]
            with ExitStack() as inner:
                m = Buffers()
                m.w_tok = inner.enter_context(nc.sbuf_tensor("w_in_tok", [P, FT, 256 + 2 * KVW + 3 * NH], F32))
                m.w_keys = inner.enter_context(nc.sbuf_tensor("w_in_keys", [P, FT, 4 * KVW], F32))
                w_in = w["w_in"].rearrange("l (f p) n -> l p f n", p=P)[l]
                tok, keys, _ = mixer1_columns()
                ahead = column_loads(m.w_tok, w_in, tok) + column_loads(m.w_keys, w_in, keys)
                ffn_phase(nc, k, *ffn_weights(1, l), x, ln=norm(1), mod=mod_part(l, 1), loaded=tiles,
                          ahead=[(k.b_gate[0:1, :], w["b_gate"].unsqueeze(1)[l])] + ahead)
                mixer1(nc, k, w, l, m, first_loads(tiles, *ffn_weights(2, l)))
            ffn_phase(nc, k, *ffn_weights(2, l), x, ln=norm(3), mod=mod_part(l, 2), loaded=tiles,
                      ahead=first_loads(tiles, *ffn_weights(1, l * -1 + 1)), reloads=True)
        block1.close()
        second_block(nc, k, w)
        store_phase(nc, k, out)


def store_phase(nc, k, out):
    with ExitStack() as ctx:
        rows = ctx.enter_context(nc.sbuf_tensor("out_rows", [P, TT, D], F32))
        with phase(nc, ["turned", "ready", "stored"]) as (block, s):

            @block.tensor
            def _(pe):
                for tt in range(TT):
                    for f in range(FT):
                        last = pe.transpose(k.ps[:, 2 * tt + f // 4, f % 4 * P:(f % 4 + 1) * P], k.x_T[:, f, tt * P:(tt + 1) * P],
                                            k.ident[:, :])
                    last.then_inc(s["turned"], 1)

            @block.vector
            def _(dve):
                for tt in range(TT):
                    dve.wait_ge(s["turned"], tt + 1)
                    dve.tensor_copy(rows[:, tt, :], k.ps[:, 2 * tt:2 * tt + 2, :].rearrange("p b n -> p (b n)")).then_inc(s["ready"], 1)

            @block.sync
            def _(sp):
                for tt in range(TT):
                    sp.wait_ge(s["ready"], tt + 1)
                    sp.dma_start(out[0, tt * P:(tt + 1) * P, :], rows[:, tt, :]).then_inc(s["stored"], 16)
                sp.wait_ge(s["stored"], 16 * TT)


_INS = ['x', 'ln1_g', 'ln1_b', 'ffn1_w_gate', 'ffn1_w_up', 'ffn1_w_down', 'w_in', 'b_gate', 'pool_w', 'pool_scale',
        'cmp_pos_k', 'cmp_k_w1', 'cmp_k_w2', 'cmp_pos_v', 'cmp_v_w1', 'cmp_v_w2', 'w_out', 'ln2_g', 'ln2_b',
        'ffn2_w_gate', 'ffn2_w_up', 'ffn2_w_down', 'ln3_g', 'ln3_b', 'c_2', 'ctx_2', 'c_ctx_2', 'w_mod_2', 'b_mod_2',
        'norm_pre_mix_2', 'norm_post_mix_2', 'norm_pre_ffn_2', 'norm_post_ffn_2', 'even_w_in_2', 'even_w_out_2',
        'even_q_norm_2', 'even_k_norm_2', 'hgrn_out_norm_2', 'odd_w_qkv_2', 'odd_w_out_2', 'odd_rpb_2', 'ffn_w_up_2',
        'ffn_conv_w_2', 'ffn_conv_b_2', 'ffn_w_down_2']


def kernel(**inputs):
    import concourse.bacc as _bacc
    from concourse.bass_utils import run_bass_kernel_spmd as _run

    nc = _bacc.Bacc("TRN2", target_bir_lowering=False, num_devices=1)
    arrays, w = {}, {}
    host = {name: np.ascontiguousarray(inputs[name]) for name in _INS}
    host.update(shape_constants())
    for name, a in host.items():
        arrays[f"in_{name}"] = a
        w[name] = nc.dram_tensor(f"in_{name}", a.shape, mybir.dt.from_np(a.dtype), kind="ExternalInput").ap()
    out = nc.dram_tensor("out", (1, S, D), F32, kind="ExternalOutput").ap()
    build(nc, w, out)
    r = _run(nc, [arrays], core_ids=[0])
    return r.results[0]["out"]
```
